# Optimizing a Trainium2 kernel written in Bass

```python
import jax, jax.numpy as jnp
from jax import lax
import numpy as np

D_MODEL = 1024
BATCH = 1
SEQ = 256
DEPTH = 1

SSM_HEADS = 16
SSM_HEAD_DIM = 64
SSM_WIDTH = SSM_HEADS * SSM_HEAD_DIM
SSM_GROUPS = 2
SSM_STATE = 128
CONV_WIDTH = 4
CHUNK = 128
CONV_DIM = SSM_WIDTH + 2 * SSM_GROUPS * SSM_STATE
ATT_HEADS = 16
ATT_HEAD_DIM = 64
ATT_WIDTH = ATT_HEADS * ATT_HEAD_DIM
Q_BLOCK = 128
MIX_WIDTH = SSM_WIDTH + ATT_WIDTH
D_FF = 4 * D_MODEL
SPLITS = [SSM_WIDTH,
          SSM_WIDTH + CONV_DIM,
          SSM_WIDTH + CONV_DIM + SSM_HEADS,
          SSM_WIDTH + CONV_DIM + SSM_HEADS + ATT_WIDTH,
          SSM_WIDTH + CONV_DIM + SSM_HEADS + 2 * ATT_WIDTH,
          SSM_WIDTH + CONV_DIM + SSM_HEADS + 3 * ATT_WIDTH]
IN_COLS = SPLITS[-1] + ATT_HEADS
DEEPNORM_ALPHA = (2.0 * DEPTH) ** 0.25
DEEPNORM_BETA = (8.0 * DEPTH) ** -0.25
LN_EPS = 1e-5
RMS_EPS = 1e-5


def layer_norm(x, g, b):
    xf = x.astype(jnp.float32)
    mu = jnp.mean(xf, axis=-1, keepdims=True)
    var = jnp.mean(jnp.square(xf - mu), axis=-1, keepdims=True)
    return ((xf - mu) * lax.rsqrt(var + LN_EPS) * g + b).astype(x.dtype)

def rms_norm(x, w):
    xf = x.astype(jnp.float32)
    return xf * lax.rsqrt(jnp.mean(xf * xf, axis=-1, keepdims=True) + RMS_EPS) * w

def causal_depthwise_conv(u, w, b):
    out = lax.conv_general_dilated(
        u, w[:, None, :].astype(u.dtype), window_strides=(1,),
        padding=[(CONV_WIDTH - 1, 0)], dimension_numbers=('NWC', 'WIO', 'NWC'),
        feature_group_count=u.shape[-1])
    return out + b

def segsum(a):
    cs = jnp.cumsum(a, axis=-1)
    diff = cs[..., :, None] - cs[..., None, :]
    t = a.shape[-1]
    mask = jnp.tril(jnp.ones((t, t), dtype=bool))
    return jnp.where(mask, diff, -jnp.inf)

def ssd_chunked(xh, dt, A, Bm, Cm):
    b, s, h, p = xh.shape
    g, n = Bm.shape[-2], Bm.shape[-1]
    e = h // g
    nc = s // CHUNK
    xc = (xh.astype(jnp.float32) * dt[..., None]).reshape(b, nc, CHUNK, g, e, p)
    Bc = Bm.astype(jnp.float32).reshape(b, nc, CHUNK, g, n)
    Cc = Cm.astype(jnp.float32).reshape(b, nc, CHUNK, g, n)
    a = (dt * A).reshape(b, nc, CHUNK, g, e).transpose(0, 3, 4, 1, 2)
    a_cs = jnp.cumsum(a, axis=-1)
    decay_in = jnp.exp(segsum(a))
    cb = jnp.einsum('bclgn,bcsgn->bgcls', Cc, Bc)
    scores = cb[:, :, None] * decay_in
    y_diag = jnp.einsum('bgecls,bcsgep->bclgep', scores, xc)
    decay_to_end = jnp.exp(a_cs[..., -1:] - a_cs).transpose(0, 3, 4, 1, 2)
    states = jnp.einsum('bclgn,bclgep->bcgepn', Bc, xc * decay_to_end[..., None])
    chunk_tot = jnp.pad(a_cs[..., -1], [(0, 0), (0, 0), (0, 0), (1, 0)])
    decay_chunk = jnp.exp(segsum(chunk_tot))
    states = jnp.concatenate([jnp.zeros_like(states[:, :1]), states], axis=1)
    new_states = jnp.einsum('bgezc,bcgepn->bzgepn', decay_chunk, states)
    prev_states = new_states[:, :-1]
    decay_out = jnp.exp(a_cs).transpose(0, 3, 4, 1, 2)
    y_off = jnp.einsum('bclgn,bcgepn->bclgep', Cc, prev_states) * decay_out[..., None]
    return (y_diag + y_off).reshape(b, s, h, p)

def forgetting_attention(q, k, v, log_f):
    s, d = q.shape[1], q.shape[-1]
    scale = d ** -0.5
    cum = jnp.cumsum(log_f, axis=1).transpose(0, 2, 1)
    outs = []
    for i in range(s // Q_BLOCK):
        q0, q1 = i * Q_BLOCK, (i + 1) * Q_BLOCK
        logits = jnp.einsum('bqhd,bkhd->bhqk', q[:, q0:q1], k[:, :q1],
                            preferred_element_type=jnp.float32) * scale
        logits = logits + (cum[:, :, q0:q1, None] - cum[:, :, None, :q1])
        mask = jnp.arange(q0, q1)[:, None] >= jnp.arange(q1)[None, :]
        logits = jnp.where(mask, logits, -jnp.inf)
        probs = jax.nn.softmax(logits, axis=-1)
        outs.append(jnp.einsum('bhqk,bkhd->bqhd', probs.astype(v.dtype), v[:, :q1]))
    return jnp.concatenate(outs, axis=1)

def hybrid_mixer(h, w_in, conv_w, conv_b, dt_bias, a_log, d_skip, ssm_norm_w, f_bias,
                 attn_norm_w, w_out):
    b, s, _ = h.shape
    proj = jnp.einsum('bsd,dk->bsk', h, w_in)
    z, xbc, dt_raw, q, k, v, f_raw = jnp.split(proj, SPLITS, axis=-1)
    xbc = jax.nn.silu(causal_depthwise_conv(xbc, conv_w, conv_b))
    xs, Bm, Cm = jnp.split(xbc, [SSM_WIDTH, SSM_WIDTH + SSM_GROUPS * SSM_STATE], axis=-1)
    xs = xs.reshape(b, s, SSM_HEADS, SSM_HEAD_DIM)
    Bm = Bm.reshape(b, s, SSM_GROUPS, SSM_STATE)
    Cm = Cm.reshape(b, s, SSM_GROUPS, SSM_STATE)
    dt = jax.nn.softplus(dt_raw.astype(jnp.float32) + dt_bias)
    A = -jnp.exp(a_log.astype(jnp.float32))
    y = ssd_chunked(xs, dt, A, Bm, Cm) + d_skip[:, None] * xs
    y_ssm = rms_norm(y.reshape(b, s, SSM_WIDTH) * jax.nn.silu(z), ssm_norm_w)
    q = q.reshape(b, s, ATT_HEADS, ATT_HEAD_DIM)
    k = k.reshape(b, s, ATT_HEADS, ATT_HEAD_DIM)
    v = v.reshape(b, s, ATT_HEADS, ATT_HEAD_DIM)
    log_f = jax.nn.log_sigmoid(f_raw.astype(jnp.float32) + f_bias)
    y_att = forgetting_attention(q, k, v, log_f).reshape(b, s, ATT_WIDTH)
    y_att = rms_norm(y_att, attn_norm_w)
    y_mix = jnp.concatenate([y_ssm, y_att.astype(y_ssm.dtype)], axis=-1)
    return jnp.einsum('bsk,kd->bsd', y_mix.astype(h.dtype), w_out)

def first_inputs(seed: int = 0) -> dict:
    key = jax.random.key(seed)
    ks = jax.random.split(key, 24)
    f32 = jnp.float32
    nrm = lambda k, shape, s: jax.random.normal(k, shape, f32) * s
    dt0 = jnp.exp(jax.random.uniform(ks[6], (DEPTH, SSM_HEADS), f32,
                                     np.log(1e-3).astype(np.float32), np.log(1e-1).astype(np.float32)))
    return {
        "x": nrm(ks[0], (BATCH, SEQ, D_MODEL), 1.0),
        "c": nrm(ks[1], (BATCH, D_MODEL), 1.0),
        "w_ada": nrm(ks[2], (DEPTH, D_MODEL, 6 * D_MODEL), 0.5 * D_MODEL ** -0.5),
        "b_ada": nrm(ks[3], (DEPTH, 6 * D_MODEL), 0.01),
        "w_in": nrm(ks[4], (DEPTH, D_MODEL, IN_COLS), D_MODEL ** -0.5),
        "conv_w": nrm(ks[5], (DEPTH, CONV_WIDTH, CONV_DIM), CONV_WIDTH ** -0.5),
        "conv_b": nrm(ks[7], (DEPTH, CONV_DIM), 0.01),
        "dt_bias": dt0 + jnp.log(-jnp.expm1(-dt0)),
        "a_log": jnp.log(jax.random.uniform(ks[8], (DEPTH, SSM_HEADS), f32, 1.0, 16.0)),
        "d_skip": 1.0 + nrm(ks[9], (DEPTH, SSM_HEADS), 0.1),
        "ssm_norm_w": 1.0 + nrm(ks[10], (DEPTH, SSM_WIDTH), 0.05),
        "f_bias": jax.random.uniform(ks[11], (DEPTH, ATT_HEADS), f32, 1.0, 4.0),
        "attn_norm_w": 1.0 + nrm(ks[12], (DEPTH, ATT_WIDTH), 0.05),
        "w_out": nrm(ks[13], (DEPTH, MIX_WIDTH, D_MODEL), DEEPNORM_BETA * MIX_WIDTH ** -0.5),
        "ln1_g": 1.0 + nrm(ks[14], (DEPTH, D_MODEL), 0.05),
        "ln1_b": nrm(ks[15], (DEPTH, D_MODEL), 0.01),
        "w_ff_in": nrm(ks[16], (DEPTH, D_MODEL, D_FF), D_MODEL ** -0.5),
        "w_ff_out": nrm(ks[17], (DEPTH, D_FF, D_MODEL), DEEPNORM_BETA * D_FF ** -0.5),
        "ln2_g": 1.0 + nrm(ks[18], (DEPTH, D_MODEL), 0.05),
        "ln2_b": nrm(ks[19], (DEPTH, D_MODEL), 0.01),
    }

def first_block(x, c, w_ada, b_ada, w_in, conv_w, conv_b, dt_bias, a_log, d_skip, ssm_norm_w,
              f_bias, attn_norm_w, w_out, ln1_g, ln1_b, w_ff_in, w_ff_out, ln2_g, ln2_b):
    c_act = jax.nn.silu(c)
    for l in range(DEPTH):
        mod = jnp.einsum('bd,de->be', c_act, w_ada[l]) + b_ada[l]
        sh1, sc1, g1, sh2, sc2, g2 = [m[:, None, :] for m in jnp.split(mod, 6, axis=-1)]
        h = x * (1.0 + sc1) + sh1
        y = hybrid_mixer(h, w_in[l], conv_w[l], conv_b[l], dt_bias[l], a_log[l], d_skip[l],
                         ssm_norm_w[l], f_bias[l], attn_norm_w[l], w_out[l])
        x = layer_norm(DEEPNORM_ALPHA * x + (1.0 + g1) * y, ln1_g[l], ln1_b[l])
        h = x * (1.0 + sc2) + sh2
        ff = jnp.einsum('bsf,fd->bsd',
                        jnp.square(jax.nn.relu(jnp.einsum('bsd,df->bsf', h, w_ff_in[l]))),
                        w_ff_out[l])
        x = layer_norm(DEEPNORM_ALPHA * x + (1.0 + g2) * ff, ln2_g[l], ln2_b[l])
    return x


DEPTH_2 = 2

N_MIXERS = 4
N_MEM = 256
EPS = 1e-6
NEG = -1e30
D_FF_2 = ((8 * D_MODEL // 3 + 255) // 256) * 256

POOL_WINDOWS = (2, 4, 8, 16)
POOL_GROUP = D_MODEL // len(POOL_WINDOWS)

NSA_HEADS = 16
NSA_KV_HEADS = 4
NSA_HEAD_DIM = D_MODEL // NSA_HEADS
NSA_CMP_BLOCK = 32
NSA_CMP_STRIDE = 16
NSA_SEL_BLOCK = 64
NSA_N_SELECT = 16
NSA_WINDOW = 512
NSA_CMP_HIDDEN = 4 * NSA_HEAD_DIM
NSA_Q_BLOCK = 64
NSA_KV_WIDTH = NSA_KV_HEADS * NSA_HEAD_DIM
NSA_FORCE = 1e4
NSA_IN_WIDTH = D_MODEL + 6 * NSA_KV_WIDTH + 3 * NSA_HEADS

GLA_HEADS = 4
GLA_DK = D_MODEL // 2 // GLA_HEADS
GLA_DV = D_MODEL // GLA_HEADS
GLA_GATE_RANK = 16
GLA_TAU = 16.0
GLA_CHUNK = 64
GLA_IN_WIDTH = 2 * GLA_HEADS * GLA_DK + 2 * GLA_HEADS * GLA_DV + GLA_GATE_RANK

CONV_WIDTH_2 = 31

XATTN_HEADS = 4
XATTN_HEAD_DIM = D_MODEL // XATTN_HEADS


F32 = jnp.float32

def n_layers_of(m):
    return len(range(m, DEPTH_2, N_MIXERS))

def rms_norm_2(x, g):
    xf = x.astype(F32)
    y = xf * lax.rsqrt(jnp.mean(xf * xf, axis=-1, keepdims=True) + EPS)
    return (y * g.astype(F32)).astype(x.dtype)

def swiglu_ffn(h, w_in, w_out):
    g, u = jnp.split(h @ w_in, 2, axis=-1)
    return (jax.nn.silu(g) * u) @ w_out

def pool_mixer(h, w, b, scale):
    B, S, D = h.shape
    hf = h.astype(F32)
    c = jnp.pad(jnp.cumsum(hf, axis=1), ((0, 0), (1, 0), (0, 0)))
    t = jnp.arange(S)
    groups = []
    for gi, win in enumerate(POOL_WINDOWS):
        cg = c[:, :, gi * POOL_GROUP:(gi + 1) * POOL_GROUP]
        start = jnp.maximum(t + 1 - win, 0)
        win_sum = cg[:, 1:] - jnp.take(cg, start, axis=1)
        cnt = (t + 1 - start).astype(F32)[None, :, None]
        groups.append(win_sum / cnt - hf[:, :, gi * POOL_GROUP:(gi + 1) * POOL_GROUP])
    p = jnp.stack(groups, axis=2)
    y = jnp.einsum('bsgc,gcd->bsgd', p, w.astype(F32)).reshape(B, S, D) + b.astype(F32)
    return (y * scale.astype(F32)).astype(h.dtype)

def nsa_mixer(h, w_in, cmp_pos, cmp_w1, cmp_w2, w_o):
    B, S, D = h.shape
    H, G, dh = NSA_HEADS, NSA_KV_HEADS, NSA_HEAD_DIM
    R = H // G
    SEL = NSA_SEL_BLOCK
    proj = (h @ w_in).astype(F32)
    splits = np.cumsum([D] + [NSA_KV_WIDTH] * 6).tolist()
    q, kc, vc, ks, vs, kw, vw, gates = jnp.split(proj, splits, axis=-1)
    q = q.reshape(B, S, G, R, dh).transpose(0, 2, 3, 1, 4) * dh ** -0.5
    gates = jax.nn.sigmoid(gates).reshape(B, S, G, R, 3).transpose(0, 2, 3, 1, 4)

    def kv_heads(a):
        return a.reshape(B, S, G, dh).transpose(0, 2, 1, 3)

    n_cmp = (S - NSA_CMP_BLOCK) // NSA_CMP_STRIDE + 1
    cmp_idx = np.arange(n_cmp)[:, None] * NSA_CMP_STRIDE + np.arange(NSA_CMP_BLOCK)[None, :]

    def compress(a, pos, w1, w2):
        blk = (a[:, :, cmp_idx] + pos.astype(F32)).reshape(B, G, n_cmp, NSA_CMP_BLOCK * dh)
        return jax.nn.gelu(blk @ w1.astype(F32)) @ w2.astype(F32)

    k_cmp = compress(kv_heads(kc), cmp_pos[0], cmp_w1[0], cmp_w2[0])
    v_cmp = compress(kv_heads(vc), cmp_pos[1], cmp_w1[1], cmp_w2[1])
    cmp_end = jnp.asarray(cmp_idx[:, -1])

    n_slc = S // SEL
    cs = np.arange(n_cmp) * NSA_CMP_STRIDE
    ss = np.arange(n_slc) * SEL
    ov = np.clip(np.minimum(cs[:, None] + NSA_CMP_BLOCK, ss[None, :] + SEL)
                 - np.maximum(cs[:, None], ss[None, :]), 0, None) / NSA_CMP_BLOCK
    ov = jnp.asarray(ov, F32)
    k_eff = min(NSA_N_SELECT, n_slc)
    blk_ids = jnp.arange(n_slc)

    ks_blk = kv_heads(ks).reshape(B, G, n_slc, SEL, dh)
    vs_blk = kv_heads(vs).reshape(B, G, n_slc, SEL, dh)
    kw_pad = jnp.pad(kv_heads(kw), ((0, 0), (0, 0), (NSA_WINDOW, 0), (0, 0)))
    vw_pad = jnp.pad(kv_heads(vw), ((0, 0), (0, 0), (NSA_WINDOW, 0), (0, 0)))
    bi = jnp.arange(B)[:, None, None, None]
    gi = jnp.arange(G)[None, :, None, None]
    Qb = min(NSA_Q_BLOCK, S)
    n_qb = S // Qb

    def block(qi):
        s0 = qi * Qb
        t = s0 + jnp.arange(Qb)
        qb = lax.dynamic_slice_in_dim(q, s0, Qb, axis=3)
        gb = lax.dynamic_slice_in_dim(gates, s0, Qb, axis=3)
        vis = cmp_end[None, :] <= t[:, None]
        sc = jnp.where(vis, jnp.einsum('bgrqd,bgnd->bgrqn', qb, k_cmp), NEG)
        p_cmp = jax.nn.softmax(sc, axis=-1) * jnp.any(vis, axis=-1)[:, None]
        o_cmp = jnp.einsum('bgrqn,bgnd->bgrqd', p_cmp, v_cmp)
        imp = jnp.einsum('bgrqn,nm->bgqm', p_cmp, ov)
        cur = t // SEL
        forced = (blk_ids[None, :] == 0) | (blk_ids[None, :] == cur[:, None]) | (blk_ids[None, :] == cur[:, None] - 1)
        imp = jnp.where(forced, NSA_FORCE, imp)
        imp = jnp.where(blk_ids[None, :] * SEL <= t[:, None], imp, -1.0)
        _, idx = lax.top_k(imp, k_eff)
        ksel = ks_blk[bi, gi, idx].reshape(B, G, Qb, k_eff * SEL, dh)
        vsel = vs_blk[bi, gi, idx].reshape(B, G, Qb, k_eff * SEL, dh)
        pos = (idx[..., None] * SEL + jnp.arange(SEL)).reshape(B, G, Qb, k_eff * SEL)
        sc = jnp.einsum('bgrqd,bgqkd->bgrqk', qb, ksel)
        sc = jnp.where((pos <= t[:, None])[:, :, None], sc, NEG)
        o_slc = jnp.einsum('bgrqk,bgqkd->bgrqd', jax.nn.softmax(sc, axis=-1), vsel)
        kwin = lax.dynamic_slice_in_dim(kw_pad, s0, NSA_WINDOW + Qb, axis=2)
        vwin = lax.dynamic_slice_in_dim(vw_pad, s0, NSA_WINDOW + Qb, axis=2)
        wpos = s0 - NSA_WINDOW + jnp.arange(NSA_WINDOW + Qb)
        wmask = (wpos[None, :] <= t[:, None]) & (wpos[None, :] > t[:, None] - NSA_WINDOW) & (wpos[None, :] >= 0)
        sc = jnp.where(wmask, jnp.einsum('bgrqd,bgkd->bgrqk', qb, kwin), NEG)
        o_win = jnp.einsum('bgrqk,bgkd->bgrqd', jax.nn.softmax(sc, axis=-1), vwin)
        return gb[..., 0:1] * o_cmp + gb[..., 1:2] * o_slc + gb[..., 2:3] * o_win

    o = lax.map(block, jnp.arange(n_qb))
    o = o.transpose(1, 0, 4, 2, 3, 5).reshape(B, S, H * dh)
    return o.astype(h.dtype) @ w_o

def gla_mixer(h, w_in, w_gate_up, b_gate, norm_g, w_o):
    B, S, D = h.shape
    Hh, dk, dv, C = GLA_HEADS, GLA_DK, GLA_DV, GLA_CHUNK
    proj = (h @ w_in).astype(F32)
    qw, vw = Hh * dk, Hh * dv
    q, k, v, og, gdown = jnp.split(proj, [qw, 2 * qw, 2 * qw + vw, 2 * qw + 2 * vw], axis=-1)
    log_a = jax.nn.log_sigmoid(gdown @ w_gate_up.astype(F32) + b_gate.astype(F32)) / GLA_TAU
    nc = S // C

    def heads(a, d):
        return a.reshape(B, nc, C, Hh, d).transpose(0, 3, 1, 2, 4)

    q = heads(q, dk) * dk ** -0.5
    k = heads(k, dk)
    v = heads(v, dv)
    b = jnp.cumsum(heads(log_a, dk), axis=3)
    b_last = b[:, :, :, -1:, :]
    q_t = q * jnp.exp(b)
    k_t = k * jnp.exp(-b)
    causal = jnp.tril(jnp.ones((C, C), dtype=bool))
    A = jnp.where(causal, jnp.einsum('bhncd,bhnsd->bhncs', q_t, k_t), 0.0)
    o_intra = jnp.einsum('bhncs,bhnsv->bhncv', A, v)
    kv = jnp.einsum('bhncd,bhncv->bhndv', k * jnp.exp(b_last - b), v)
    decay = jnp.exp(b_last[:, :, :, 0, :])

    def step(state, inp):
        kv_n, dec_n = inp
        return dec_n[..., None] * state + kv_n, state

    init = jnp.zeros((B, Hh, dk, dv), F32)
    _, s_prev = lax.scan(step, init, (kv.transpose(2, 0, 1, 3, 4), decay.transpose(2, 0, 1, 3)))
    s_prev = s_prev.transpose(1, 2, 0, 3, 4)
    o = o_intra + jnp.einsum('bhncd,bhndv->bhncv', q_t, s_prev)
    o = rms_norm_2(o.transpose(0, 2, 3, 1, 4).reshape(B, S, Hh, dv), norm_g)
    o = o.reshape(B, S, Hh * dv) * jax.nn.silu(og)
    return o.astype(h.dtype) @ w_o

def conv_mixer(h, w_in, b_in, w_dw, b_dw, ln_g, ln_b, w_out, b_out):
    D = h.shape[-1]
    a, gate = jnp.split(h @ w_in + b_in, 2, axis=-1)
    u = a * jax.nn.sigmoid(gate)
    u = jnp.pad(u, ((0, 0), (CONV_WIDTH_2 - 1, 0), (0, 0)))
    u = lax.conv_general_dilated(u, w_dw[:, None, :].astype(u.dtype), window_strides=(1,), padding='VALID',
                                 dimension_numbers=('NWC', 'WIO', 'NWC'), feature_group_count=D) + b_dw
    uf = u.astype(F32)
    mu = jnp.mean(uf, axis=-1, keepdims=True)
    var = jnp.mean(jnp.square(uf - mu), axis=-1, keepdims=True)
    uf = (uf - mu) * lax.rsqrt(var + EPS) * ln_g.astype(F32) + ln_b.astype(F32)
    return jax.nn.silu(uf).astype(h.dtype) @ w_out + b_out

def memory_cross_attention(h, mem_n, w_q, w_kv, w_o):
    B, S, D = h.shape
    N = mem_n.shape[1]
    Hx, dh = XATTN_HEADS, XATTN_HEAD_DIM
    q = (h @ w_q).astype(F32).reshape(B, S, Hx, dh) * dh ** -0.5
    k, v = jnp.split((mem_n @ w_kv).astype(F32), 2, axis=-1)
    k = k.reshape(B, N, Hx, dh)
    v = v.reshape(B, N, Hx, dh)
    p = jax.nn.softmax(jnp.einsum('bqhd,bkhd->bhqk', q, k), axis=-1)
    o = jnp.einsum('bhqk,bkhd->bqhd', p, v).reshape(B, S, D)
    return o.astype(h.dtype) @ w_o

def second_inputs(seed: int = 0) -> dict:
    key = jax.random.key(seed)
    keys = iter(jax.random.split(key, 64))
    D, F, L = D_MODEL, D_FF_2, DEPTH_2
    nA, nB, nC, nD = (n_layers_of(m) for m in range(N_MIXERS))

    def w(shape, fan_in):
        return jax.random.normal(next(keys), shape, F32) * fan_in ** -0.5

    def gain(shape):
        return 1.0 + 0.02 * jax.random.normal(next(keys), shape, F32)

    def small(shape, s=0.02):
        return s * jax.random.normal(next(keys), shape, F32)

    return {
        "x": jax.random.normal(next(keys), (BATCH, SEQ, D), F32),
        "mem": jax.random.normal(next(keys), (BATCH, N_MEM, D), F32),
        "ffn1_norm": gain((L, D)),
        "ffn1_w_in": w((L, D, 2 * F), D),
        "ffn1_w_out": w((L, F, D), F),
        "mix_norm": gain((L, D)),
        "xattn_norm": gain((L, D)),
        "mem_norm": gain((L, D)),
        "xattn_w_q": w((L, D, D), D),
        "xattn_w_kv": w((L, D, 2 * D), D),
        "xattn_w_o": w((L, D, D), D),
        "ffn2_norm": gain((L, D)),
        "ffn2_w_in": w((L, D, 2 * F), D),
        "ffn2_w_out": w((L, F, D), F),
        "pool_w": w((nA, len(POOL_WINDOWS), POOL_GROUP, POOL_GROUP), POOL_GROUP),
        "pool_b": small((nA, D)),
        "pool_scale": 1.0 + 0.1 * jax.random.normal(next(keys), (nA, D), F32),
        "nsa_w_in": w((nB, D, NSA_IN_WIDTH), D),
        "nsa_cmp_pos": small((nB, 2, NSA_CMP_BLOCK, NSA_HEAD_DIM), 0.1),
        "nsa_cmp_w1": w((nB, 2, NSA_CMP_BLOCK * NSA_HEAD_DIM, NSA_CMP_HIDDEN), NSA_CMP_BLOCK * NSA_HEAD_DIM),
        "nsa_cmp_w2": w((nB, 2, NSA_CMP_HIDDEN, NSA_HEAD_DIM), NSA_CMP_HIDDEN),
        "nsa_w_o": w((nB, D, D), D),
        "gla_w_in": w((nC, D, GLA_IN_WIDTH), D),
        "gla_w_gate_up": w((nC, GLA_GATE_RANK, GLA_HEADS * GLA_DK), GLA_GATE_RANK),
        "gla_b_gate": small((nC, GLA_HEADS * GLA_DK)),
        "gla_norm": gain((nC, GLA_DV)),
        "gla_w_o": w((nC, D, D), D),
        "conv_w_in": w((nD, D, 2 * D), D),
        "conv_b_in": small((nD, 2 * D)),
        "conv_dw": w((nD, CONV_WIDTH_2, D), CONV_WIDTH_2),
        "conv_b_dw": small((nD, D)),
        "conv_ln_g": gain((nD, D)),
        "conv_ln_b": small((nD, D)),
        "conv_w_out": w((nD, D, D), D),
        "conv_b_out": small((nD, D)),
        "final_norm": gain((D,)),
    }

def second_block(x, mem, ffn1_norm, ffn1_w_in, ffn1_w_out, mix_norm, xattn_norm, mem_norm,
              xattn_w_q, xattn_w_kv, xattn_w_o, ffn2_norm, ffn2_w_in, ffn2_w_out,
              pool_w, pool_b, pool_scale,
              nsa_w_in, nsa_cmp_pos, nsa_cmp_w1, nsa_cmp_w2, nsa_w_o,
              gla_w_in, gla_w_gate_up, gla_b_gate, gla_norm, gla_w_o,
              conv_w_in, conv_b_in, conv_dw, conv_b_dw, conv_ln_g, conv_ln_b, conv_w_out, conv_b_out,
              final_norm):
    for i in range(DEPTH_2):
        m, j = i % N_MIXERS, i // N_MIXERS
        x = x + 0.5 * swiglu_ffn(rms_norm_2(x, ffn1_norm[i]), ffn1_w_in[i], ffn1_w_out[i])
        h = rms_norm_2(x, mix_norm[i])
        if m == 0:
            y = pool_mixer(h, pool_w[j], pool_b[j], pool_scale[j])
        elif m == 1:
            y = nsa_mixer(h, nsa_w_in[j], nsa_cmp_pos[j], nsa_cmp_w1[j], nsa_cmp_w2[j], nsa_w_o[j])
        elif m == 2:
            y = gla_mixer(h, gla_w_in[j], gla_w_gate_up[j], gla_b_gate[j], gla_norm[j], gla_w_o[j])
        else:
            y = conv_mixer(h, conv_w_in[j], conv_b_in[j], conv_dw[j], conv_b_dw[j],
                           conv_ln_g[j], conv_ln_b[j], conv_w_out[j], conv_b_out[j])
        x = x + y
        x = x + memory_cross_attention(rms_norm_2(x, xattn_norm[i]), rms_norm_2(mem, mem_norm[i]),
                                       xattn_w_q[i], xattn_w_kv[i], xattn_w_o[i])
        x = x + 0.5 * swiglu_ffn(rms_norm_2(x, ffn2_norm[i]), ffn2_w_in[i], ffn2_w_out[i])
    return rms_norm_2(x, final_norm)


def setup_inputs(seed=0):
    out = dict(first_inputs(seed))
    for name, value in second_inputs(seed + 1).items():
        if name != "x":
            out[name + "_2"] = value
    return out


def reference(
    x, c, w_ada, b_ada, w_in, conv_w, conv_b, dt_bias, a_log, d_skip, ssm_norm_w, f_bias,
    attn_norm_w, w_out, ln1_g, ln1_b, w_ff_in, w_ff_out, ln2_g, ln2_b, mem_2, ffn1_norm_2,
    ffn1_w_in_2, ffn1_w_out_2, mix_norm_2, xattn_norm_2, mem_norm_2, xattn_w_q_2, xattn_w_kv_2,
    xattn_w_o_2, ffn2_norm_2, ffn2_w_in_2, ffn2_w_out_2, pool_w_2, pool_b_2, pool_scale_2,
    nsa_w_in_2, nsa_cmp_pos_2, nsa_cmp_w1_2, nsa_cmp_w2_2, nsa_w_o_2, gla_w_in_2,
    gla_w_gate_up_2, gla_b_gate_2, gla_norm_2, gla_w_o_2, conv_w_in_2, conv_b_in_2, conv_dw_2,
    conv_b_dw_2, conv_ln_g_2, conv_ln_b_2, conv_w_out_2, conv_b_out_2, final_norm_2,
):
    x = first_block(
        x, c, w_ada, b_ada, w_in, conv_w, conv_b, dt_bias, a_log, d_skip, ssm_norm_w, f_bias,
        attn_norm_w, w_out, ln1_g, ln1_b, w_ff_in, w_ff_out, ln2_g, ln2_b,
    )
    return second_block(
        x, mem_2, ffn1_norm_2, ffn1_w_in_2, ffn1_w_out_2, mix_norm_2, xattn_norm_2, mem_norm_2,
        xattn_w_q_2, xattn_w_kv_2, xattn_w_o_2, ffn2_norm_2, ffn2_w_in_2, ffn2_w_out_2,
        pool_w_2, pool_b_2, pool_scale_2, nsa_w_in_2, nsa_cmp_pos_2, nsa_cmp_w1_2, nsa_cmp_w2_2,
        nsa_w_o_2, gla_w_in_2, gla_w_gate_up_2, gla_b_gate_2, gla_norm_2, gla_w_o_2,
        conv_w_in_2, conv_b_in_2, conv_dw_2, conv_b_dw_2, conv_ln_g_2, conv_ln_b_2,
        conv_w_out_2, conv_b_out_2, final_norm_2,
    )


_drawn_inputs = setup_inputs


def setup_inputs(seed=0):
    import zlib

    import numpy as np

    out = dict(_drawn_inputs(seed))
    spreads = {}
    factors = {'b_ada': 3.237,
     'conv_b': 8.0,
     'ssm_norm_w': 3.103,
     'attn_norm_w': 3.121,
     'ln1_b': 5.349,
     'ln2_b': 5.633,
     'ffn1_norm_2': 5.324,
     'mix_norm_2': 3.997,
     'xattn_norm_2': 8.0,
     'mem_norm_2': 8.0,
     'ffn2_norm_2': 6.377,
     'pool_b_2': 3.204,
     'nsa_cmp_pos_2': 2.68,
     'final_norm_2': 2.804}
    for name, (base, spread) in spreads.items():
        noise = np.random.default_rng([zlib.crc32(name.encode()), seed]).standard_normal(out[name].shape)
        drawn = base * np.exp(spread * noise) if base else spread * noise
        out[name] = __import__('jax').numpy.asarray(drawn.astype(out[name].dtype))
    for name, factor in factors.items():
        out[name] = (out[name] * factor).astype(out[name].dtype)
    return out
```

```python
from contextlib import ExitStack

import concourse.bass as bass
from concourse import mybir

F32 = mybir.dt.float32
F32R = mybir.dt.float32r
ACT = mybir.ActivationFunctionType
ALU = mybir.AluOpType
AX = mybir.AxisListType

P = 128
S = 256
D = 1024
KC = D // P
H = 16
HD = 64
XH = 4
G_KV = 4
NCMP = (S - 32) // 16 + 1
HB = 8 * NCMP
CMP_J = 16
HID1 = 4 * D // P
HID2 = 22
RING = 4
SLOT = 2048
AHEAD = 2
NEG = -1e30
ALPHA = 2.0 ** 0.25
EPS1, EPS2 = 1e-5, 1e-6

_WIDTHS = [("b_ada", 48), ("conv_w", 48), ("conv_b", 12), ("ssm_w", 8), ("attn_w", 8),
           ("ln1_g", 8), ("ln1_b", 8), ("ln2_g", 8), ("ln2_b", 8), ("ffn1", 16), ("mix", 16),
           ("xattn", 16), ("mem", 16), ("ffn2", 16), ("pool_b", 8), ("pool_s", 8), ("final", 8),
           ("pos_k", 16), ("pos_v", 16), ("w2k", 256), ("w2v", 128)]
COL, NPAR = {}, 0
for _name, _width in _WIDTHS:
    COL[_name] = NPAR
    NPAR += _width

_FFN = lambda l, f: [(f"f{f}in{l}", HID2, SLOT, True), (f"f{f}out{l}", 16, 11 * P, True)]
_XATTN = lambda l: [(f"xk{l}", 4, SLOT, True), (f"xv{l}", 4, SLOT, True), (f"xq{l}", 4, SLOT, True),
                    (f"xo{l}", 4, SLOT, True)]
STAGES = ([("adaA", 8, SLOT, False), ("z", 4, SLOT, True), ("xbc", 6, SLOT, True), ("dtf", 1, 256, True),
           ("adaB", 16, SLOT, False), ("q", 4, SLOT, True), ("k", 4, SLOT, True), ("v", 4, SLOT, True),
           ("wout", 8, SLOT, True), ("ffin", 16, SLOT, True), ("ffout", 16, SLOT, True)]
          + _FFN(0, 1) + [("pool", 1, SLOT, True)] + _XATTN(0) + _FFN(0, 2)
          + _FFN(1, 1) + [("nq", 4, SLOT, True), ("nkc", 1, SLOT, True), ("nvc", 1, SLOT, True),
                          ("nks", 1, SLOT, True), ("nkw", 1, SLOT, True), ("nvs", 1, SLOT, True),
                          ("nvw", 1, SLOT, True), ("ng", 1, 384, True), ("cmpk", 2, SLOT, True),
                          ("cmpv", 2, SLOT, True), ("no", 4, SLOT, True)] + _XATTN(1) + _FFN(1, 2))


_FAMILIES = {
    "att": ([("fox", 32), ("xa0", 8), ("ns", 32), ("nw", 32), ("xa1", 8)],
            {k: None for k in ("qk", "l", "p", "tp", "pt", "pv")} | {"o": 4}),
    "res": ([("wout", 1), ("ln1", 1), ("ffout", 1), ("ln2", 1), ("f1out0", 1), ("pool", 1), ("xo0", 1),
             ("f2out0", 1), ("f1out1", 1), ("no", 1), ("xo1", 1), ("f2out1", 1)],
            {"hi": 8, "lo": 8, "sq": 8, "acc": 8, "mean": 1, "root": 1}),
    "ffn": ([("ffin", 16), ("f1in0", 22), ("f2in0", 22), ("f1in1", 22), ("f2in1", 22)],
            {k: None for k in ("sg", "h", "hi", "lo")}),
    "mix": ([("ssmt", 1), ("foxt", 1), ("xa0t", 1), ("nsat", 1), ("xa1t", 1)],
            {"y": 1, "tr": 4, "tev": 4, "hi": 8, "lo": 8}),
}
_ODD = {("wout", "hi"): 0, ("wout", "lo"): 0, ("wout", "sq"): 0,
        ("ln1", "sq"): 0, ("ln1", "acc"): 0, ("ln1", "mean"): 0, ("ln1", "root"): 0,
        ("ffout", "hi"): 0, ("ffout", "lo"): 0, ("ffout", "sq"): 0, ("ffin", "sg"): 0,
        ("f1out0", "hi"): 0, ("f1out0", "lo"): 0, ("f2out1", "hi"): 0, ("f2out1", "lo"): 0,
        ("f1out1", "mean"): 2, ("f1out1", "root"): 2}
SHARED = {}
for _fam, (_steps, _kinds) in _FAMILIES.items():
    for _kind, _each in _kinds.items():
        _before = 0
        for _step, _units in _steps:
            SHARED[f"{_step}.{_kind}"] = (f"{_fam}_{_kind}", _before)
            _before += _ODD.get((_step, _kind), _units if _each is None else _each)


class Stage:

    def __init__(self, name, slots, size, split, n0, m0, j0):
        self.name, self.slots, self.size, self.split = name, slots, size, split
        self.n0, self.m0, self.j0 = n0, m0, j0


def plan():
    out, n, m, j = {}, 0, 0, 0
    for name, slots, size, split in STAGES:
        out[name] = Stage(name, slots, size, split, n, m, j)
        n += slots
        m += slots if split else 0
        if name == "pool":
            j += 4
        elif split:
            j += slots // 2 if "out" in name and name != "wout" else slots
    return out


def build(nc, w, xT_d, memT_d, par_d, rows_d, cond_d, out_d):
    st = plan()
    order = list(st.values())
    split_order = [(s, k) for s in order if s.split for k in range(s.slots)]
    ctx = ExitStack()
    with ctx:
        def sb(name, shape, dt=F32, stack=ctx):
            return stack.enter_context(nc.sbuf_tensor(name, shape, dt))

        def sem(name):
            return ctx.enter_context(nc.semaphore(name))

        with ExitStack() as a:
            raw = [sb(f"raw{b}", [P, SLOT], F32, a) for b in range(RING)]
        w_lo = [sb(f"w_lo{b}", [P, SLOT], F32R) for b in range(RING)]
        w_hi = [sb(f"w_hi{b}", [P, SLOT], F32R) for b in range(RING)]
        X = sb("X", [P, KC, S])
        x_hi = sb("x_hi", [P, KC, S], F32R)
        x_lo = sb("x_lo", [P, KC, S], F32R)
        memN = sb("memN", [P, KC, S])
        par = sb("par", [P, NPAR])
        rows = sb("rows", [P, 64])
        ident = sb("ident", [P, P])
        U = sb("U", [P, P])
        SG = sb("SG", [P, S])
        mask = sb("mask", [P, S])
        ones_d = sb("ones_d", [P, P])
        ones = sb("ones", [P, P])
        zero = sb("zero", [P, 1])
        eps1 = sb("eps1", [P, 1])
        eps2 = sb("eps2", [P, 1])
        mod = sb("mod", [P, 48])
        mod1 = sb("mod1", [P, 48])
        R = sb("R", [P, S])
        Rs = sb("Rs", [P, S])
        RT = sb("RT", [P, 2])
        RTs = sb("RTs", [P, 2])
        acc = sb("acc", [P, S])
        icnt = sb("icnt", [P, 4, 16])
        pool_bs = sb("pool_bs", [P, KC])
        nmax = sb("nmax", [P, 96])
        ssum = sb("ssum", [P, 96])

        mtmp = sb("mtmp", [P, 2, S])
        vis = sb("vis", [P, 1])
        cmask = sb("cmask", [P, 2, NCMP])
        KC_T = sb("KC_T", [P, G_KV, NCMP])
        own_rows = sb("own_rows", [P, 8])
        wc = sb("wc", [P, 2, H])
        gates = sb("gates", [P, 2, 48])
        tok = {n: sb("tok_" + n, [P, 2, 32]) for n in ("v", "mag", "e", "den", "y", "y2", "poly", "sp")}
        dt_t = sb("dt_t", [P, 2, H])
        lf = sb("lf", [P, 2, H])
        a_t = sb("a_t", [P, 2, H])
        negA = sb("negA", [P, H])
        dend = sb("dend", [P, H])
        dout = sb("dout", [P, H])
        rtok = sb("rtok", [P, 2])
        rtoks = sb("rtoks", [P, 2])
        rs = sb("rs", [P, 8])

        def place(name, shape, dt, kib):
            with ExitStack() as a:
                if kib:
                    sb(f"pad_{name}", [P, int(kib * 256)], F32, a)
                return sb(name, shape, dt, a)

        gu = [place(f"gu{b}", [P, 2, S], F32, 2 * b) for b in range(2)]
        sg = [place(f"sg{b}", [P, 2 * S], F32, 4 + 2 * b) for b in range(2)]
        hb = [place(f"hb{b}", [P, 2 * S], F32, 8 + 2 * b) for b in range(2)]
        Lm = [place(f"Lm{b}", [P, S], F32, b) for b in range(2)]
        Pr = [place(f"Pr{b}", [P, S], F32, 2 + b) for b in range(2)]
        PT = [place(f"PT{b}", [P, 2, P], F32, 4 + b) for b in range(2)]
        RB = [place(f"RB{b}", [P, 384], F32, 6 + 1.5 * b) for b in range(2)]
        Ot = place("Ot", [P, 512], F32, 9)
        AS = [place(f"AS{b}", [P, 4, P], F32, 2 * b) for b in range(2)]
        E = [place(f"E{b}", [P, 4, P], F32, 4 + 2 * b) for b in range(2)]
        CB = place("CB", [P, 4, P], F32, 8)
        HG = place("HG", [P, 2, 60], F32, 10)
        work_space = sb("work_space", [P, 12 * 256])

        hid_hi = place("hid_hi", [P, 32, S], F32R, 0)
        hid_lo = place("hid_lo", [P, 32, S], F32R, 32)
        T8 = place("T8", [P, KC, S], F32, 64)
        AO = place("AO", [P, 2, D], F32, 72)
        CX = place("CX", [P, 12, S + 4], F32, 0)
        Zs = place("Zs", [P, 2, D], F32, 16)
        XsT = place("XsT", [P, 2, D], F32, 24)
        XB = place("XB", [P, 12, S], F32, 32)
        STt = place("STt", [P, 2, 512], F32, 44)
        xc = place("xc", [P, 2, D], F32, 48)
        Y = place("Y", [P, 2, D], F32, 56)
        BT = place("BT", [P, 2, P], F32, 72)
        xce = place("xce", [P, D], F32, 68)
        cond = place("cond", [P, D], F32, 74)
        qT = place("qT", [P, KC, S], F32, 16)
        kT = place("kT", [P, KC, S], F32, 24)
        V = place("V", [P, 2, D], F32, 48)
        ksd = place("ksd", [P, G_KV, S], F32, 24)
        kwd = place("kwd", [P, G_KV, S], F32, 28)
        vs = place("vs", [P, 2, 256], F32, 48)
        vw = place("vw", [P, 2, 256], F32, 50)
        Z = place("Z", [P, G_KV, S], F32, 52)
        bk = place("bk", [P, CMP_J, G_KV, NCMP], F32, 56)
        bk_hi = [place(f"bk_hi{b}", [P, CMP_J, 60], F32R, 60 + 8 * b) for b in range(2)]
        bk_lo = [place(f"bk_lo{b}", [P, CMP_J, 60], F32R, 64 + 8 * b) for b in range(2)]
        LC = place("LC", [P, 2, H * NCMP], F32, 52)
        HX = place("HX", [P, 2, HB], F32, 54)
        VB = place("VB", [P, 512], F32, 56)
        wa = place("wa", [P, KC, S], F32, 16)
        wb = place("wb", [P, KC, S], F32, 24)
        arena = sb("arena", [P, 80 * 256])

        def pb(name):
            return ctx.enter_context(nc.psum_tensor(name, [P, 512], F32))

        G = [pb(f"G{b}") for b in range(2)]
        L = [pb(f"L{b}") for b in range(2)]
        T = [pb(f"T{b}") for b in range(2)]
        O = [pb(f"O{b}") for b in range(2)]

        sems = {}

        def q(name):
            key = SHARED[name][0] if name in SHARED else name.replace(".", "_")
            if key not in sems:
                sems[key] = sem(key)
            return sems[key]

        def nth(name, count):
            return (SHARED[name][1] if name in SHARED else 0) + count

        s_load = [sem(f"s_load{b}") for b in range(RING)]
        s_hi = sem("s_hi")
        s_lo = sem("s_lo")
        s_mm = sem("s_mm")
        s_ev = [sem(f"s_ev{b}") for b in range(2)]
        s_in = sem("s_in")
        s_par = sem("s_par")
        s_out = sem("s_out")

        def pc(name, k=0):
            return par[:, COL[name] + k:COL[name] + k + 1]

        def bc(ap, shape):
            return ap.broadcast_to(shape)

        class Chain:

            def __init__(self, eng, name):
                self.eng, self.sem, self.n = eng, q(name), 0

            def __call__(self, ins):
                self.n += 1
                ins.then_inc(self.sem, 1)
                self.eng.wait_ge(self.sem, self.n)

        def taken(eng, j, i=0, groups=4):
            eng.wait_ge(s_ev[j % 2], j // 2 + 1 + i * (groups // 2))

        def all_taken(eng, j):
            for back in (1, 2):
                taken(eng, j - back)

        def tiles2(bank):
            return bank[:, :].rearrange("p (f c) -> p f c", f=2)

        def h8(ap):
            return ap.rearrange("p (h d) -> p h d", h=8)

        block = ctx.enter_context(nc.Block())

        @block.sync
        def _(sp):
            sp.dma_start(cond[:], cond_d).then_inc(q("cond_in"), 16)
            sp.dma_start(memN[:], memT_d).then_inc(q("mem_in"), 16)

            users = [(s.split, (s.m0 if s.split else s.n0 - s.m0) + k) for s in order for k in range(s.slots)]

            def load(s, slot, i=0):
                n = s.n0 + slot
                if n >= RING:
                    before = users[n - RING]
                    if before[0]:
                        sp.wait_ge(s_mm, before[1] + 1 + i * RING)
                    else:
                        sp.wait_ge(q("ada"), before[1] + 1)
                sp.dma_start(raw[n % RING][:, 0:s.size], w[s.name][slot + i * RING]).then_inc(s_load[n % RING], 16)

            for s in order:
                turns = s.slots // RING
                if s.split and turns >= 2:
                    with sp.Fori(0, turns) as i:
                        for slot in range(RING):
                            load(s, slot, i)
                    rest = range(turns * RING, s.slots)
                else:
                    rest = range(s.slots)
                for slot in rest:
                    load(s, slot)
                    if s.n0 == 0 and slot == 1:
                        sp.dma_start(par[:], par_d).then_inc(s_par, 16)
                        sp.dma_start(rows[:], rows_d).then_inc(s_par, 16)
                        sp.dma_start(X[:], xT_d).then_inc(s_in, 16)
            for ft in range(KC):
                sp.wait_ge(q("final"), ft + 1)
                sp.dma_start(out_d[:, ft, :], T8[:, ft, :]).then_inc(s_out, 16)
            sp.wait_ge(s_out, 16 * KC)

        @block.tensor
        def _(pe):
            mm = nc.tensor.matmul

            def mm3(out, l_hi, l_lo, r_hi, r_lo, start, stop):
                mm(out, l_hi, r_hi, start=start, stop=False)
                mm(out, l_hi, r_lo, start=False, stop=False)
                return mm(out, l_lo, r_hi, start=False, stop=stop)

            def slot_begins(s, slot, j, i, groups):
                pe.wait_ge(s_lo, s.m0 + slot + 1 + i * RING)
                if j is not None and j >= 2:
                    pe.wait_ge(s_ev[j % 2], j // 2 + i * (groups // 2))

            def gemm_a(s, slot, j, x_h, x_l, kn=KC, nf=2, k0=0, start=True, stop=True, cols=S,
                       ready=None, i=0, groups=4):
                n = s.n0 + slot
                slot_begins(s, slot, j if start else None, i, groups)
                wh = w_hi[n % RING][:, 0:kn * nf * P].rearrange("p (k f c) -> p k f c", k=kn, f=nf)
                wl = w_lo[n % RING][:, 0:kn * nf * P].rearrange("p (k f c) -> p k f c", k=kn, f=nf)
                for f in range(nf):
                    for k in range(kn):
                        if ready and f == 0:
                            pe.wait_ge(q(ready), nth(ready, k + 1))
                        last = mm3(G[j % 2][:, f * S:f * S + cols], wh[:, k, f, :], wl[:, k, f, :],
                                   x_h[:, k0 + k, 0:cols], x_l[:, k0 + k, 0:cols],
                                   start and k == 0, stop and k == kn - 1)
                last.then_inc(s_mm, 1)

            def gemm_b(s, slot, j, x_h, x_l, width=256, ready=None, k0=0):
                n = s.n0 + slot
                slot_begins(s, slot, j, 0, 4)
                wh = w_hi[n % RING][:, 0:KC * width].rearrange("p (k c) -> p k c", k=KC)
                wl = w_lo[n % RING][:, 0:KC * width].rearrange("p (k c) -> p k c", k=KC)
                for t in range(2):
                    for k in range(KC):
                        if ready and t == 0:
                            pe.wait_ge(q(ready), nth(ready, k + 1))
                        tk = slice(t * P, t * P + P)
                        last = mm3(G[j % 2][:, t * width:(t + 1) * width], x_h[:, k0 + k, tk], x_l[:, k0 + k, tk],
                                   wh[:, k, :], wl[:, k, :], k == 0, k == KC - 1)
                last.then_inc(s_mm, 1)

            def mean(name, bank, by_token=False):
                pe.wait_ge(q(name + ".acc"), nth(name + ".acc", KC))
                last = mm(bank[:, 0:S], ones_d[:], acc[:], start=True, stop=True)
                last.then_inc(q(name + ".mean"), 1)
                if by_token:
                    for t in range(2):
                        last = mm(T[0][:, t:t + 1], acc[:, t * P:(t + 1) * P], ones_d[:, 0:1], start=True, stop=True)
                    last.then_inc(q(name + ".mean"), 1)

            def mean8(name, bank):
                for k in range(KC):
                    last = mm(bank[:, 0:S], ones_d[:], T8[:, k, :], start=k == 0, stop=k == KC - 1)
                last.then_inc(q(name + ".var"), 1)

            def transposes(name, src):
                pe.wait_ge(q(name + ".y"), nth(name + ".y", 1))
                for b in range(4):
                    if b >= 2:
                        pe.wait_ge(q(name + ".tev"), nth(name + ".tev", b - 1))
                    for f in range(2):
                        for t in range(2):
                            ft = 2 * b + f
                            last = nc.tensor.transpose(T[b % 2][:, f * S + t * P:f * S + t * P + P],
                                                       src[:, t, ft * P:(ft + 1) * P], ident[:])
                    last.then_inc(q(name + ".tr"), 1)

            def attention(name, heads, hd, keys, qk, pv):
                units = [(h, t) for h in range(heads) for t in range(2)]
                per = 512 // hd
                for step in range(len(units) + 2):
                    if step < len(units):
                        h, t = units[step]
                        if step >= 2:
                            pe.wait_ge(q(name + ".l"), nth(name + ".l", step - 1))
                        qk(h, t, L[step % 2]).then_inc(q(name + ".qk"), 1)
                    if 1 <= step <= len(units):
                        u = step - 1
                        h, t = units[u]
                        nk = keys(t)
                        pe.wait_ge(q(name + ".p"), nth(name + ".p", u + 1))
                        if u >= 2:
                            pe.wait_ge(q(name + ".pt"), nth(name + ".pt", u - 1))
                        for c in range((nk + P - 1) // P):
                            w_ = min(P, nk - c * P)
                            last = nc.tensor.transpose(T[u % 2][0:w_, c * P:(c + 1) * P],
                                                       Pr[u % 2][:, c * P:c * P + w_], ident[:])
                        last.then_inc(q(name + ".tp"), 1)
                    if step >= 2:
                        u = step - 2
                        h, t = units[u]
                        nk = keys(t)
                        pe.wait_ge(q(name + ".pt"), nth(name + ".pt", u + 1))
                        half = h // per
                        if half and h % per == 0:
                            pe.wait_ge(q(name + ".o"), nth(name + ".o", 2 * (half - 1) + t + 1))
                        nch = (nk + P - 1) // P
                        for c in range(nch):
                            w_ = min(P, nk - c * P)
                            last = mm(O[t][:, (h % per) * hd:(h % per + 1) * hd], PT[u % 2][0:w_, c, :],
                                      pv(h, c), start=c == 0, stop=c == nch - 1)
                        last.then_inc(q(name + ".pv"), 1)

            pe.wait_ge(q("consts"), 1)
            pe.wait_ge(q("mem.sq"), 1)
            mean8("mem", L[1])
            for slot in range(4):
                gemm_b(st["z"], slot, st["z"].j0 + slot, x_hi, x_lo, ready="h0.lo" if slot == 0 else None)
            for slot in range(6):
                gemm_a(st["xbc"], slot, st["xbc"].j0 + slot, x_hi, x_lo)
            gemm_b(st["dtf"], 0, st["dtf"].j0, x_hi, x_lo, width=32)
            pe.wait_ge(q("ssm.a"), 1)
            mm(L[1][:, 0:H], SG[:, P:2 * P], a_t[:, 0, :], start=True, stop=True)
            mm(L[1][:, H:2 * H], U[:], a_t[:, 1, :], start=True, stop=True).then_inc(q("ssm.cs"), 1)
            for b in range(4):
                t, fh = divmod(b, 2)
                pe.wait_ge(q("ssm.conv"), 4 * fh + 4)
                if b >= 2:
                    pe.wait_ge(q("ssm.xt"), b - 1)
                for k in range(4):
                    last = nc.tensor.transpose(T[b % 2][:, k * P:(k + 1) * P], XB[:, 4 * fh + k, t * P:(t + 1) * P], ident[:])
                last.then_inc(q("ssm.xtr"), 1)
            pe.wait_ge(q("ssm.conv"), 12)
            for g in range(2):
                last = nc.tensor.transpose(L[0][:, g * P:(g + 1) * P], XB[:, 8 + g, 0:P], ident[:])
            last.then_inc(q("ssm.bt"), 1)
            for cg in range(4):
                c, g = divmod(cg, 2)
                last = mm(O[0][:, cg * P:(cg + 1) * P], XB[:, 8 + g, c * P:(c + 1) * P],
                          XB[:, 10 + g, c * P:(c + 1) * P], start=True, stop=True)
            last.then_inc(q("ssm.cb"), 1)
            pe.wait_ge(q("ssm.xce"), 1)
            pe.wait_ge(q("ssm.bts"), 1)
            for g in range(2):
                pe.wait_ge(q("ssm.xt"), 3 + g)
                mm(T[g][:, :], BT[:, g, :], xce[:, g * 512:(g + 1) * 512], start=True, stop=True).then_inc(q("ssm.state"), 1)
            for g in range(2):
                pe.wait_ge(q("ssm.st"), g + 1)
                mm(L[g][:, :], XB[:, 10 + g, P:2 * P], STt[:, g, :], start=True, stop=True).then_inc(q("ssm.off"), 1)
            pe.wait_ge(q("ssm.cbm"), 1)
            for u in range(9):
                if u < 8:
                    pe.wait_ge(q("ssm.as"), u + 1)
                    if u >= 2:
                        pe.wait_ge(q("ssm.e"), u - 1)
                    for k in range(4):
                        last = mm(T[u % 2][:, k * P:(k + 1) * P], AS[u % 2][:, k, :], U[:], start=True, stop=True)
                    last.then_inc(q("ssm.seg"), 1)
                if u >= 1:
                    v = u - 1
                    c, g, hq = v // 4, v // 2 % 2, v % 2
                    pe.wait_ge(q("ssm.sc"), v + 1)
                    if v >= 4 and hq == 0:
                        pe.wait_ge(q("ssm.yo"), v // 2 - 1)
                    for k in range(4):
                        h = 8 * g + 4 * hq + k
                        last = mm(O[g][:, (4 * hq + k) * HD:(4 * hq + k + 1) * HD], E[v % 2][:, k, :],
                                  xc[:, c, h * HD:(h + 1) * HD], start=True, stop=True)
                    last.then_inc(q("ssm.ydiag"), 1)
            transposes("ssmt", Y)

            for slot in range(4):
                gemm_a(st["q"], slot, st["q"].j0 + slot, x_hi, x_lo)
            for slot in range(4):
                gemm_a(st["k"], slot, st["k"].j0 + slot, x_hi, x_lo)
            for slot in range(4):
                gemm_b(st["v"], slot, st["v"].j0 + slot, x_hi, x_lo)

            def qk_fox(h, t, bank):
                half = slice((h % 2) * HD, (h % 2 + 1) * HD)
                if t == 0:
                    pe.wait_ge(q("fox.rb"), h + 1)
                    mm(bank[:, 0:P], U[:], RB[h % 2][:, 0:P], start=True, stop=False)
                    return mm(bank[:, 0:P], qT[half, h // 2, 0:P], kT[half, h // 2, 0:P], start=False, stop=True)
                mm(bank[:, 0:S], U[:], RB[h % 2][:, P:3 * P], start=True, stop=False)
                mm(bank[:, 0:P], ones[:], RB[h % 2][:, 0:P], start=False, stop=False)
                return mm(bank[:, 0:S], qT[half, h // 2, P:S], kT[half, h // 2, :], start=False, stop=True)

            all_taken(pe, st["wout"].j0)
            attention("fox", H, HD, lambda t: P * (t + 1), qk_fox, lambda h, c: V[:, c, h * HD:(h + 1) * HD])
            transposes("foxt", AO)

            s = st["wout"]
            pe.wait_ge(q("ssmt.lo"), nth("ssmt.lo", KC))
            pe.wait_ge(q("foxt.lo"), nth("foxt.lo", KC))
            for slot in range(8):
                gemm_a(s, slot, s.j0 + slot, hid_hi, hid_lo, kn=16, nf=1)
            mean("wout", L[0])
            pe.wait_ge(q("wout.sq8"), 1)
            mean8("wout", L[1])

            def ffn_in(s, ready, after_first=None):
                gemm_a(s, 0, s.j0, x_hi, x_lo, ready=ready)
                if after_first:
                    after_first()
                for slot in range(1, 4):
                    gemm_a(s, slot, s.j0 + slot, x_hi, x_lo)
                turns = s.slots // RING - 1
                with pe.Fori(0, turns) as i:
                    for slot in range(4, 8):
                        gemm_a(s, slot, s.j0 + slot, x_hi, x_lo, i=i)
                for slot in range(4 + 4 * turns, s.slots):
                    gemm_a(s, slot, s.j0 + slot, x_hi, x_lo)

            def ffn_out(s, hidden, chunks, per_slot):
                kn = chunks // 2

                def tile_of(g, i=0, first=False):
                    for part in range(2):
                        if first:
                            pe.wait_ge(q(hidden), nth(hidden, (part + 1) * kn // per_slot))
                        gemm_a(s, 2 * g + part, s.j0 + g, hid_hi, hid_lo, kn=kn, nf=1, k0=part * kn,
                               start=part == 0, stop=part == 1, i=i, groups=2)

                tile_of(0, first=True)
                tile_of(1)
                with pe.Fori(0, 3) as i:
                    tile_of(2, i)
                    tile_of(3, i)

            ffn_in(st["ffin"], "ln1.lo")
            ffn_out(st["ffout"], "ffin.lo", HID1, 2)
            mean("ffout", L[0])
            pe.wait_ge(q("ffout.sq8"), 1)
            mean8("ffout", L[1])

            def ffn(l, f, before):
                ffn_in(st[f"f{f}in{l}"], before + ".lo", lambda: mean(before, L[0]))
                ffn_out(st[f"f{f}out{l}"], f"f{f}in{l}.lo", HID2, 1)

            def xattn(l, before):
                name = f"xa{l}"
                j = {x: st[f"x{x}{l}"].j0 for x in "kvqo"}
                for slot in range(4):
                    gemm_a(st[f"xk{l}"], slot, j["k"] + slot, hid_hi, hid_lo, k0=8,
                           ready=f"mem{l}.lo" if slot == 0 else None)
                for slot in range(4):
                    gemm_b(st[f"xv{l}"], slot, j["v"] + slot, hid_hi, hid_lo, k0=8)
                for slot in range(4):
                    gemm_a(st[f"xq{l}"], slot, j["q"] + slot, x_hi, x_lo,
                           ready=before + ".lo" if slot == 0 else None)
                    if slot == 0:
                        mean(before, L[0])
                all_taken(pe, j["o"])

                def qk(h, t, bank):
                    for c in range(2):
                        last = mm(bank[:, 0:S], qT[:, 2 * h + c, t * P:(t + 1) * P], kT[:, 2 * h + c, :],
                                  start=c == 0, stop=c == 1)
                    return last

                attention(name, XH, 256, lambda t: S, qk, lambda h, c: V[:, c, h * 256:(h + 1) * 256])
                transposes(name + "t", AO)
                for slot in range(4):
                    gemm_a(st[f"xo{l}"], slot, j["o"] + slot, hid_hi, hid_lo,
                           ready=name + "t.lo" if slot == 0 else None)

            ffn(0, 1, "ln2")
            mean("f1out0", L[0])
            s = st["pool"]
            pe.wait_ge(s_lo, s.m0 + 1)
            for g in range(4):
                j = s.j0 + g
                pe.wait_ge(s_ev[j % 2], j // 2)
                pe.wait_ge(q("pmix.lo"), g + 1)
                wh = w_hi[s.n0 % RING][:, :].rearrange("p (g k f c) -> p g k f c", g=4, k=2, f=2)
                wl = w_lo[s.n0 % RING][:, :].rearrange("p (g k f c) -> p g k f c", g=4, k=2, f=2)
                for f in range(2):
                    for k in range(2):
                        last = mm3(G[j % 2][:, f * S:(f + 1) * S], wh[:, g, k, f, :], wl[:, g, k, f, :],
                                   x_hi[:, 2 * g + k, :], x_lo[:, 2 * g + k, :], k == 0, k == 1)
                last.then_inc(q("pmix.mm") if g < 3 else s_mm, 1)
            xattn(0, "pool")
            ffn(0, 2, "xo0")

            ffn(1, 1, "f2out0")
            for slot in range(4):
                gemm_a(st["nq"], slot, st["nq"].j0 + slot, x_hi, x_lo,
                       ready="f1out1.lo" if slot == 0 else None)
                if slot == 0:
                    mean("f1out1", L[0], by_token=True)
            for name in ("nkc", "nvc", "nks", "nkw"):
                gemm_a(st[name], 0, st[name].j0, x_hi, x_lo)
            for name, width in (("nvs", 256), ("nvw", 256), ("ng", 48)):
                gemm_b(st[name], 0, st[name].j0, x_hi, x_lo, width=width)
            for b, name in enumerate(("cmpk", "cmpv")):
                pe.wait_ge(q("nsa.bk"), b + 1)
                for slot in range(2):
                    gemm_a(st[name], slot, st[name].j0 + slot, bk_hi[b], bk_lo[b], kn=16, nf=1, cols=60)
            w2k = par[:, COL["w2k"]:COL["w2k"] + 256].rearrange("p (k c) -> p k c", k=2)
            w2v = par[:, COL["w2v"]:COL["w2v"] + 128].rearrange("p (k c) -> p k c", k=2)
            all_taken(pe, st["cmpv"].j0)
            for k in range(2):
                last = mm(T[0][:, 0:60], w2k[:, k, :], HG[:, k, :], start=k == 0, stop=k == 1)
            last.then_inc(q("nsa.kc"), 1)
            all_taken(pe, st["no"].j0)
            for k in range(2):
                last = mm(T[1][0:HB, 0:HD], HX[:, k, :], w2v[:, k, :], start=k == 0, stop=k == 1)
            last.then_inc(q("nsa.kc"), 1)
            pe.wait_ge(q("nsa.ready"), 1)
            for t in range(2):
                for h in range(H):
                    half = slice((h % 2) * HD, (h % 2 + 1) * HD)
                    mm((L, G)[t][h % 2][:, h // 2 * NCMP:(h // 2 + 1) * NCMP], qT[half, h // 2, t * P:(t + 1) * P],
                       KC_T[half, h // 4, :], start=True, stop=True).then_inc(q("nc.qk"), 1)
            pe.wait_ge(q("nsa.vc"), 1)
            for t in range(2):
                pe.wait_ge(q("nc.w"), t + 1)
                for half in range(2):
                    last = nc.tensor.transpose(T[t][0:HB, half * P:(half + 1) * P],
                                               LC[:, t, half * HB:(half + 1) * HB], ident[:])
                last.then_inc(q("nc.tp"), 1)
            for t in range(2):
                pe.wait_ge(q("nc.pt"), t + 1)
                for half in range(2):
                    mm((O, G)[t][half][:, :], PT[t][0:HB, half, :], VB[0:HB, :], start=True, stop=True)\
                        .then_inc(q("nc.pv"), 1)

            def qk_nsa(keys_of):
                def f(h, t, bank):
                    half = slice((h % 2) * HD, (h % 2 + 1) * HD)
                    k = keys_of(half, h // 4, t)
                    return mm(bank[:, 0:k.shape[-1]], qT[half, h // 2, t * P:(t + 1) * P], k, start=True, stop=True)
                return f

            pe.wait_ge(q("nc.o"), 4)
            attention("ns", H, HD, lambda t: P * (t + 1), qk_nsa(lambda hf, g, t: ksd[hf, g, 0:P * (t + 1)]),
                      lambda h, c: vs[:, c, (h // 4) * HD:(h // 4 + 1) * HD])
            pe.wait_ge(q("ns.o"), nth("ns.o", 4))
            attention("nw", H, HD, lambda t: P * (t + 1), qk_nsa(lambda hf, g, t: kwd[hf, g, 0:P * (t + 1)]),
                      lambda h, c: vw[:, c, (h // 4) * HD:(h // 4 + 1) * HD])
            transposes("nsat", AO)
            for slot in range(4):
                gemm_a(st["no"], slot, st["no"].j0 + slot, hid_hi, hid_lo,
                       ready="nsat.lo" if slot == 0 else None)
            xattn(1, "no")
            ffn(1, 2, "xo1")
            mean("f2out1", L[0])

        @block.scalar
        def _(act):
            act_ = nc.scalar.activation
            own = Chain(act, "act_own")
            at = [0]

            def split(s, slot, i=0):
                n = s.n0 + slot
                act.wait_ge(s_load[n % RING], 16 * (n // RING + 1) + 16 * i)
                act_(w_hi[n % RING][:, 0:s.size], raw[n % RING][:, 0:s.size], ACT.Copy).then_inc(s_hi, 1)

            def splits_to(k):
                while at[0] <= min(k, len(split_order) - 1):
                    split(*split_order[at[0]])
                    at[0] += 1

            def result(s, slot, i=0):
                act.wait_ge(s_mm, s.m0 + slot + 1 + i * RING)

            def root(name, bank, eps, event=".mean", count=1, out=Rs[:]):
                act.wait_ge(q(name + event), nth(name + event, count))
                act_(out, bank, ACT.Sqrt, bias=eps[:]).then_inc(q(name + ".root"), 1)

            def copies(s, outs, func=ACT.Copy, scale=1.0):
                for slot in range(s.slots):
                    splits_to(s.m0 + slot + AHEAD)
                    result(s, slot)
                    act_(outs(slot), tiles2(G[(s.j0 + slot) % 2]), func, scale=scale).then_inc(s_ev[(s.j0 + slot) % 2], 1)

            def row_squares(name, src, junk):
                act.wait_ge(q(name + ".in"), nth(name + ".in", 1))
                for t in range(2):
                    act_(junk, src[:, t, :], ACT.Square, accum_out=rtok[:, t:t + 1]).then_inc(q(name + ".ss"), 1)
                    act.wait_ge(q(name + ".ss"), nth(name + ".ss", t + 1))
                act_(rtoks[:], rtok[:], ACT.Sqrt, bias=eps1[:], scale=1.0 / D).then_inc(q(name + ".root"), 1)

            def features_hi(name, chunk0, gain=None):
                for b in range(4):
                    act.wait_ge(q(name + ".tr"), nth(name + ".tr", b + 1))
                    for f in range(2):
                        ft = 2 * b + f
                        act_(hid_hi[:, chunk0 + ft, :], T[b % 2][:, f * S:(f + 1) * S], ACT.Copy,
                             scale=pc(gain, ft) if gain else 1.0).then_inc(q(name + ".hi"), 1)

            def attention(name, heads, keys, base):
                for u in range(2 * heads):
                    h, t = divmod(u, 2)
                    act.wait_ge(q(name + ".l"), nth(name + ".l", u + 1))
                    if u >= 2:
                        act.wait_ge(q(name + ".tp"), nth(name + ".tp", u - 1))
                    nk, col = keys(t), base + t * heads + h
                    act_(Pr[u % 2][:, 0:nk], Lm[u % 2][:, 0:nk], ACT.Exp, bias=nmax[:, col:col + 1], scale=-1.0,
                         accum_out=ssum[:, col:col + 1]).then_inc(q(name + ".p"), 1)

            def hi_and_squares(name, ft, gain, squares=True):
                if gain:
                    act_(x_hi[:, ft, :], X[:, ft, :], ACT.Copy, scale=pc(*gain(ft))).then_inc(q(name + ".hi"), 1)
                if squares:
                    act_(T8[:, ft, :], X[:, ft, :], ACT.Square).then_inc(q(name + ".sq"), 1)

            def residual(name, s, gain, nf, per):
                for g in range(KC // nf):
                    if s.name != "pool":
                        splits_to(s.m0 + g * per + per - 1 + AHEAD)
                    taken(act, s.j0 + g)
                    for f in range(nf):
                        hi_and_squares(name, g * nf + f, gain)

            def ffn_in(s, before, width, chunks):
                def slot_(slot, i=0):
                    j = s.j0 + slot
                    if chunks == 2:
                        result(s, slot, i)
                        act_(sg[slot % 2][:, :], G[j % 2][:, :], ACT.Relu).then_inc(s_ev[j % 2], 1)
                    else:
                        taken(act, j, i)
                        act_(sg[slot % 2][:, 0:S], gu[slot % 2][:, 0, :], ACT.Silu).then_inc(q(s.name + ".sg"), 1)
                    act.wait_ge(q(s.name + ".h"), nth(s.name + ".h", slot + 1 + i * RING))
                    c0 = chunks * slot + i * (chunks * RING)
                    act_(hid_hi[:, bass.ds(c0, chunks), :], hb[slot % 2][:, 0:width].rearrange("p (k c) -> p k c", k=chunks),
                         ACT.Copy).then_inc(q(s.name + ".hi"), 1)

                for slot in range(4):
                    splits_to(s.m0 + slot + AHEAD)
                    if slot == 0 and before:
                        root(before, L[0][:, 0:S], eps2)
                    slot_(slot)
                turns = (s.slots - AHEAD) // RING - 1
                with act.Fori(0, turns) as i:
                    for slot in range(4, 8):
                        split(s, slot + AHEAD, i)
                        slot_(slot, i)
                at[0] += turns * RING
                for slot in range(4 + 4 * turns, s.slots):
                    splits_to(s.m0 + slot + AHEAD)
                    slot_(slot)

            act.wait_ge(q("cond_in"), 16)
            act_(cond[:], cond[:], ACT.Silu).then_inc(q("cact"), 1)
            act.wait_ge(q("mem_in"), 16)
            act_(T8[:], memN[:], ACT.Square).then_inc(q("mem.sq"), 1)
            act.wait_ge(q("consts"), 1)
            act.wait_ge(s_par, 32)
            root("mem", L[1][:, 0:S], eps2, ".var")
            splits_to(1)
            for ft in range(KC):
                act.wait_ge(q("h0.t"), ft + 1)
                act_(x_hi[:, ft, :], T8[:, ft, :], ACT.Copy).then_inc(q("h0.hi"), 1)
            copies(st["z"], lambda k: Zs[:, :, k * 256:(k + 1) * 256], ACT.Silu)
            s = st["xbc"]

            def conv_silu(ft):
                act.wait_ge(q("ssm.cv"), ft + 1)
                act_(XB[:, ft, :], XB[:, ft, :], ACT.Silu).then_inc(q("ssm.conv"), 1)

            act.wait_ge(q("ssm.pad"), 1)
            for slot in range(s.slots):
                splits_to(min(s.m0 + slot + AHEAD, st["dtf"].m0))
                result(s, slot)
                act_(CX[:, 2 * slot:2 * slot + 2, 3:3 + S], tiles2(G[(s.j0 + slot) % 2]), ACT.Copy)\
                    .then_inc(s_ev[(s.j0 + slot) % 2], 1)
                if slot:
                    conv_silu(2 * slot - 2)
                    conv_silu(2 * slot - 1)
            conv_silu(10)
            conv_silu(11)
            act.wait_ge(q("ssm.v"), 1)
            own(act_(tok["mag"][:], tok["v"][:], ACT.Abs))
            act_(tok["e"][:], tok["mag"][:], ACT.Exp, scale=-1.0).then_inc(q("ssm.exp"), 1)
            act_(negA[:], rows[:, 32:48], ACT.Exp).then_inc(q("ssm.exp"), 1)
            act.wait_ge(q("ssm.cs"), 1)
            act_(dend[:], L[1][:, 0:H], ACT.Exp).then_inc(q("ssm.ex"), 1)
            act_(dout[:], L[1][:, H:2 * H], ACT.Exp).then_inc(q("ssm.ex"), 1)
            for b in range(4):
                t, fh = divmod(b, 2)
                act.wait_ge(q("ssm.xtr"), b + 1)
                act_(XsT[:, t, fh * 512:(fh + 1) * 512], T[b % 2][:, :], ACT.Copy).then_inc(q("ssm.xt"), 1)
            act.wait_ge(q("ssm.bt"), 1)
            act_(BT[:], L[0][:, 0:S].rearrange("p (g c) -> p g c", g=2), ACT.Copy).then_inc(q("ssm.bts"), 1)
            for g in range(2):
                act.wait_ge(q("ssm.state"), g + 1)
                act_(STt[:, g, :], T[g][:, :], ACT.Copy).then_inc(q("ssm.st"), 1)
            for u in range(8):
                act.wait_ge(q("ssm.seg"), u + 1)
                if u >= 2:
                    act.wait_ge(q("ssm.ydiag"), u - 1)
                act_(E[u % 2][:], T[u % 2][:, :].rearrange("p (k c) -> p k c", k=4), ACT.Exp).then_inc(q("ssm.e"), 1)
            splits_to(st["q"].m0 + 1)
            row_squares("ssmt", Y, xce[:])
            features_hi("ssmt", 0, "ssm_w")

            for name, out in (("q", qT), ("k", kT)):
                copies(st[name], lambda k: out[:, 2 * k:2 * k + 2, :], scale=0.125 if name == "q" else 1.0)
            copies(st["v"], lambda k: V[:, :, k * 256:(k + 1) * 256])
            attention("fox", H, lambda t: P * (t + 1), 0)
            row_squares("foxt", AO, T8[:, 0:4, :].rearrange("p a b -> p (a b)"))
            features_hi("foxt", 8, "attn_w")

            def layer_norm(name, s, lng, lnb, after, per):
                act_(X[:], X[:], ACT.Copy, scale=ALPHA).then_inc(q(name + ".ax"), 1)
                for g in range(KC):
                    splits_to(s.m0 + g * per + per - 1 + AHEAD)
                act.wait_ge(q(name + ".cent"), nth(name + ".cent", 1))
                act_(T8[:], X[:], ACT.Square).then_inc(q(name + ".sq8"), 1)
                root(name, L[1][:, 0:S], eps1, ".var")
                act.wait_ge(q(name + ".xn"), nth(name + ".xn", 1))
                for ft in range(KC):
                    act_(X[:, ft, :], X[:, ft, :], ACT.Identity, bias=pc(lnb, ft), scale=pc(lng, ft))\
                        .then_inc(q(name + ".xf"), 1)
                for ft in range(KC):
                    after(ft)

            def after1(ft):
                act.wait_ge(q("ln1.t"), ft + 1)
                act_(x_hi[:, ft, :], T8[:, ft, :], ACT.Copy).then_inc(q("ln1.hi"), 1)

            def after2(ft):
                act.wait_ge(q("ffout.xf"), ft + 1)
                hi_and_squares("ln2", ft, lambda k: ("ffn1", k))

            layer_norm("wout", st["wout"], "ln1_g", "ln1_b", after1, 1)
            ffn_in(st["ffin"], None, 512, 2)
            layer_norm("ffout", st["ffout"], "ln2_g", "ln2_b", after2, 2)

            def xattn(l, before):
                name = f"xa{l}"
                copies(st[f"xk{l}"], lambda k: kT[:, 2 * k:2 * k + 2, :])
                copies(st[f"xv{l}"], lambda k: V[:, :, k * 256:(k + 1) * 256])
                for slot in range(4):
                    splits_to(st[f"xq{l}"].m0 + slot + AHEAD)
                    if slot == 0:
                        root(before, L[0][:, 0:S], eps2)
                attention(name, XH, lambda t: S, 0)
                features_hi(name + "t", 0)
                residual(f"xo{l}", st[f"xo{l}"], lambda ft: ("ffn2", 8 * l + ft), 2, 1)

            ffn_in(st["f1in0"], "ln2", 256, 1)
            residual("f1out0", st["f1out0"], None, 1, 2)
            root("f1out0", L[0][:, 0:S], eps2)
            splits_to(st["pool"].m0 + AHEAD)
            for g in range(4):
                act.wait_ge(q("pmix.p"), g + 1)
                src = (wa, wb)[g % 2]
                act_(x_hi[:, 2 * g:2 * g + 2, :], src[:, 2 * g:2 * g + 2, :], ACT.Copy).then_inc(q("pmix.hi"), 1)
            residual("pool", st["pool"], lambda ft: ("xattn", ft), 2, 0)
            xattn(0, "pool")
            ffn_in(st["f2in0"], "xo0", 256, 1)
            residual("f2out0", st["f2out0"], lambda ft: ("ffn1", 8 + ft), 1, 2)

            ffn_in(st["f1in1"], "f2out0", 256, 1)
            residual("f1out1", st["f1out1"], lambda ft: ("mix", 8 + ft), 1, 2)
            splits_to(st["nq"].m0 + AHEAD)
            root("f1out1", L[0][:, 0:S], eps2)
            root("f1out1", T[0][:, 0:2], eps2, count=2, out=RTs[:])
            for slot in range(1, 4):
                splits_to(st["nq"].m0 + slot + AHEAD)
            for b, name in enumerate(("nkc", "nvc")):
                splits_to(st[name].m0 + AHEAD)
                act.wait_ge(q("nsa.blk"), b + 1)
                act_(bk_hi[b][:], bk[:].rearrange("p j g n -> p j (g n)"), ACT.Copy).then_inc(q("nsa.bkh"), 1)
            splits_to(st["nks"].m0 + AHEAD)
            splits_to(st["nkw"].m0 + AHEAD)
            for name, out in (("nvs", vs), ("nvw", vw)):
                s = st[name]
                splits_to(s.m0 + AHEAD)
                result(s, 0)
                if name == "nvs":
                    act.wait_ge(q("nsa.rt"), 1)
                for t in range(2):
                    last = act_(out[:, t, :], G[s.j0 % 2][:, t * 256:(t + 1) * 256], ACT.Copy, scale=RT[:, t:t + 1])
                last.then_inc(s_ev[s.j0 % 2], 1)
            s = st["ng"]
            splits_to(s.m0 + AHEAD)
            result(s, 0)
            for t in range(2):
                last = act_(gates[:, t, :], G[s.j0 % 2][:, t * 48:(t + 1) * 48], ACT.Sigmoid, scale=RT[:, t:t + 1])
            last.then_inc(s_ev[s.j0 % 2], 1)
            for b, name in enumerate(("cmpk", "cmpv")):
                s = st[name]
                for slot in range(2):
                    splits_to(s.m0 + slot + AHEAD)
                    result(s, slot)
                    hidden = G[(s.j0 + slot) % 2][:, 0:60]
                    if b == 0:
                        out = HG[:, slot, :]
                    else:
                        out = HX[:, slot, :].rearrange("p (g h n) -> p g h n", g=G_KV, h=2)
                        hidden = bc(hidden.rearrange("p (g n) -> p g n", g=G_KV).unsqueeze(2), [P, G_KV, 2, NCMP])
                    act_(out, hidden, ACT.Gelu_apprx_tanh)\
                        .then_inc(s_ev[(s.j0 + slot) % 2], 1)
            act.wait_ge(q("nsa.kc"), 1)
            act_(KC_T[:], T[0][:, 0:60].rearrange("p (g n) -> p g n", g=G_KV), ACT.Copy).then_inc(q("nsa.ready"), 1)
            for t in range(2):
                act.wait_ge(q("nc.l"), t + 1)
                act_(LC[:, t, :], LC[:, t, :], ACT.Exp).then_inc(q("nc.p"), 1)
            for t in range(2):
                for half in range(2):
                    act.wait_ge(q("nc.pv"), 2 * t + half + 1)
                    act_(AO[:, t, :].rearrange("p (h two d) -> p two h d", two=2, d=HD)[:, half], h8((O, G)[t][half][:, :]),
                         ACT.Copy).then_inc(q("nc.o"), 1)
            attention("ns", H, lambda t: P * (t + 1), 32)
            attention("nw", H, lambda t: P * (t + 1), 64)
            features_hi("nsat", 0)
            residual("no", st["no"], lambda ft: ("xattn", 8 + ft), 2, 1)
            xattn(1, "no")
            ffn_in(st["f2in1"], "xo1", 256, 1)
            residual("f2out1", st["f2out1"], None, 1, 2)
            root("f2out1", L[0][:, 0:S], eps2)

        @block.vector
        def _(dve):
            v = nc.vector
            own = Chain(dve, "dve_own")
            at = [0]

            def split(s, slot, i=0):
                b = (s.n0 + slot) % RING
                dve.wait_ge(s_hi, s.m0 + slot + 1 + i * RING)
                v.tensor_tensor(w_lo[b][:, 0:s.size], raw[b][:, 0:s.size], w_hi[b][:, 0:s.size].bitcast(F32),
                                ALU.subtract).then_inc(s_lo, 1)

            def splits_to(k):
                while at[0] <= min(k, len(split_order) - 1):
                    split(*split_order[at[0]])
                    at[0] += 1

            def result(s, slot, i=0):
                dve.wait_ge(s_mm, s.m0 + slot + 1 + i * RING)

            def splits_over(s):
                for slot in range(s.slots):
                    splits_to(s.m0 + slot + AHEAD)

            def inverse(name):
                dve.wait_ge(q(name + ".root"), nth(name + ".root", 1))
                own(v.reciprocal(R[:], Rs[:]))

            def row_scale(name, src):
                dve.wait_ge(q(name + ".root"), nth(name + ".root", 1))
                own(v.reciprocal(rtok[:], rtoks[:]))
                for t in range(2):
                    last = v.tensor_scalar(src[:, t, :], src[:, t, :], rtok[:, t:t + 1], None, ALU.mult)
                last.then_inc(q(name + ".y"), 1)

            def features_lo(name, chunk0, gain=None):
                for b in range(4):
                    dve.wait_ge(q(name + ".hi"), nth(name + ".hi", 2 * b + 2))
                    for f in range(2):
                        ft = 2 * b + f
                        v.scalar_tensor_tensor(hid_lo[:, chunk0 + ft, :], T[b % 2][:, f * S:(f + 1) * S],
                                               pc(gain, ft) if gain else 1.0, hid_hi[:, chunk0 + ft, :].bitcast(F32),
                                               ALU.mult, ALU.subtract).then_inc(q(name + ".lo"), 1)
                    dve.wait_ge(q(name + ".lo"), nth(name + ".lo", 2 * b + 2))
                    dve.nop().then_inc(q(name + ".tev"), 1)

            def attention(name, heads, hd, keys, masks, base, take):
                units = [(h, t) for h in range(heads) for t in range(2)]
                per = 512 // hd
                for step in range(len(units) + 2):
                    if step < len(units):
                        h, t = units[step]
                        nk, col = keys(t), base + t * heads + h
                        dve.wait_ge(q(name + ".qk"), nth(name + ".qk", step + 1))
                        if step >= 2:
                            dve.wait_ge(q(name + ".p"), nth(name + ".p", step - 1))
                        v.tensor_tensor_reduce(out=Lm[step % 2][:, 0:nk], in0=L[step % 2][:, 0:nk], in1=masks(t),
                                               scale=-1.0, scalar=3e38, op0=ALU.add, op1=ALU.min,
                                               accum_out=nmax[:, col:col + 1]).then_inc(q(name + ".l"), 1)
                    if 1 <= step <= len(units):
                        u = step - 1
                        h, t = units[u]
                        nk = keys(t)
                        rows_, nch = min(nk, P), (nk + P - 1) // P
                        dve.wait_ge(q(name + ".tp"), nth(name + ".tp", u + 1))
                        if u >= 2:
                            dve.wait_ge(q(name + ".pv"), nth(name + ".pv", u - 1))
                        v.tensor_copy(PT[u % 2][0:rows_, 0:nch, :],
                                      T[u % 2][0:rows_, 0:nch * P].rearrange("p (c n) -> p c n", c=nch))\
                            .then_inc(q(name + ".pt"), 1)
                    if step >= 3 and (step - 1) % (2 * per) == 0:
                        half = (step - 1) // (2 * per) - 1
                        for t in range(2):
                            dve.wait_ge(q(name + ".pv"), nth(name + ".pv", 2 * per * (half + 1) - 1 + t))
                            cols = slice(base + t * heads + half * per, base + t * heads + (half + 1) * per)
                            own(v.reciprocal(rs[:, 0:per], ssum[:, cols]))
                            take(half, t)
                            dve.wait_ge(q(name + ".o"), nth(name + ".o", 2 * half + t + 1))

            def out_view(half, t):
                return AO[:, t, half * 512:(half + 1) * 512]

            def plain_take(name, per):
                def take(half, t):
                    v.tensor_tensor(out_view(half, t).rearrange("p (h d) -> p h d", h=per),
                                    O[t][:, :].rearrange("p (h d) -> p h d", h=per),
                                    bc(rs[:, 0:per].unsqueeze(2), [P, per, 512 // per]), ALU.mult)\
                        .then_inc(q(name + ".o"), 1)
                return take

            def residual(name, s, nf, per, factor, gain):
                def lo(ft):
                    dve.wait_ge(q(name + ".hi"), nth(name + ".hi", ft + 1))
                    v.scalar_tensor_tensor(x_lo[:, ft, :], X[:, ft, :], pc(*gain(ft)), x_hi[:, ft, :].bitcast(F32),
                                           ALU.mult, ALU.subtract).then_inc(q(name + ".lo"), 1)

                for g in range(KC // nf):
                    j = s.j0 + g
                    if s.name == "pool":
                        if g < 3:
                            dve.wait_ge(q("pmix.mm"), g + 1)
                        else:
                            result(s, 0)
                    else:
                        splits_to(s.m0 + g * per + per - 1 + AHEAD)
                        result(s, g * per + per - 1)
                    for f in range(nf):
                        ft = g * nf + f
                        last = v.scalar_tensor_tensor(X[:, ft, :], G[j % 2][:, f * S:(f + 1) * S],
                                                      factor if isinstance(factor, float) else factor(ft),
                                                      X[:, ft, :], ALU.mult, ALU.add)
                    last.then_inc(s_ev[j % 2], 1)
                    if gain and g:
                        for f in range(nf):
                            lo((g - 1) * nf + f)
                if gain:
                    for f in range(nf):
                        lo(KC - nf + f)

            def ffn_in(s, before, width, chunks):
                def lo(slot, i=0):
                    dve.wait_ge(q(s.name + ".hi"), nth(s.name + ".hi", slot + 1 + i * RING))
                    c0 = chunks * slot + i * (chunks * RING)
                    v.tensor_tensor(hid_lo[:, bass.ds(c0, chunks), :],
                                    hb[slot % 2][:, 0:width].rearrange("p (k c) -> p k c", k=chunks),
                                    hid_hi[:, bass.ds(c0, chunks), :].bitcast(F32), ALU.subtract)\
                        .then_inc(q(s.name + ".lo"), 1)

                def slot_(slot, split_ahead, i=0):
                    j = s.j0 + slot
                    if chunks == 2:
                        split_ahead()
                    if chunks == 1:
                        result(s, slot, i)
                        v.tensor_tensor(gu[slot % 2][:], tiles2(G[j % 2]), bc(R[:].unsqueeze(1), [P, 2, S]), ALU.mult)\
                            .then_inc(s_ev[j % 2], 1)
                        split_ahead()
                    if slot:
                        lo(slot - 1, i)
                    if chunks == 1:
                        dve.wait_ge(q(s.name + ".sg"), nth(s.name + ".sg", slot + 1 + i * RING))
                        taken(dve, j, i)
                        other = gu[slot % 2][:, 1, :]
                    else:
                        taken(dve, j, i)
                        other = sg[slot % 2][:, 0:width]
                    v.tensor_tensor(hb[slot % 2][:, 0:width], sg[slot % 2][:, 0:width], other, ALU.mult)\
                        .then_inc(q(s.name + ".h"), 1)

                for slot in range(4):
                    if slot == 0 and before:
                        inverse(before)
                    slot_(slot, lambda: splits_to(s.m0 + slot + AHEAD))
                turns = (s.slots - AHEAD) // RING - 1
                with dve.Fori(0, turns) as i:
                    for slot in range(4, 8):
                        slot_(slot, lambda: split(s, slot + AHEAD, i), i)
                at[0] += turns * RING
                for slot in range(4 + 4 * turns, s.slots):
                    slot_(slot, lambda: splits_to(s.m0 + slot + AHEAD))
                lo(s.slots - 1)

            def modulation(s, slot):
                n = s.n0 + slot
                dve.wait_ge(s_load[n % RING], 16 * (n // RING + 1))
                for f in range(2):
                    col = 2 * (n - s.m0) + f
                    w_ = raw[n % RING][:, f * D:(f + 1) * D]
                    last = v.tensor_tensor_reduce(out=w_, in0=w_, in1=cond[:], scale=1.0, scalar=0.0, op0=ALU.mult,
                                                  op1=ALU.add, accum_out=mod[:, col:col + 1])
                last.then_inc(q("ada"), 1)

            def biased(s, a_, b_):
                dve.wait_ge(q("ada"), s.n0 - s.m0 + s.slots)
                own(v.tensor_tensor(mod[:, a_:b_], mod[:, a_:b_], par[:, COL["b_ada"] + a_:COL["b_ada"] + b_], ALU.add))
                own(v.tensor_scalar(mod1[:, a_:b_], mod[:, a_:b_], 1.0, None, ALU.add))

            dve.wait_ge(q("cact"), 1)
            for slot in range(st["adaA"].slots):
                modulation(st["adaA"], slot)
            dve.wait_ge(s_par, 32)
            biased(st["adaA"], 0, 16)
            splits_to(-1)
            dve.wait_ge(s_in, 16)
            splits_to(1)
            for ft in range(KC + 1):
                if ft < KC:
                    v.tensor_scalar(T8[:, ft, :], X[:, ft, :], mod1[:, 8 + ft:9 + ft], mod[:, ft:ft + 1],
                                    ALU.mult, ALU.add).then_inc(q("h0.t"), 1)
                if ft:
                    dve.wait_ge(q("h0.hi"), ft)
                    v.tensor_tensor(x_lo[:, ft - 1, :], T8[:, ft - 1, :], x_hi[:, ft - 1, :].bitcast(F32),
                                    ALU.subtract).then_inc(q("h0.lo"), 1)
            dve.wait_ge(q("mem.root"), 1)
            own(v.reciprocal(R[:], Rs[:]))
            own(v.tensor_tensor(memN[:], memN[:], bc(R[:].unsqueeze(1), [P, KC, S]), ALU.mult))
            splits_over(st["z"])

            s = st["xbc"]
            for slot in range(s.slots):
                splits_to(min(s.m0 + slot + AHEAD, st["dtf"].m0))
                taken(dve, s.j0 + slot)
                for ft in (2 * slot, 2 * slot + 1):
                    own(v.tensor_scalar(XB[:, ft, :], CX[:, ft, 3:3 + S], pc("conv_w", 36 + ft), pc("conv_b", ft),
                                        ALU.mult, ALU.add))
                    for k in (2, 1, 0):
                        last = v.scalar_tensor_tensor(XB[:, ft, :], CX[:, ft, k:k + S], pc("conv_w", 12 * k + ft),
                                                      XB[:, ft, :], ALU.mult, ALU.add)
                        if k:
                            own(last)
                    last.then_inc(q("ssm.cv"), 1)

            s = st["dtf"]
            result(s, 0)
            t32 = lambda c0: bc(rows[:, c0:c0 + 32].unsqueeze(1), [P, 2, 32])
            v.tensor_tensor(tok["v"][:], G[s.j0 % 2][:, 0:64].rearrange("p (t c) -> p t c", t=2), t32(0), ALU.add)\
                .then_inc(s_ev[s.j0 % 2], 1)
            taken(dve, s.j0)
            v.tensor_scalar(tok["v"][:, :, 16:32], tok["v"][:, :, 16:32], -1.0, None, ALU.mult).then_inc(q("ssm.v"), 1)
            dve.wait_ge(q("ssm.exp"), 2)
            own(v.tensor_scalar(tok["den"][:], tok["e"][:], 2.0, None, ALU.add))
            own(v.reciprocal(tok["y"][:], tok["den"][:]))
            own(v.tensor_tensor(tok["y"][:], tok["y"][:], tok["e"][:], ALU.mult))
            own(v.tensor_tensor(tok["y2"][:], tok["y"][:], tok["y"][:], ALU.mult))
            own(v.tensor_scalar(tok["poly"][:], tok["y2"][:], 2.0 / 17, 2.0 / 15, ALU.mult, ALU.add))
            for k in (13, 11, 9, 7, 5, 3, 1):
                own(v.tensor_tensor(tok["poly"][:], tok["poly"][:], tok["y2"][:], ALU.mult))
                own(v.tensor_scalar(tok["poly"][:], tok["poly"][:], 2.0 / k, None, ALU.add))
            own(v.tensor_tensor(tok["poly"][:], tok["poly"][:], tok["y"][:], ALU.mult))
            own(v.scalar_tensor_tensor(tok["sp"][:], tok["v"][:], 0.0, tok["poly"][:], ALU.max, ALU.add))
            own(v.tensor_copy(dt_t[:], tok["sp"][:, :, 0:16]))
            own(v.tensor_scalar(lf[:], tok["sp"][:, :, 16:32], -1.0, None, ALU.mult))
            own(v.tensor_scalar(negA[:], negA[:], -1.0, None, ALU.mult))
            v.tensor_tensor(a_t[:], dt_t[:], bc(negA[:].unsqueeze(1), [P, 2, H]), ALU.mult).then_inc(q("ssm.a"), 1)

            ada_b = iter(range(st["adaB"].slots))

            def modulations(count):
                for _ in range(count):
                    modulation(st["adaB"], next(ada_b))

            modulations(3)
            heads8 = lambda ap: bc(ap.unsqueeze(2), [P, 8, HD])
            for b in range(4):
                t, fh = divmod(b, 2)
                dve.wait_ge(q("ssm.xt"), b + 1)
                own(v.tensor_tensor(h8(xc[:, t, fh * 512:(fh + 1) * 512]), h8(XsT[:, t, fh * 512:(fh + 1) * 512]),
                                    heads8(dt_t[:, t, 8 * fh:8 * fh + 8]), ALU.mult))
            dve.wait_ge(q("ssm.ex"), 2)
            v.tensor_tensor(xce[:].rearrange("p (h d) -> p h d", h=H), xc[:, 0, :].rearrange("p (h d) -> p h d", h=H),
                            bc(dend[:].unsqueeze(2), [P, H, HD]), ALU.mult).then_inc(q("ssm.xce"), 1)
            modulations(1)
            dve.wait_ge(q("ssm.cb"), 1)
            v.tensor_tensor(CB[:], O[0][:, :].rearrange("p (k c) -> p k c", k=4), bc(U[:].unsqueeze(1), [P, 4, P]),
                            ALU.mult).then_inc(q("ssm.cbm"), 1)
            dve.wait_ge(q("ssm.cbm"), 1)
            for u in range(9):
                if u < 8:
                    dve.wait_ge(q("ssm.e"), u + 1)
                    v.tensor_tensor(E[u % 2][:], E[u % 2][:], bc(CB[:, u // 2, :].unsqueeze(1), [P, 4, P]), ALU.mult)\
                        .then_inc(q("ssm.sc"), 1)
                    modulations(1)
                if u and u % 2 == 0:
                    c, g = divmod(u // 2 - 1, 2)
                    cols = slice(g * 512, (g + 1) * 512)
                    dve.wait_ge(q("ssm.ydiag"), u)
                    if u == 2:
                        dve.wait_ge(q("ssm.dx"), 1)
                    v.tensor_tensor(Y[:, c, cols], O[g][:, :], Y[:, c, cols], ALU.add).then_inc(q("ssm.yo"), 1)
                    if c == 1:
                        dve.wait_ge(q("ssm.off"), g + 1)
                        tmp = T8[:, 0:2, :].rearrange("p a b -> p (a b)")
                        own(v.tensor_tensor(h8(tmp), h8(L[g][:, :]), heads8(dout[:, 8 * g:8 * g + 8]), ALU.mult))
                        dve.wait_ge(q("ssm.yo"), u // 2)
                        own(v.tensor_tensor(Y[:, c, cols], Y[:, c, cols], tmp, ALU.add))
            dve.wait_ge(q("ssm.yo"), 4)
            v.tensor_tensor(Y[:], Y[:], Zs[:], ALU.mult).then_inc(q("ssmt.in"), 1)
            modulations(4)
            biased(st["adaB"], 16, 48)
            splits_to(st["q"].m0 + 1)
            row_scale("ssmt", Y)
            features_lo("ssmt", 0, "ssm_w")

            for name in "qkv":
                splits_over(st[name])
            causal = lambda t: mask[:, P:2 * P] if t == 0 else mask[:, :]
            attention("fox", H, HD, lambda t: P * (t + 1), causal, 0, plain_take("fox", 8))
            dve.wait_ge(q("fox.o"), nth("fox.o", 4))
            dve.nop().then_inc(q("foxt.in"), 1)
            row_scale("foxt", AO)
            features_lo("foxt", 8, "attn_w")

            def layer_norm(name, s, gate0, per):
                dve.wait_ge(q(name + ".ax"), nth(name + ".ax", 1))
                for g in range(KC):
                    j = s.j0 + g
                    splits_to(s.m0 + g * per + per - 1 + AHEAD)
                    result(s, g * per + per - 1)
                    v.scalar_tensor_tensor(X[:, g, :], G[j % 2][:, 0:S], mod1[:, gate0 + g:gate0 + g + 1], X[:, g, :],
                                           ALU.mult, ALU.add).then_inc(s_ev[j % 2], 1)
                dve.wait_ge(q(name + ".mean"), nth(name + ".mean", 1))
                v.tensor_tensor(X[:], X[:], bc(L[0][:, 0:S].unsqueeze(1), [P, KC, S]), ALU.subtract)\
                    .then_inc(q(name + ".cent"), 1)
                dve.wait_ge(q(name + ".root"), nth(name + ".root", 1))
                own(v.reciprocal(R[:], Rs[:]))
                v.tensor_tensor(X[:], X[:], bc(R[:].unsqueeze(1), [P, KC, S]), ALU.mult).then_inc(q(name + ".xn"), 1)

            layer_norm("wout", st["wout"], 16, 1)
            for ft in range(KC + 1):
                if ft < KC:
                    dve.wait_ge(q("wout.xf"), ft + 1)
                    v.tensor_scalar(T8[:, ft, :], X[:, ft, :], mod1[:, 32 + ft:33 + ft], mod[:, 24 + ft:25 + ft],
                                    ALU.mult, ALU.add).then_inc(q("ln1.t"), 1)
                if ft:
                    dve.wait_ge(q("ln1.hi"), nth("ln1.hi", ft))
                    v.tensor_tensor(x_lo[:, ft - 1, :], T8[:, ft - 1, :], x_hi[:, ft - 1, :].bitcast(F32),
                                    ALU.subtract).then_inc(q("ln1.lo"), 1)
            ffn_in(st["ffin"], None, 512, 2)
            layer_norm("ffout", st["ffout"], 40, 2)
            for ft in range(KC):
                dve.wait_ge(q("ln2.hi"), nth("ln2.hi", ft + 1))
                v.scalar_tensor_tensor(x_lo[:, ft, :], X[:, ft, :], pc("ffn1", ft), x_hi[:, ft, :].bitcast(F32),
                                       ALU.mult, ALU.subtract).then_inc(q("ln2.lo"), 1)

            def scaled_queries(s, scale, before):
                for slot in range(4):
                    j = s.j0 + slot
                    splits_to(s.m0 + slot + AHEAD)
                    if slot == 0:
                        inverse(before)
                    result(s, slot)
                    v.scalar_tensor_tensor(qT[:, 2 * slot:2 * slot + 2, :], tiles2(G[j % 2]), scale,
                                           bc(R[:].unsqueeze(1), [P, 2, S]), ALU.mult, ALU.mult).then_inc(s_ev[j % 2], 1)

            def xattn(l, before):
                name = f"xa{l}"
                splits_over(st[f"xk{l}"])
                splits_over(st[f"xv{l}"])
                scaled_queries(st[f"xq{l}"], 0.0625, before)
                attention(name, XH, 256, lambda t: S, lambda t: bc(zero[:], [P, S]), 0, plain_take(name, 2))
                dve.wait_ge(q(name + ".o"), nth(name + ".o", 4))
                dve.nop().then_inc(q(name + "t.y"), 1)
                features_lo(name + "t", 0)
                residual(f"xo{l}", st[f"xo{l}"], 2, 1, 1.0, lambda ft: ("ffn2", 8 * l + ft))

            ffn_in(st["f1in0"], "ln2", 256, 1)
            residual("f1out0", st["f1out0"], 1, 2, 0.5, None)
            inverse("f1out0")
            splits_to(st["pool"].m0 + AHEAD)
            for ft in range(KC):
                last = v.scalar_tensor_tensor(T8[:, ft, :], X[:, ft, :], pc("mix", ft), R[:], ALU.mult, ALU.mult)
            own(last)
            own(v.reciprocal(icnt[:], icnt[:]))
            src = T8
            for g, dst in enumerate((wa, wb, wa, wb)):
                w_, c0 = 1 << g, 2 * g
                own(v.tensor_copy(dst[:, c0:KC, 0:w_], src[:, c0:KC, 0:w_]))
                own(v.tensor_tensor(dst[:, c0:KC, w_:S], src[:, c0:KC, w_:S], src[:, c0:KC, 0:S - w_], ALU.add))
                src = dst
            for g, dst in enumerate((wa, wb, wa, wb)):
                c = slice(2 * g, 2 * g + 2)
                own(v.tensor_tensor(dst[:, c, 0:16], dst[:, c, 0:16], bc(icnt[:, g, :].unsqueeze(1), [P, 2, 16]), ALU.mult))
                own(v.tensor_tensor(dst[:, c, 0:16], dst[:, c, 0:16], T8[:, c, 0:16], ALU.subtract))
                v.scalar_tensor_tensor(dst[:, c, 16:S], dst[:, c, 16:S], 1.0 / (2 << g), T8[:, c, 16:S],
                                       ALU.mult, ALU.subtract).then_inc(q("pmix.p"), 1)
                dve.wait_ge(q("pmix.hi"), g + 1)
                v.tensor_tensor(x_lo[:, c, :], dst[:, c, :], x_hi[:, c, :].bitcast(F32), ALU.subtract)\
                    .then_inc(q("pmix.lo"), 1)
            own(v.tensor_tensor(pool_bs[:], par[:, COL["pool_b"]:COL["pool_b"] + 8],
                                par[:, COL["pool_s"]:COL["pool_s"] + 8], ALU.mult))
            for ft in range(KC):
                last = v.tensor_scalar(X[:, ft, :], X[:, ft, :], pool_bs[:, ft:ft + 1], None, ALU.add)
            own(last)
            residual("pool", st["pool"], 2, 0, lambda ft: pc("pool_s", ft), lambda ft: ("xattn", ft))
            xattn(0, "pool")
            ffn_in(st["f2in0"], "xo0", 256, 1)
            residual("f2out0", st["f2out0"], 1, 2, 0.5, lambda ft: ("ffn1", 8 + ft))

            ffn_in(st["f1in1"], "f2out0", 256, 1)
            residual("f1out1", st["f1out1"], 1, 2, 0.5, lambda ft: ("mix", 8 + ft))
            scaled_queries(st["nq"], 0.125, "f1out1")
            dve.wait_ge(q("f1out1.root"), nth("f1out1.root", 2))
            v.reciprocal(RT[:], RTs[:]).then_inc(q("nsa.rt"), 1)

            def both_halves(s, dst, shift):
                result(s, 0)
                src = tiles2(G[s.j0 % 2])
                for half in range(2):
                    for to in range(2):
                        d_ = shift * to
                        a_, b_ = slice(half * 64, half * 64 + 64), slice(to * 64, to * 64 + 64)
                        last = v.tensor_tensor(dst[b_, half:G_KV:2, 0:S - d_], src[a_, :, d_:S],
                                               bc(R[a_, d_:S].unsqueeze(1), [64, 2, S - d_]), ALU.mult)
                last.then_inc(s_ev[s.j0 % 2], 1)

            for b, name in enumerate(("nkc", "nvc")):
                s = st[name]
                splits_to(s.m0 + AHEAD)
                both_halves(s, Z, 1)
                taken(dve, s.j0)
                Zr = Z[:, :, :].rearrange("p g (n s) -> p s g n", s=16)
                pos = COL["pos_k" if b == 0 else "pos_v"]
                for hj in range(2):
                    last = v.tensor_tensor(bk[:, 8 * hj:8 * hj + 8], Zr[:, 0:16:2, :, hj:hj + NCMP],
                                           bc(par[:, pos + 8 * hj:pos + 8 * hj + 8].unsqueeze(2).unsqueeze(3),
                                              [P, 8, G_KV, NCMP]), ALU.add)
                last.then_inc(q("nsa.blk"), 1)
                dve.wait_ge(q("nsa.bkh"), b + 1)
                v.tensor_tensor(bk_lo[b][:], bk[:].rearrange("p j g n -> p j (g n)"), bk_hi[b][:].bitcast(F32),
                                ALU.subtract).then_inc(q("nsa.bk"), 1)
            for name, dst in (("nks", ksd), ("nkw", kwd)):
                splits_to(st[name].m0 + AHEAD)
                both_halves(st[name], dst, 0)
            for name in ("nvs", "nvw", "ng", "cmpk", "cmpv"):
                splits_over(st[name])

            def gated_take(name, branch):
                def take(half, t):
                    g_ = gates[:, t, 24 * half + branch:24 * half + 24:3]
                    own(v.tensor_tensor(rs[:], rs[:], g_, ALU.mult))
                    o3 = h8(O[t][:, :])
                    v.tensor_tensor(h8(Ot[:]), o3, heads8(rs[:]), ALU.mult).then_inc(q(name + ".o"), 1)
                    dve.wait_ge(q(name + ".o"), nth(name + ".o", 2 * half + t + 1))
                    own(v.tensor_tensor(out_view(half, t), out_view(half, t), Ot[:], ALU.add))
                return take

            dve.wait_ge(q("nsa.kc"), 2)
            v.tensor_tensor(h8(VB[0:HB, :]), bc(T[1][0:HB, 0:HD].unsqueeze(1), [HB, 8, HD]),
                            bc(own_rows[0:HB, :].unsqueeze(2), [HB, 8, HD]), ALU.mult)\
                .then_inc(q("nsa.vc"), 1)
            heads = lambda ap: ap.rearrange("p (h n) -> p h n", h=H)
            each = lambda ap: bc(ap.unsqueeze(2), [P, H, NCMP])
            for t in range(2):
                dve.wait_ge(q("nc.qk"), H * (t + 1))
                for odd in range(2):
                    own(v.tensor_tensor(heads(LC[:, t, :])[:, 8 * odd:8 * odd + 8],
                                        (L, G)[t][odd][:, 0:HB].rearrange("p (h n) -> p h n", h=8),
                                        bc(cmask[:, t, :].unsqueeze(1), [P, 8, NCMP]), ALU.add))
                own(v.tensor_reduce(out=wc[:, t, :], in_=heads(LC[:, t, :]), op=ALU.max, axis=AX.X))
                v.tensor_tensor(heads(LC[:, t, :]), heads(LC[:, t, :]), each(wc[:, t, :]), ALU.subtract)\
                    .then_inc(q("nc.l"), 1)
            for t in range(2):
                dve.wait_ge(q("nc.p"), t + 1)
                own(v.tensor_reduce(out=wc[:, t, :], in_=heads(LC[:, t, :]), op=ALU.add, axis=AX.X))
                own(v.reciprocal(wc[:, t, :], wc[:, t, :]))
                own(v.tensor_tensor(wc[:, t, :].rearrange("p (two h) -> p two h", two=2),
                                    wc[:, t, :].rearrange("p (two h) -> p two h", two=2),
                                    gates[:, t, :].rearrange("p (h two b) -> p b two h", two=2, b=3)[:, 0], ALU.mult))
                if t == 0:
                    own(v.tensor_scalar(wc[:, t, :], wc[:, t, :], vis[:], None, ALU.mult))
                v.tensor_tensor(heads(LC[:, t, :]), heads(LC[:, t, :]), each(wc[:, t, :]), ALU.mult).then_inc(q("nc.w"), 1)
            for t in range(2):
                dve.wait_ge(q("nc.tp"), t + 1)
                v.tensor_copy(PT[t][0:HB, :, :], T[t][0:HB, 0:2 * P].rearrange("p (c n) -> p c n", c=2)).then_inc(q("nc.pt"), 1)
            dve.wait_ge(q("nc.o"), 4)
            attention("ns", H, HD, lambda t: P * (t + 1), causal, 32, gated_take("ns", 1))
            attention("nw", H, HD, lambda t: P * (t + 1), causal, 64, gated_take("nw", 2))
            dve.nop().then_inc(q("nsat.y"), 1)
            features_lo("nsat", 0)
            residual("no", st["no"], 2, 1, 1.0, lambda ft: ("xattn", 8 + ft))
            xattn(1, "no")
            ffn_in(st["f2in1"], "xo1", 256, 1)
            residual("f2out1", st["f2out1"], 1, 2, 0.5, None)
            inverse("f2out1")
            for ft in range(KC):
                v.scalar_tensor_tensor(T8[:, ft, :], X[:, ft, :], pc("final", ft), R[:], ALU.mult, ALU.mult)\
                    .then_inc(q("final"), 1)

        @block.gpsimd
        def _(pool):
            g_ = nc.gpsimd
            own = Chain(pool, "pool_own")

            def select(out, pattern, cm, op, fill, base=0):
                own(g_.affine_select(out=out, in_=out, compare_op=op, fill=fill, base=base, pattern=pattern,
                                     channel_multiplier=cm))

            for t_, x_ in ((ones_d, 1.0 / D), (ones, 1.0), (zero, 0.0), (eps1, EPS1), (eps2, EPS2), (ident, 0.0),
                           (U, 1.0), (SG, 1.0), (mask, 0.0), (vis, 1.0), (own_rows, 1.0), (cmask, 0.0)):
                last = g_.memset(t_[:], x_)
            own(last)
            select(ident[:], [[-1, P]], 1, ALU.not_equal, 1.0)
            select(U[:], [[1, P]], -1, ALU.is_ge, 0.0)
            select(SG[:, P:2 * P], [[-1, P]], 1, ALU.is_gt, 0.0)
            select(mask[:, P:2 * P], [[-1, P]], 1, ALU.is_ge, NEG)
            select(vis[:], [[0, 1]], 1, ALU.is_ge, 0.0, base=-31)
            for t in range(2):
                select(cmask[:, t, :], [[-16, NCMP]], 1, ALU.is_ge, NEG, base=P * t - 31)
            select(own_rows[:], [[-NCMP, 8]], 1, ALU.is_ge, 0.0)
            select(own_rows[:], [[NCMP, 8]], -1, ALU.is_ge, 0.0, base=NCMP - 1)
            own(g_.iota(icnt[:, 3, :], [[1, 16]], base=1, channel_multiplier=0, allow_small_or_imprecise_dtypes=True))
            for g in range(4):
                last = g_.tensor_scalar(icnt[:, g, :], icnt[:, 3, :], float(2 << g), None, ALU.min)
            own(last)
            g_.nop().then_inc(q("consts"), 1)
            own(g_.memset(CX[:, :, 0:3], 0.0))
            g_.nop().then_inc(q("ssm.pad"), 1)

            pool.wait_ge(q("ssm.a"), 1)
            for u in range(8):
                c, g, hq = u // 4, u // 2 % 2, u % 2
                if u >= 2:
                    pool.wait_ge(q("ssm.seg"), u - 1)
                g_.tensor_tensor(AS[u % 2][:], bc(SG[:, P:2 * P].unsqueeze(1), [P, 4, P]),
                                 bc(a_t[:, c, 8 * g + 4 * hq:8 * g + 4 * hq + 4].unsqueeze(2), [P, 4, P]), ALU.mult)\
                    .then_inc(q("ssm.as"), 1)
                if u == 1:
                    pool.wait_ge(q("ssm.xt"), 4)
                    for t in range(2):
                        last = g_.tensor_tensor(Y[:, t, :].rearrange("p (h d) -> p h d", h=H),
                                                XsT[:, t, :].rearrange("p (h d) -> p h d", h=H),
                                                bc(rows[:, 48:64].unsqueeze(2), [P, H, HD]), ALU.mult)
                    last.then_inc(q("ssm.dx"), 1)
            pool.wait_ge(q("ssmt.y"), nth("ssmt.y", 1))
            for h in range(H):
                if h >= 2:
                    pool.wait_ge(q("fox.qk"), nth("fox.qk", 2 * h - 2))
                g_.tensor_scalar(RB[h % 2][:, 0:P], SG[:, P:2 * P], lf[:, 0, h:h + 1], None, ALU.mult)
                g_.tensor_scalar(RB[h % 2][:, P:3 * P], SG[:, :], lf[:, 1, h:h + 1], None, ALU.mult)\
                    .then_inc(q("fox.rb"), 1)

            def sums(name, src, event, count=lambda k: k + 1):
                for ft in range(KC):
                    event(ft)
                    if ft == 0:
                        ins = g_.tensor_copy(acc[:], src[:, 0, :])
                    else:
                        pool.wait_ge(q(name + ".acc"), nth(name + ".acc", ft))
                        ins = g_.tensor_tensor(acc[:], acc[:], src[:, ft, :], ALU.add)
                    ins.then_inc(q(name + ".acc"), 1)

            def squares(name):
                sums(name, T8, lambda ft: pool.wait_ge(q(name + ".sq"), nth(name + ".sq", ft + 1)))

            def mem(l):
                for ft in range(KC):
                    own(g_.tensor_scalar(mtmp[:, ft % 2, :], memN[:, ft, :], pc("mem", 8 * l + ft), None, ALU.mult))
                    own(g_.tensor_copy(hid_hi[:, 8 + ft, :], mtmp[:, ft % 2, :]))
                    g_.tensor_tensor(hid_lo[:, 8 + ft, :], mtmp[:, ft % 2, :], hid_hi[:, 8 + ft, :].bitcast(F32),
                                     ALU.subtract).then_inc(q(f"mem{l}.lo"), 1)

            sums("wout", X, lambda ft: taken(pool, st["wout"].j0 + ft))
            sums("ffout", X, lambda ft: taken(pool, st["ffout"].j0 + ft))
            squares("ln2")
            squares("f1out0")
            mem(0)
            squares("pool")
            squares("xo0")
            squares("f2out0")
            squares("f1out1")
            mem(1)
            squares("no")
            squares("xo1")
            squares("f2out1")


def _cols(a):
    import numpy as np
    return np.ascontiguousarray(np.reshape(a, (-1, P)).T)


def _slots(a, cols):
    import numpy as np
    k, n = a.shape
    a = np.reshape(a, (k // P, P, n // cols, cols))
    return np.ascontiguousarray(np.transpose(a, (2, 1, 0, 3)).reshape(n // cols, P, -1))


def _rows(a):
    import numpy as np
    a = np.reshape(a.T, (a.shape[1] // (2 * P), 2, P, D))
    return np.ascontiguousarray(np.transpose(a, (0, 2, 1, 3)).reshape(-1, P, 2 * D))


def _tiles(a, parts):
    import numpy as np
    k, n = a.shape
    a = np.reshape(a, (parts, k // P // parts, P, n // P, P))
    return np.ascontiguousarray(np.transpose(a, (3, 0, 2, 1, 4)).reshape(n // P * parts, P, -1))


def _pairs(a):
    import numpy as np
    k, n = a.shape
    a = np.reshape(a, (k // P, P, 2, n // 2 // P, P))
    return np.ascontiguousarray(np.transpose(a, (3, 1, 0, 2, 4)).reshape(n // 2 // P, P, -1))


def _features(a):
    import numpy as np
    return np.ascontiguousarray(np.transpose(np.reshape(a, (S, KC, P)), (2, 1, 0)))


def lay_out(x):
    import numpy as np
    g = lambda n: np.asarray(x[n])
    out = {}
    ada, w_in = g("w_ada")[0], g("w_in")[0]
    out["adaA"], out["adaB"] = _rows(ada[:, :2048]), _rows(ada[:, 2048:])
    out["z"], out["xbc"] = _slots(w_in[:, :1024], 256), _slots(w_in[:, 1024:2560], 256)
    out["dtf"] = _slots(np.concatenate([w_in[:, 2560:2576], w_in[:, 5648:5664]], 1), 32)
    for k, name in enumerate("qkv"):
        out[name] = _slots(w_in[:, 2576 + 1024 * k:3600 + 1024 * k], 256)
    out["wout"] = _tiles(g("w_out")[0], 1)
    out["ffin"], out["ffout"] = _slots(g("w_ff_in")[0], 256), _tiles(g("w_ff_out")[0], 2)
    for l in range(2):
        for f in (1, 2):
            out[f"f{f}in{l}"] = _pairs(g(f"ffn{f}_w_in_2")[l])
            out[f"f{f}out{l}"] = _tiles(g(f"ffn{f}_w_out_2")[l], 2)
        kv = g("xattn_w_kv_2")[l]
        out[f"xk{l}"], out[f"xv{l}"] = _slots(kv[:, :1024], 256), _slots(kv[:, 1024:], 256)
        out[f"xq{l}"], out[f"xo{l}"] = _slots(g("xattn_w_q_2")[l], 256), _slots(g("xattn_w_o_2")[l], 256)
    pool = np.reshape(g("pool_w_2")[0], (4, 2, P, 256))
    out["pool"] = np.ascontiguousarray(np.transpose(pool, (2, 0, 1, 3)).reshape(1, P, -1))
    nsa = g("nsa_w_in_2")[0]
    out["nq"] = _slots(nsa[:, :1024], 256)
    for k, name in enumerate(("nkc", "nvc", "nks", "nvs", "nkw", "nvw")):
        out[name] = _slots(nsa[:, 1024 + 256 * k:1280 + 256 * k], 256)
    out["ng"] = _slots(nsa[:, 2560:], 48)
    out["cmpk"], out["cmpv"] = (_tiles(g("nsa_cmp_w1_2")[0, k], 1) for k in range(2))
    out["no"] = _slots(g("nsa_w_o_2")[0], 256)

    conv = g("conv_w")[0]
    w2 = np.reshape(g("nsa_cmp_w2_2")[0], (2, 2, P, HD))
    w2k = np.transpose(w2[0], (1, 0, 2))
    pos = np.reshape(g("nsa_cmp_pos_2")[0], (2, CMP_J, P))
    parts = {"b_ada": _cols(g("b_ada")),
             "conv_w": np.concatenate([_cols(conv[k]) for k in range(4)], 1), "conv_b": _cols(g("conv_b")),
             "ssm_w": _cols(g("ssm_norm_w")), "attn_w": _cols(g("attn_norm_w")),
             "ln1_g": _cols(g("ln1_g")), "ln1_b": _cols(g("ln1_b")), "ln2_g": _cols(g("ln2_g")),
             "ln2_b": _cols(g("ln2_b")), "ffn1": _cols(g("ffn1_norm_2")), "mix": _cols(g("mix_norm_2")),
             "xattn": _cols(g("xattn_norm_2")), "mem": _cols(g("mem_norm_2")), "ffn2": _cols(g("ffn2_norm_2")),
             "pool_b": _cols(g("pool_b_2")), "pool_s": _cols(g("pool_scale_2")), "final": _cols(g("final_norm_2")),
             "pos_k": pos[0].T, "pos_v": pos[1].T,
             "w2k": np.concatenate([w2k, w2k], 2).reshape(P, 256),
             "w2v": np.transpose(w2[1], (1, 0, 2)).reshape(P, 128)}
    par = np.ascontiguousarray(np.concatenate([parts[n] for n, _ in _WIDTHS], 1))
    rows = np.concatenate([g("dt_bias")[0], g("f_bias")[0], g("a_log")[0], g("d_skip")[0]])
    rows = np.ascontiguousarray(np.broadcast_to(rows, (P, 64)))
    cond = np.ascontiguousarray(np.broadcast_to(g("c"), (P, D)))
    return out, _features(g("x")[0]), _features(g("mem_2")[0]), par, rows, cond


def kernel(**inputs):
    import numpy as np
    import concourse.bacc as bacc
    from concourse.bass_utils import run_bass_kernel_spmd

    streams, x, mem, par, rows, cond = lay_out(inputs)
    nc = bacc.Bacc("TRN2", target_bir_lowering=False, num_devices=1)
    arrays = {}

    def given(name, a):
        arrays[name] = a
        return nc.dram_tensor(name, a.shape, F32, kind="ExternalInput").ap()

    w = {name: given("w_" + name, streams[name]) for name, *_ in STAGES}
    args = [given(n, a) for n, a in (("xT", x), ("memT", mem), ("par_in", par), ("rows_in", rows),
                                 ("cond_in", cond))]
    out = nc.dram_tensor("out", (P, KC, S), F32, kind="ExternalOutput").ap()
    build(nc, w, *args, out)
    got = run_bass_kernel_spmd(nc, [arrays], core_ids=[0]).results[0]["out"]
    return np.ascontiguousarray(np.transpose(got, (2, 1, 0)).reshape(1, S, D))
```

```python
from contextlib import ExitStack

import concourse.bass as bass
from concourse import mybir

F32 = mybir.dt.float32
F32R = mybir.dt.float32r
ACT = mybir.ActivationFunctionType
ALU = mybir.AluOpType
AX = mybir.AxisListType

P = 128
S = 256
D = 1024
KC = D // P
H = 16
HD = 64
XH = 4
G_KV = 4
NCMP = (S - 32) // 16 + 1
GB = G_KV * NCMP
HB = 8 * NCMP
CMP_J = 16
HID1 = 4 * D // P
HID2 = 22
RING = 4
SLOT = 2048
AHEAD = 2
SHARE = 8
NEG = -1e30
ALPHA = 2.0 ** 0.25
EPS1, EPS2 = 1e-5, 1e-6

_WIDTHS = [("b_ada", 48), ("conv_w", 48), ("conv_b", 12), ("ssm_w", 8), ("attn_w", 8),
           ("ln1_g", 8), ("ln1_b", 8), ("ln2_g", 8), ("ln2_b", 8), ("ffn1", 16), ("mix", 16),
           ("xattn", 16), ("mem", 16), ("ffn2", 16), ("pool_b", 8), ("pool_s", 8), ("final", 8),
           ("pos_k", 16), ("pos_v", 16), ("w2k", 256), ("w2v", 128)]
COL, NPAR = {}, 0
for _name, _width in _WIDTHS:
    COL[_name] = NPAR
    NPAR += _width

_FFN = lambda l, f: [(f"f{f}in{l}", HID2, SLOT), (f"f{f}out{l}", 16, 11 * P)]
_XMEM = lambda l: [(f"xk{l}", 4, SLOT), (f"xv{l}", 4, SLOT)]
_XATTN = lambda l: [(f"xq{l}", 4, SLOT), (f"xo{l}", 4, SLOT)]
STAGES = (_XMEM(0) + [("dtf", 1, 256), ("xbc", 6, SLOT), ("z", 4, SLOT), ("q", 4, SLOT),
                      ("k", 4, SLOT), ("v", 4, SLOT), ("wouta", 4, SLOT), ("woutb", 4, SLOT),
                      ("ffin", 16, SLOT), ("ffout", 16, SLOT)]
          + _FFN(0, 1) + [("pool", 1, SLOT)] + _XATTN(0) + _FFN(0, 2)
          + _FFN(1, 1) + [("nq", 4, SLOT), ("nkc", 1, SLOT), ("nvc", 1, SLOT),
                          ("nks", 1, SLOT), ("nkw", 1, SLOT), ("nvs", 1, SLOT),
                          ("nvw", 1, SLOT), ("ng", 1, 384), ("cmpk", 2, SLOT),
                          ("cmpv", 2, SLOT)] + _XMEM(1) + [("no", 4, SLOT)] + _XATTN(1) + _FFN(1, 2))
MOD_SLOTS, MOD_FIRST = 24, 8


_FAMILIES = {
    "att": ([("fox", 32), ("xa0", 8), ("ns", 32), ("nw", 32), ("xa1", 8)],
            {k: None for k in ("qk", "l", "p", "tp", "pt", "pv")} | {"o": 4}),
    "res": ([("wout", 1), ("ln1", 1), ("ffout", 1), ("ln2", 1), ("f1out0", 1), ("pool", 1), ("xo0", 1),
             ("f2out0", 1), ("f1out1", 1), ("no", 1), ("xo1", 1), ("f2out1", 1)],
            {"hi": 8, "lo": 8, "sq": 8, "acc": 8, "mean": 1, "root": 1}),
    "ffn": ([("ffin", 16), ("f1in0", 22), ("f2in0", 22), ("f1in1", 22), ("f2in1", 22)],
            {k: None for k in ("sg", "h", "hi", "lo")}),
    "mix": ([("ssmt", 1), ("foxt", 1), ("xa0t", 1), ("nsat", 1), ("xa1t", 1)],
            {"y": 1, "tr": 4, "tev": 4, "hi": 8, "lo": 8}),
}
_ODD = {("wout", "hi"): 0, ("wout", "lo"): 0, ("wout", "sq"): 0,
        ("ln1", "sq"): 0, ("ln1", "acc"): 0, ("ln1", "mean"): 0, ("ln1", "root"): 0,
        ("ffout", "hi"): 0, ("ffout", "lo"): 0, ("ffout", "sq"): 0, ("ffin", "sg"): 0,
        ("f1out0", "hi"): 0, ("f1out0", "lo"): 0, ("f2out1", "hi"): 0, ("f2out1", "lo"): 0,
        ("f1out1", "mean"): 2, ("f1out1", "root"): 2}
SHARED = {}
for _fam, (_steps, _kinds) in _FAMILIES.items():
    for _kind, _each in _kinds.items():
        _before = 0
        for _step, _units in _steps:
            SHARED[f"{_step}.{_kind}"] = (f"{_fam}_{_kind}", _before)
            _before += _ODD.get((_step, _kind), _units if _each is None else _each)


class Stage:

    def __init__(self, name, slots, size, n0, j0):
        self.name, self.slots, self.size, self.n0, self.j0 = name, slots, size, n0, j0


def plan():
    out, n, j = {}, 0, 0
    for name, slots, size in STAGES:
        out[name] = Stage(name, slots, size, n, j)
        n += slots
        if name == "pool":
            j += 4
        else:
            j += slots // 2 if name[:3] == "cmp" or name[0] == "f" and "out" in name else slots
    return out


def build(nc, w, xT_d, memT_d, par_d, rows_d, cond_d, out_d):
    st = plan()
    split_order = [(s, k) for s in st.values() for k in range(s.slots)]
    mem_kv = nc.dram_tensor("mem_kv", (2, P, KC * S), F32).ap()
    ctx = ExitStack()
    with ctx:
        def sb(name, shape, dt=F32, stack=ctx):
            return stack.enter_context(nc.sbuf_tensor(name, shape, dt))

        def sem(name):
            return ctx.enter_context(nc.semaphore(name))

        with ExitStack() as a:
            raw = [sb(f"raw{b}", [P, SLOT], F32, a) for b in range(RING)]
        w_lo = [sb(f"w_lo{b}", [P, SLOT], F32R) for b in range(RING)]
        w_hi = [sb(f"w_hi{b}", [P, SLOT], F32R) for b in range(RING)]
        X = sb("X", [P, KC, S])
        x_hi = sb("x_hi", [P, KC, S], F32R)
        x_lo = sb("x_lo", [P, KC, S], F32R)
        memN = sb("memN", [P, KC, S])
        par = sb("par", [P, NPAR])
        rows = sb("rows", [P, 64])
        ident = sb("ident", [P, P])
        U = sb("U", [P, P])
        SG = sb("SG", [P, S])
        mask = sb("mask", [P, S])
        ones_d = sb("ones_d", [P, P])
        ones = sb("ones", [P, P])
        zero = sb("zero", [P, 1])
        eps1 = sb("eps1", [P, 1])
        eps2 = sb("eps2", [P, 1])
        mod = sb("mod", [P, 48])
        mod1 = sb("mod1", [P, 48])
        R = sb("R", [P, S])
        Rs = sb("Rs", [P, S])
        RT = sb("RT", [P, 2])
        RTs = sb("RTs", [P, 2])
        acc = sb("acc", [P, S])
        icnt = sb("icnt", [P, 4, 16])
        pool_bs = sb("pool_bs", [P, KC])
        nmax = sb("nmax", [P, 96])
        ssum = sb("ssum", [P, 96])

        mtmp = sb("mtmp", [P, 2, S])
        vis = sb("vis", [P, 1])
        cmask = sb("cmask", [P, 2, NCMP])
        KC_T = sb("KC_T", [P, G_KV, NCMP])
        own_rows = sb("own_rows", [P, 8])
        wc = sb("wc", [P, 2, H])
        gates = sb("gates", [P, 2, 48])
        tok = {n: sb("tok_" + n, [P, 2, 32]) for n in ("v", "mag", "e", "den", "y", "y2", "poly", "sp")}
        dt_t = sb("dt_t", [P, 2, H])
        lf = sb("lf", [P, 2, H])
        a_t = sb("a_t", [P, 2, H])
        negA = sb("negA", [P, H])
        dend = sb("dend", [P, H])
        dout = sb("dout", [P, H])
        rtok = sb("rtok", [P, 2])
        rtoks = sb("rtoks", [P, 2])
        rs = sb("rs", [P, 8])

        def place(name, shape, dt, kib):
            with ExitStack() as a:
                if kib:
                    sb(f"pad_{name}", [P, int(kib * 256)], F32, a)
                return sb(name, shape, dt, a)

        gu = [place(f"gu{b}", [P, 2, S], F32, 2 * b) for b in range(2)]
        sg = [place(f"sg{b}", [P, 2 * S], F32, 4 + 2 * b) for b in range(2)]
        hb = [place(f"hb{b}", [P, 2 * S], F32, 8 + 2 * b) for b in range(2)]
        Lm = [place(f"Lm{b}", [P, S], F32, b) for b in range(2)]
        Pr = [place(f"Pr{b}", [P, S], F32, 2 + b) for b in range(2)]
        PT = [place(f"PT{b}", [P, 2, P], F32, 4 + b) for b in range(2)]
        Ot = place("Ot", [P, 512], F32, 9)
        AS = [place(f"AS{b}", [P, 4, P], F32, 2 * b) for b in range(2)]
        E = [place(f"E{b}", [P, 4, P], F32, 4 + 2 * b) for b in range(2)]
        cond = place("cond", [P, D], F32, 8)
        HG = place("HG", [P, 2, 60], F32, 10)
        work_space = sb("work_space", [P, 12 * 256])

        hid_hi = place("hid_hi", [P, 32, S], F32R, 0)
        hid_lo = place("hid_lo", [P, 32, S], F32R, 32)
        T8 = place("T8", [P, KC, S], F32, 64)
        AO = place("AO", [P, 2, D], F32, 72)
        CX = place("CX", [P, 12, S + 4], F32, 0)
        Zs = place("Zs", [P, 2, D], F32, 16)
        XsT = place("XsT", [P, 2, D], F32, 24)
        XB = place("XB", [P, 12, S], F32, 32)
        STt = place("STt", [P, 2, 512], F32, 44)
        mod_w = [place(f"mod_w{k}", [P, SLOT], F32, kib) for k, kib in enumerate((8, 40, 0, 32))]
        mod_w2 = [place(f"mod_x{k}", [P, SLOT], F32, kib) for k, kib in enumerate((8, 40, 56))]
        mh = place("mh", [P, KC, S], F32R, 48)
        ml = place("ml", [P, KC, S], F32R, 56)
        V0 = place("V0", [P, 2, D], F32, 16)
        xc = place("xc", [P, 2, D], F32, 48)
        Y = place("Y", [P, 2, D], F32, 56)
        BT = place("BT", [P, 2, P], F32, 72)
        xce = place("xce", [P, D], F32, 68)
        CB = place("CB", [P, 4, P], F32, 78)
        RB = [place(f"RB{b}", [P, 384], F32, 68 + 1.5 * b) for b in range(2)]
        qT = place("qT", [P, KC, S], F32, 16)
        kT = place("kT", [P, KC, S], F32, 24)
        V = place("V", [P, 2, D], F32, 48)
        ksd = place("ksd", [P, G_KV, S], F32, 24)
        kwd = place("kwd", [P, G_KV, S], F32, 28)
        vs = place("vs", [P, 2, 256], F32, 48)
        vw = place("vw", [P, 2, 256], F32, 50)
        Z = place("Z", [P, G_KV, S], F32, 52)
        bk = place("bk", [P, CMP_J, G_KV, NCMP], F32, 56)
        bk_hi = [place(f"bk_hi{b}", [P, CMP_J, 60], F32R, 60 + 8 * b) for b in range(2)]
        bk_lo = [place(f"bk_lo{b}", [P, CMP_J, 60], F32R, 64 + 8 * b) for b in range(2)]
        Xk = place("Xk", [P, KC, S], F32, 40)
        Xv = place("Xv", [P, 2, D], F32, 8)
        LC = place("LC", [P, 2, H * NCMP], F32, 52)
        HX = place("HX", [P, 2, HB], F32, 54)
        VB = place("VB", [P, 512], F32, 56)
        GH = [place(f"GH{b}", [GB, 256], F32, 58 + b) for b in range(2)]
        wa = place("wa", [P, KC, S], F32, 16)
        wb = place("wb", [P, KC, S], F32, 24)
        arena = sb("arena", [P, 80 * 256])

        def pb(name):
            return ctx.enter_context(nc.psum_tensor(name, [P, 512], F32))

        G = [pb(f"G{b}") for b in range(2)]
        L = [pb(f"L{b}") for b in range(2)]
        T = [pb(f"T{b}") for b in range(2)]
        O = [pb(f"O{b}") for b in range(2)]

        sems = {}

        def q(name):
            key = SHARED[name][0] if name in SHARED else name.replace(".", "_")
            if key not in sems:
                sems[key] = sem(key)
            return sems[key]

        def nth(name, count):
            return (SHARED[name][1] if name in SHARED else 0) + count

        s_load = [sem(f"s_load{b}") for b in range(RING)]
        s_hi = sem("s_hi")
        s_lo = sem("s_lo")
        s_mm = sem("s_mm")
        s_ev = [sem(f"s_ev{b}") for b in range(2)]
        s_in = sem("s_in")
        s_par = sem("s_par")
        s_spill = sem("s_spill")
        s_back = sem("s_back")
        s_out = sem("s_out")

        def mod_buffer(k):
            if k < MOD_FIRST:
                return mod_w[k % 4], (k % 4, 16 * (k // 4 + 1))
            k -= MOD_FIRST
            return mod_w2[k % 3], (4 + k % 3, 16 * (k // 3 + 1))

        def xbc_slot(slot):
            return (slot + 4) % 6

        def pc(name, k=0):
            return par[:, COL[name] + k:COL[name] + k + 1]

        def bc(ap, shape):
            return ap.broadcast_to(shape)

        class Chain:

            def __init__(self, eng, name):
                self.eng, self.sem, self.n = eng, q(name), 0

            def __call__(self, ins):
                self.n += 1
                ins.then_inc(self.sem, 1)
                self.eng.wait_ge(self.sem, self.n)

        def taken(eng, j, i=0, groups=4):
            eng.wait_ge(s_ev[j % 2], j // 2 + 1 + i * (groups // 2))

        def all_taken(eng, j):
            for back in (1, 2):
                taken(eng, j - back)

        def tiles2(bank):
            return bank[:, :].rearrange("p (f c) -> p f c", f=2)

        def h8(ap):
            return ap.rearrange("p (h d) -> p h d", h=8)

        block = ctx.enter_context(nc.Block())

        @block.sync
        def _(sp):
            sp.dma_start(memN[:], memT_d).then_inc(q("mem_in"), 16)
            sp.dma_start(par[:], par_d).then_inc(s_par, 16)
            sp.dma_start(rows[:], rows_d).then_inc(s_par, 16)
            sp.dma_start(cond[:], cond_d).then_inc(q("cond_in"), 16)

            def load(s, slot, i=0):
                n = s.n0 + slot
                if n >= RING:
                    sp.wait_ge(s_mm, n - RING + 1 + i * RING)
                sp.dma_start(raw[n % RING][:, 0:s.size], w[s.name][slot + i * RING]).then_inc(s_load[n % RING], 16)

            for s in st.values():
                turns = s.slots // RING
                if s.name == "dtf":
                    all_taken(sp, st["xv0"].j0)
                    sp.dma_start(mem_kv[0], kT[:]).then_inc(s_spill, 16)
                if s.name == "xo0":
                    sp.wait_ge(s_mm, st["f1out0"].n0 + 16)
                    sp.wait_ge(s_spill, 32)
                    sp.dma_start(Xk[:], mem_kv[0]).then_inc(s_back, 16)
                    sp.dma_start(Xv[:], mem_kv[1]).then_inc(s_back, 16)
                if turns >= 2:
                    with sp.Fori(0, turns) as i:
                        for slot in range(RING):
                            load(s, slot, i)
                for slot in range(turns * RING if turns >= 2 else 0, s.slots):
                    load(s, slot)
                    if s.n0 + slot == 3:
                        sp.dma_start(X[:], xT_d).then_inc(s_in, 16)
                    if s.name == "xbc" and slot == 4:
                        all_taken(sp, st["dtf"].j0)
                        sp.dma_start(mem_kv[1], V0[:]).then_inc(s_spill, 16)
            for ft in range(KC):
                sp.wait_ge(q("final"), ft + 1)
                sp.dma_start(out_d[:, ft, :], T8[:, ft, :]).then_inc(s_out, 16)
            sp.wait_ge(s_out, 16 * KC)

        @block.tensor
        def _(pe):
            mm = nc.tensor.matmul

            def mm3(out, l_hi, l_lo, r_hi, r_lo, start, stop):
                mm(out, l_hi, r_hi, start=start, stop=False)
                mm(out, l_hi, r_lo, start=False, stop=False)
                return mm(out, l_lo, r_hi, start=False, stop=stop)

            def slot_begins(s, slot, j, i, groups):
                pe.wait_ge(s_lo, s.n0 + slot + 1 + i * RING)
                if j is not None and j >= 2:
                    pe.wait_ge(s_ev[j % 2], j // 2 + i * (groups // 2))

            def gemm_a(s, slot, j, x_h, x_l, kn=KC, nf=2, k0=0, start=True, stop=True, cols=S,
                       ready=None, i=0, groups=4):
                n = s.n0 + slot
                slot_begins(s, slot, j if start else None, i, groups)
                wh = w_hi[n % RING][:, 0:kn * nf * P].rearrange("p (k f c) -> p k f c", k=kn, f=nf)
                wl = w_lo[n % RING][:, 0:kn * nf * P].rearrange("p (k f c) -> p k f c", k=kn, f=nf)
                for f in range(nf):
                    for k in range(kn):
                        if ready and f == 0:
                            pe.wait_ge(q(ready), nth(ready, k + 1))
                        last = mm3(G[j % 2][:, f * S:f * S + cols], wh[:, k, f, :], wl[:, k, f, :],
                                   x_h[:, k0 + k, 0:cols], x_l[:, k0 + k, 0:cols],
                                   start and k == 0, stop and k == kn - 1)
                last.then_inc(s_mm, 1)

            def gemm_b(s, slot, j, x_h, x_l, width=256, ready=None, k0=0):
                n = s.n0 + slot
                slot_begins(s, slot, j, 0, 4)
                wh = w_hi[n % RING][:, 0:KC * width].rearrange("p (k c) -> p k c", k=KC)
                wl = w_lo[n % RING][:, 0:KC * width].rearrange("p (k c) -> p k c", k=KC)
                for t in range(2):
                    for k in range(KC):
                        if ready and t == 0:
                            pe.wait_ge(q(ready), nth(ready, k + 1))
                        tk = slice(t * P, t * P + P)
                        last = mm3(G[j % 2][:, t * width:(t + 1) * width], x_h[:, k0 + k, tk], x_l[:, k0 + k, tk],
                                   wh[:, k, :], wl[:, k, :], k == 0, k == KC - 1)
                last.then_inc(s_mm, 1)

            def share(s, at_, x_h, x_l, tokens_first=False, ready=None):
                slot, part = divmod(at_, SHARE)
                if slot >= s.slots:
                    return
                n, j, each = s.n0 + slot, s.j0 + slot, 2 * KC // SHARE
                if part == 0:
                    slot_begins(s, slot, j, 0, 4)
                wh = w_hi[n % RING][:, :].rearrange("p (k c) -> p k c", k=KC)
                wl = w_lo[n % RING][:, :].rearrange("p (k c) -> p k c", k=KC)
                for both in range(part * each, (part + 1) * each):
                    f, k = divmod(both, KC)
                    if ready and at_ < SHARE // 2:
                        pe.wait_ge(q(ready), nth(ready, k + 1))
                    c = slice(f * P, f * P + P)
                    if tokens_first:
                        last = mm3(G[j % 2][:, f * S:(f + 1) * S], x_h[:, k, c], x_l[:, k, c],
                                   wh[:, k, :], wl[:, k, :], k == 0, k == KC - 1)
                    else:
                        last = mm3(G[j % 2][:, f * S:(f + 1) * S], wh[:, k, c], wl[:, k, c],
                                   x_h[:, k, :], x_l[:, k, :], k == 0, k == KC - 1)
                if part == SHARE - 1:
                    last.then_inc(s_mm, 1)

            def mean(name, bank, by_token=False):
                pe.wait_ge(q(name + ".acc"), nth(name + ".acc", KC))
                last = mm(bank[:, 0:S], ones_d[:], acc[:], start=True, stop=True)
                last.then_inc(q(name + ".mean"), 1)
                if by_token:
                    for t in range(2):
                        last = mm(T[0][:, t:t + 1], acc[:, t * P:(t + 1) * P], ones_d[:, 0:1], start=True, stop=True)
                    last.then_inc(q(name + ".mean"), 1)

            def mean8(name, bank, ready=None):
                for k in range(KC):
                    if ready:
                        pe.wait_ge(q(ready), k + 1)
                    last = mm(bank[:, 0:S], ones_d[:], T8[:, k, :], start=k == 0, stop=k == KC - 1)
                last.then_inc(q(name + ".var"), 1)

            def transposes(name, src):
                pe.wait_ge(q(name + ".y"), nth(name + ".y", 1))
                for b in range(4):
                    if b >= 2:
                        pe.wait_ge(q(name + ".tev"), nth(name + ".tev", b - 1))
                    for f in range(2):
                        for t in range(2):
                            ft = 2 * b + f
                            last = nc.tensor.transpose(T[b % 2][:, f * S + t * P:f * S + t * P + P],
                                                       src[:, t, ft * P:(ft + 1) * P], ident[:])
                    last.then_inc(q(name + ".tr"), 1)

            def attention(name, heads, hd, keys, qk, pv, beside=None):
                units = [(h, t) for h in range(heads) for t in range(2)]
                per = 512 // hd
                for step in range(len(units) + 2):
                    if step < len(units):
                        h, t = units[step]
                        if step >= 2:
                            pe.wait_ge(q(name + ".l"), nth(name + ".l", step - 1))
                        qk(h, t, L[step % 2]).then_inc(q(name + ".qk"), 1)
                    if 1 <= step <= len(units):
                        u = step - 1
                        h, t = units[u]
                        nk = keys(t)
                        pe.wait_ge(q(name + ".p"), nth(name + ".p", u + 1))
                        if u >= 2:
                            pe.wait_ge(q(name + ".pt"), nth(name + ".pt", u - 1))
                        for c in range((nk + P - 1) // P):
                            w_ = min(P, nk - c * P)
                            last = nc.tensor.transpose(T[u % 2][0:w_, c * P:(c + 1) * P],
                                                       Pr[u % 2][:, c * P:c * P + w_], ident[:])
                        last.then_inc(q(name + ".tp"), 1)
                    if step >= 2:
                        u = step - 2
                        h, t = units[u]
                        nk = keys(t)
                        pe.wait_ge(q(name + ".pt"), nth(name + ".pt", u + 1))
                        half = h // per
                        if half and h % per == 0:
                            pe.wait_ge(q(name + ".o"), nth(name + ".o", 2 * (half - 1) + t + 1))
                        nch = (nk + P - 1) // P
                        for c in range(nch):
                            w_ = min(P, nk - c * P)
                            last = mm(O[t][:, (h % per) * hd:(h % per + 1) * hd], PT[u % 2][0:w_, c, :],
                                      pv(h, c), start=c == 0, stop=c == nch - 1)
                        last.then_inc(q(name + ".pv"), 1)
                    if beside:
                        beside(step)

            pe.wait_ge(q("consts"), 1)
            pe.wait_ge(q("mem.sq"), 1)
            mean8("mem", L[1])
            for slot in range(4):
                gemm_a(st["xk0"], slot, st["xk0"].j0 + slot, mh, ml, ready="mem0.lo" if slot == 0 else None)
            for slot in range(4):
                gemm_b(st["xv0"], slot, st["xv0"].j0 + slot, mh, ml)
            gemm_b(st["dtf"], 0, st["dtf"].j0, x_hi, x_lo, width=32, ready="h0.lo")
            for slot in range(6):
                gemm_a(st["xbc"], slot, st["xbc"].j0 + slot, x_hi, x_lo)

            def z_slot(slot):
                gemm_b(st["z"], slot, st["z"].j0 + slot, x_hi, x_lo)

            pe.wait_ge(q("ssm.conv"), 4)
            for g in range(2):
                last = nc.tensor.transpose(L[0][:, g * P:(g + 1) * P], XB[:, 8 + g, 0:P], ident[:])
            last.then_inc(q("ssm.bt"), 1)
            for cg in range(4):
                c, g = divmod(cg, 2)
                last = mm(O[0][:, cg * P:(cg + 1) * P], XB[:, 8 + g, c * P:(c + 1) * P],
                          XB[:, 10 + g, c * P:(c + 1) * P], start=True, stop=True)
            last.then_inc(q("ssm.cb"), 1)
            pe.wait_ge(q("ssm.a"), 1)
            mm(L[1][:, 0:H], SG[:, P:2 * P], a_t[:, 0, :], start=True, stop=True)
            mm(L[1][:, H:2 * H], U[:], a_t[:, 1, :], start=True, stop=True).then_inc(q("ssm.cs"), 1)
            z_slot(0)
            for b in range(4):
                t, fh = divmod(b, 2)
                pe.wait_ge(q("ssm.conv"), 4 * fh + 8)
                if b >= 2:
                    pe.wait_ge(q("ssm.xt"), b - 1)
                for k in range(4):
                    last = nc.tensor.transpose(T[b % 2][:, k * P:(k + 1) * P], XB[:, 4 * fh + k, t * P:(t + 1) * P], ident[:])
                last.then_inc(q("ssm.xtr"), 1)
                if b == 1:
                    z_slot(1)
            z_slot(2)
            z_slot(3)
            pe.wait_ge(q("ssm.xt"), 4)

            def chunk_states():
                pe.wait_ge(q("ssm.xce"), 1)
                pe.wait_ge(q("ssm.bts"), 1)
                all_taken(pe, st["q"].j0)
                for g in range(2):
                    mm(G[g][:, :], BT[:, g, :], xce[:, g * 512:(g + 1) * 512], start=True, stop=True)\
                        .then_inc(q("ssm.state"), 1)

            def from_states():
                for g in range(2):
                    pe.wait_ge(q("ssm.st"), g + 1)
                    mm(L[g][:, :], XB[:, 10 + g, P:2 * P], STt[:, g, :], start=True, stop=True).then_inc(q("ssm.off"), 1)

            for u in range(9):
                if u < 8:
                    pe.wait_ge(q("ssm.as"), u + 1)
                    if u >= 2:
                        pe.wait_ge(q("ssm.e"), u - 1)
                    for k in range(4):
                        last = mm(T[u % 2][:, k * P:(k + 1) * P], AS[u % 2][:, k, :], U[:], start=True, stop=True)
                    last.then_inc(q("ssm.seg"), 1)
                if u >= 1:
                    v = u - 1
                    c, g, hq = v // 4, v // 2 % 2, v % 2
                    pe.wait_ge(q("ssm.sc"), v + 1)
                    if v >= 4 and hq == 0:
                        pe.wait_ge(q("ssm.yo"), v // 2 - 1)
                    for k in range(4):
                        h = 8 * g + 4 * hq + k
                        last = mm(O[g][:, (4 * hq + k) * HD:(4 * hq + k + 1) * HD], E[v % 2][:, k, :],
                                  xc[:, c, h * HD:(h + 1) * HD], start=True, stop=True)
                    last.then_inc(q("ssm.ydiag"), 1)
                if u == 2:
                    chunk_states()
                if u == 4:
                    from_states()
            transposes("ssmt", Y)

            for slot in range(4):
                gemm_a(st["q"], slot, st["q"].j0 + slot, x_hi, x_lo)
            for slot in range(4):
                gemm_a(st["k"], slot, st["k"].j0 + slot, x_hi, x_lo)
            for slot in range(4):
                gemm_b(st["v"], slot, st["v"].j0 + slot, x_hi, x_lo)

            def qk_fox(h, t, bank):
                half = slice((h % 2) * HD, (h % 2 + 1) * HD)
                if t == 0:
                    pe.wait_ge(q("fox.rb"), h + 1)
                    mm(bank[:, 0:P], U[:], RB[h % 2][:, 0:P], start=True, stop=False)
                    return mm(bank[:, 0:P], qT[half, h // 2, 0:P], kT[half, h // 2, 0:P], start=False, stop=True)
                mm(bank[:, 0:S], U[:], RB[h % 2][:, P:3 * P], start=True, stop=False)
                mm(bank[:, 0:P], ones[:], RB[h % 2][:, 0:P], start=False, stop=False)
                return mm(bank[:, 0:S], qT[half, h // 2, P:S], kT[half, h // 2, :], start=False, stop=True)

            all_taken(pe, st["wouta"].j0)
            attention("fox", H, HD, lambda t: P * (t + 1), qk_fox, lambda h, c: V[:, c, h * HD:(h + 1) * HD],
                      lambda step: share(st["wouta"], step, hid_hi, hid_lo, ready="ssmt.lo"))
            transposes("foxt", AO)

            s = st["woutb"]
            for slot in range(4):
                gemm_a(s, slot, s.j0 + slot, hid_hi, hid_lo, k0=8, ready="foxt.lo" if slot == 0 else None)
            mean("wout", L[0])
            mean8("wout", L[1], "wout.sq8")

            def ffn_in(s, ready, after_first=None):
                gemm_a(s, 0, s.j0, x_hi, x_lo, ready=ready)
                if after_first:
                    after_first()
                for slot in range(1, 4):
                    gemm_a(s, slot, s.j0 + slot, x_hi, x_lo)
                turns = s.slots // RING - 1
                with pe.Fori(0, turns) as i:
                    for slot in range(4, 8):
                        gemm_a(s, slot, s.j0 + slot, x_hi, x_lo, i=i)
                for slot in range(4 + 4 * turns, s.slots):
                    gemm_a(s, slot, s.j0 + slot, x_hi, x_lo)

            def ffn_out(s, hidden, chunks, per_slot):
                kn = chunks // 2

                def tile_of(g, i=0, first=False):
                    for part in range(2):
                        if first:
                            pe.wait_ge(q(hidden), nth(hidden, (part + 1) * kn // per_slot))
                        gemm_a(s, 2 * g + part, s.j0 + g, hid_hi, hid_lo, kn=kn, nf=1, k0=part * kn,
                               start=part == 0, stop=part == 1, i=i, groups=2)

                tile_of(0, first=True)
                tile_of(1)
                with pe.Fori(0, 3) as i:
                    tile_of(2, i)
                    tile_of(3, i)

            ffn_in(st["ffin"], "ln1.lo")
            ffn_out(st["ffout"], "ffin.lo", HID1, 2)
            mean("ffout", L[0])
            mean8("ffout", L[1], "ffout.sq8")

            def ffn(l, f, before):
                ffn_in(st[f"f{f}in{l}"], before + ".lo", lambda: mean(before, L[0]))
                ffn_out(st[f"f{f}out{l}"], f"f{f}in{l}.lo", HID2, 1)

            def xattn(l, before):
                name = f"xa{l}"
                j = {x: st[f"x{x}{l}"].j0 for x in "qo"}
                for slot in range(4):
                    gemm_a(st[f"xq{l}"], slot, j["q"] + slot, x_hi, x_lo,
                           ready=before + ".lo" if slot == 0 else None)
                    if slot == 0:
                        mean(before, L[0])
                all_taken(pe, j["o"])
                if l == 0:
                    pe.wait_ge(s_back, 32)

                def qk(h, t, bank):
                    for c in range(2):
                        last = mm(bank[:, 0:S], qT[:, 2 * h + c, t * P:(t + 1) * P], Xk[:, 2 * h + c, :],
                                  start=c == 0, stop=c == 1)
                    return last

                attention(name, XH, 256, lambda t: S, qk, lambda h, c: Xv[:, c, h * 256:(h + 1) * 256])
                transposes(name + "t", AO)
                for slot in range(4):
                    gemm_a(st[f"xo{l}"], slot, j["o"] + slot, hid_hi, hid_lo,
                           ready=name + "t.lo" if slot == 0 else None)

            ffn(0, 1, "ln2")
            mean("f1out0", L[0])
            s = st["pool"]
            pe.wait_ge(s_lo, s.n0 + 1)
            for g in range(4):
                j = s.j0 + g
                pe.wait_ge(s_ev[j % 2], j // 2)
                pe.wait_ge(q("pmix.lo"), g + 1)
                wh = w_hi[s.n0 % RING][:, :].rearrange("p (g k f c) -> p g k f c", g=4, k=2, f=2)
                wl = w_lo[s.n0 % RING][:, :].rearrange("p (g k f c) -> p g k f c", g=4, k=2, f=2)
                for f in range(2):
                    for k in range(2):
                        last = mm3(G[j % 2][:, f * S:(f + 1) * S], wh[:, g, k, f, :], wl[:, g, k, f, :],
                                   x_hi[:, 2 * g + k, :], x_lo[:, 2 * g + k, :], k == 0, k == 1)
                last.then_inc(q("pmix.mm") if g < 3 else s_mm, 1)
            xattn(0, "pool")
            ffn(0, 2, "xo0")

            ffn(1, 1, "f2out0")
            for slot in range(4):
                gemm_a(st["nq"], slot, st["nq"].j0 + slot, x_hi, x_lo,
                       ready="f1out1.lo" if slot == 0 else None)
                if slot == 0:
                    mean("f1out1", L[0], by_token=True)
            for name in ("nkc", "nvc", "nks", "nkw"):
                gemm_a(st[name], 0, st[name].j0, x_hi, x_lo)
            for name, width in (("nvs", 256), ("nvw", 256), ("ng", 48)):
                gemm_b(st[name], 0, st[name].j0, x_hi, x_lo, width=width)
            for b, name in enumerate(("cmpk", "cmpv")):
                pe.wait_ge(q("nsa.bk"), b + 1)
                for slot in range(2):
                    s = st[name]
                    n = s.n0 + slot
                    slot_begins(s, slot, s.j0 if slot == 0 else None, 0, 4)
                    wh = w_hi[n % RING][:, :].rearrange("p (k c) -> p k c", k=KC)
                    wl = w_lo[n % RING][:, :].rearrange("p (k c) -> p k c", k=KC)
                    for k in range(KC):
                        last = mm3(G[s.j0 % 2][0:GB, 0:256], bk_hi[b][:, KC * slot + k, :], bk_lo[b][:, KC * slot + k, :],
                                   wh[:, k, :], wl[:, k, :], slot == 0 and k == 0, slot == 1 and k == KC - 1)
                    last.then_inc(s_mm, 1)
            w2k = par[:, COL["w2k"]:COL["w2k"] + 256].rearrange("p (k c) -> p k c", k=2)
            w2v = par[:, COL["w2v"]:COL["w2v"] + 128].rearrange("p (k c) -> p k c", k=2)
            for b, name in enumerate(("cmpk", "cmpv")):
                taken(pe, st[name].j0)
                for k in range(2):
                    last = nc.tensor.transpose(T[b][:, k * GB:(k + 1) * GB], GH[b][0:GB, k * P:(k + 1) * P],
                                               ident[0:GB, 0:GB])
                last.then_inc(q("nsa.ht"), 1)
            pe.wait_ge(q("nsa.hx"), 1)
            for k in range(2):
                last = mm(T[0][:, 0:60], w2k[:, k, :], HG[:, k, :], start=k == 0, stop=k == 1)
            last.then_inc(q("nsa.kc"), 1)
            pe.wait_ge(q("nsa.hx"), 2)
            for k in range(2):
                last = mm(T[1][0:HB, 0:HD], HX[:, k, :], w2v[:, k, :], start=k == 0, stop=k == 1)
            last.then_inc(q("nsa.kc"), 1)
            pe.wait_ge(q("nsa.ready"), 1)
            for t in range(2):
                for h in range(H):
                    half = slice((h % 2) * HD, (h % 2 + 1) * HD)
                    mm((L, G)[t][h % 2][:, h // 2 * NCMP:(h // 2 + 1) * NCMP], qT[half, h // 2, t * P:(t + 1) * P],
                       KC_T[half, h // 4, :], start=True, stop=True).then_inc(q("nc.qk"), 1)
            pe.wait_ge(q("nsa.vc"), 1)
            for t in range(2):
                pe.wait_ge(q("nc.w"), t + 1)
                for half in range(2):
                    last = nc.tensor.transpose(T[t][0:HB, half * P:(half + 1) * P],
                                               LC[:, t, half * HB:(half + 1) * HB], ident[:])
                last.then_inc(q("nc.tp"), 1)
            for t in range(2):
                pe.wait_ge(q("nc.pt"), t + 1)
                for half in range(2):
                    mm((O, G)[t][half][:, :], PT[t][0:HB, half, :], VB[0:HB, :], start=True, stop=True)\
                        .then_inc(q("nc.pv"), 1)

            def qk_nsa(keys_of):
                def f(h, t, bank):
                    half = slice((h % 2) * HD, (h % 2 + 1) * HD)
                    k = keys_of(half, h // 4, t)
                    return mm(bank[:, 0:k.shape[-1]], qT[half, h // 2, t * P:(t + 1) * P], k, start=True, stop=True)
                return f

            pe.wait_ge(q("nc.o"), 4)
            attention("ns", H, HD, lambda t: P * (t + 1), qk_nsa(lambda hf, g, t: ksd[hf, g, 0:P * (t + 1)]),
                      lambda h, c: vs[:, c, (h // 4) * HD:(h // 4 + 1) * HD],
                      lambda step: share(st["xk1"], step, x_hi, x_lo, ready="mem1.lo"))
            pe.wait_ge(q("ns.o"), nth("ns.o", 4))
            attention("nw", H, HD, lambda t: P * (t + 1), qk_nsa(lambda hf, g, t: kwd[hf, g, 0:P * (t + 1)]),
                      lambda h, c: vw[:, c, (h // 4) * HD:(h // 4 + 1) * HD],
                      lambda step: share(st["xv1"], step, x_hi, x_lo, tokens_first=True))
            transposes("nsat", AO)
            for slot in range(4):
                gemm_a(st["no"], slot, st["no"].j0 + slot, hid_hi, hid_lo,
                       ready="nsat.lo" if slot == 0 else None)
            xattn(1, "no")
            ffn(1, 2, "xo1")
            mean("f2out1", L[0])

        @block.scalar
        def _(act):
            act_ = nc.scalar.activation
            own = Chain(act, "act_own")
            at = [0]

            def split(s, slot, i=0):
                n = s.n0 + slot
                act.wait_ge(s_load[n % RING], 16 * (n // RING + 1) + 16 * i)
                act_(w_hi[n % RING][:, 0:s.size], raw[n % RING][:, 0:s.size], ACT.Copy).then_inc(s_hi, 1)

            def splits_to(k):
                while at[0] <= min(k, len(split_order) - 1):
                    split(*split_order[at[0]])
                    at[0] += 1

            def result(s, slot, i=0):
                act.wait_ge(s_mm, s.n0 + slot + 1 + i * RING)

            def root(name, bank, eps, event=".mean", count=1, out=Rs[:]):
                act.wait_ge(q(name + event), nth(name + event, count))
                act_(out, bank, ACT.Sqrt, bias=eps[:]).then_inc(q(name + ".root"), 1)

            def copies(s, outs, func=ACT.Copy, scale=1.0):
                for slot in range(s.slots):
                    splits_to(s.n0 + slot + AHEAD)
                    result(s, slot)
                    act_(outs(slot), tiles2(G[(s.j0 + slot) % 2]), func, scale=scale).then_inc(s_ev[(s.j0 + slot) % 2], 1)

            def row_squares(name, src, junk):
                act.wait_ge(q(name + ".in"), nth(name + ".in", 1))
                for t in range(2):
                    act_(junk, src[:, t, :], ACT.Square, accum_out=rtok[:, t:t + 1]).then_inc(q(name + ".ss"), 1)
                    act.wait_ge(q(name + ".ss"), nth(name + ".ss", t + 1))
                act_(rtoks[:], rtok[:], ACT.Sqrt, bias=eps1[:], scale=1.0 / D).then_inc(q(name + ".root"), 1)

            def features_hi(name, chunk0, gain=None):
                for b in range(4):
                    act.wait_ge(q(name + ".tr"), nth(name + ".tr", b + 1))
                    for f in range(2):
                        ft = 2 * b + f
                        act_(hid_hi[:, chunk0 + ft, :], T[b % 2][:, f * S:(f + 1) * S], ACT.Copy,
                             scale=pc(gain, ft) if gain else 1.0).then_inc(q(name + ".hi"), 1)

            def beside(s, u, out):
                slot, part = divmod(u, SHARE)
                if slot < s.slots and part < 4:
                    t, k = split_order[s.n0 + slot + AHEAD]
                    n, each = t.n0 + k, t.size // 4
                    c = slice(part * each, (part + 1) * each)
                    if part == 0:
                        act.wait_ge(s_load[n % RING], 16 * (n // RING + 1))
                    last = act_(w_hi[n % RING][:, c], raw[n % RING][:, c], ACT.Copy)
                    if part == 3:
                        last.then_inc(s_hi, 1)
                        at[0] += 1
                if part == 0:
                    if slot and out:
                        j = s.j0 + slot - 1
                        result(s, slot - 1)
                        act_(out(slot - 1), tiles2(G[j % 2]), ACT.Copy).then_inc(s_ev[j % 2], 1)

            def attention(name, heads, keys, base, beside_=lambda u: None):
                for u in range(2 * heads):
                    h, t = divmod(u, 2)
                    act.wait_ge(q(name + ".l"), nth(name + ".l", u + 1))
                    if u >= 2:
                        act.wait_ge(q(name + ".tp"), nth(name + ".tp", u - 1))
                    nk, col = keys(t), base + t * heads + h
                    act_(Pr[u % 2][:, 0:nk], Lm[u % 2][:, 0:nk], ACT.Exp, bias=nmax[:, col:col + 1], scale=-1.0,
                         accum_out=ssum[:, col:col + 1]).then_inc(q(name + ".p"), 1)
                    beside_(u)
                beside_(2 * heads)

            def hi_and_squares(name, ft, gain, squares=True):
                if gain:
                    act_(x_hi[:, ft, :], X[:, ft, :], ACT.Copy, scale=pc(*gain(ft))).then_inc(q(name + ".hi"), 1)
                if squares:
                    act_(T8[:, ft, :], X[:, ft, :], ACT.Square).then_inc(q(name + ".sq"), 1)

            def residual(name, s, gain, nf, per):
                for g in range(KC // nf):
                    if s.name != "pool":
                        splits_to(s.n0 + g * per + per - 1 + AHEAD)
                    taken(act, s.j0 + g)
                    for f in range(nf):
                        hi_and_squares(name, g * nf + f, gain)

            def ffn_in(s, before, width, chunks):
                def slot_(slot, i=0):
                    j = s.j0 + slot
                    if chunks == 2:
                        result(s, slot, i)
                        act_(sg[slot % 2][:, :], G[j % 2][:, :], ACT.Relu).then_inc(s_ev[j % 2], 1)
                    else:
                        taken(act, j, i)
                        act_(sg[slot % 2][:, 0:S], gu[slot % 2][:, 0, :], ACT.Silu).then_inc(q(s.name + ".sg"), 1)
                    act.wait_ge(q(s.name + ".h"), nth(s.name + ".h", slot + 1 + i * RING))
                    c0 = chunks * slot + i * (chunks * RING)
                    act_(hid_hi[:, bass.ds(c0, chunks), :], hb[slot % 2][:, 0:width].rearrange("p (k c) -> p k c", k=chunks),
                         ACT.Copy).then_inc(q(s.name + ".hi"), 1)

                for slot in range(4):
                    splits_to(s.n0 + slot + AHEAD)
                    if slot == 0 and before:
                        root(before, L[0][:, 0:S], eps2)
                    slot_(slot)
                turns = (s.slots - AHEAD) // RING - 1
                with act.Fori(0, turns) as i:
                    for slot in range(4, 8):
                        split(s, slot + AHEAD, i)
                        slot_(slot, i)
                at[0] += turns * RING
                for slot in range(4 + 4 * turns, s.slots):
                    splits_to(s.n0 + slot + AHEAD)
                    slot_(slot)

            act.wait_ge(q("mem_in"), 16)
            act_(T8[:], memN[:], ACT.Square).then_inc(q("mem.sq"), 1)
            act.wait_ge(q("cond_in"), 16)
            act_(cond[:], cond[:], ACT.Silu).then_inc(q("cact"), 1)
            act.wait_ge(q("consts"), 1)
            act.wait_ge(s_par, 32)
            root("mem", L[1][:, 0:S], eps2, ".var")
            for ft in range(KC):
                act.wait_ge(q("mem0.t"), ft + 1)
                act_(mh[:, ft, :], T8[:, ft, :], ACT.Copy).then_inc(q("mem0.hi"), 1)
            copies(st["xk0"], lambda k: kT[:, 2 * k:2 * k + 2, :])
            for ft in range(KC):
                act.wait_ge(q("h0.t"), ft + 1)
                act_(x_hi[:, ft, :], T8[:, ft, :], ACT.Copy).then_inc(q("h0.hi"), 1)
            copies(st["xv0"], lambda k: V0[:, :, k * 256:(k + 1) * 256])
            s = st["xbc"]

            def conv_silu(ft, count):
                act.wait_ge(q("ssm.cv"), count)
                act_(XB[:, ft, :], XB[:, ft, :], ACT.Silu).then_inc(q("ssm.conv"), 1)

            def exps():
                act.wait_ge(q("ssm.v"), 1)
                own(act_(tok["mag"][:], tok["v"][:], ACT.Abs))
                act_(tok["e"][:], tok["mag"][:], ACT.Exp, scale=-1.0).then_inc(q("ssm.exp"), 1)
                act_(negA[:], rows[:, 32:48], ACT.Exp).then_inc(q("ssm.exp"), 1)

            def z_silu(slot):
                z = st["z"]
                splits_to(min(z.n0 + slot + AHEAD, st["q"].n0 - 1))
                result(z, slot)
                if slot == 0:
                    act.wait_ge(s_spill, 32)
                act_(Zs[:, :, slot * 256:(slot + 1) * 256], tiles2(G[(z.j0 + slot) % 2]), ACT.Silu)\
                    .then_inc(s_ev[(z.j0 + slot) % 2], 1)

            splits_to(st["dtf"].n0 + AHEAD)
            exps()
            act.wait_ge(q("ssm.pad"), 1)
            for slot in range(s.slots):
                splits_to(s.n0 + slot + AHEAD)
                result(s, slot)
                f0 = 2 * xbc_slot(slot)
                act_(CX[:, f0:f0 + 2, 3:3 + S], tiles2(G[(s.j0 + slot) % 2]), ACT.Copy)\
                    .then_inc(s_ev[(s.j0 + slot) % 2], 1)
                if slot:
                    f0 = 2 * xbc_slot(slot - 1)
                    conv_silu(f0, 2 * slot - 1)
                    conv_silu(f0 + 1, 2 * slot)
            conv_silu(6, 11)
            conv_silu(7, 12)
            act.wait_ge(q("ssm.bt"), 1)
            act_(BT[:], L[0][:, 0:S].rearrange("p (g c) -> p g c", g=2), ACT.Copy).then_inc(q("ssm.bts"), 1)
            z_silu(0)
            for b in range(4):
                t, fh = divmod(b, 2)
                act.wait_ge(q("ssm.xtr"), b + 1)
                if b == 0:
                    act.wait_ge(s_spill, 16)
                act_(XsT[:, t, fh * 512:(fh + 1) * 512], T[b % 2][:, :], ACT.Copy).then_inc(q("ssm.xt"), 1)
                if b == 1:
                    z_silu(1)
            z_silu(2)
            z_silu(3)
            act.wait_ge(q("ssm.cs"), 1)
            act_(dend[:], L[1][:, 0:H], ACT.Exp).then_inc(q("ssm.ex"), 1)
            act_(dout[:], L[1][:, H:2 * H], ACT.Exp).then_inc(q("ssm.ex"), 1)
            for u in range(8):
                act.wait_ge(q("ssm.seg"), u + 1)
                if u >= 2:
                    act.wait_ge(q("ssm.ydiag"), u - 1)
                act_(E[u % 2][:], T[u % 2][:, :].rearrange("p (k c) -> p k c", k=4), ACT.Exp).then_inc(q("ssm.e"), 1)
                if u == 3:
                    for g in range(2):
                        act.wait_ge(q("ssm.state"), g + 1)
                        act_(STt[:, g, :], G[g][:, :], ACT.Copy).then_inc(q("ssm.st"), 1)
            splits_to(st["q"].n0 + 1)
            row_squares("ssmt", Y, xce[:])
            features_hi("ssmt", 0, "ssm_w")

            for name, out in (("q", qT), ("k", kT)):
                copies(st[name], lambda k: out[:, 2 * k:2 * k + 2, :], scale=0.125 if name == "q" else 1.0)
            copies(st["v"], lambda k: V[:, :, k * 256:(k + 1) * 256])
            act_(X[:], X[:], ACT.Copy, scale=ALPHA).then_inc(q("wout.ax"), 1)
            attention("fox", H, lambda t: P * (t + 1), 0, lambda u: beside(st["wouta"], u, None))
            row_squares("foxt", AO, T8[:, 0:4, :].rearrange("p a b -> p (a b)"))
            features_hi("foxt", 8, "attn_w")

            def layer_norm(name, s, lng, lnb, after, nf, per):
                if name != "wout":
                    act_(X[:], X[:], ACT.Copy, scale=ALPHA).then_inc(q(name + ".ax"), 1)
                for g in range(KC // nf):
                    splits_to(s.n0 + g * per + per - 1 + AHEAD)
                for ft in range(KC):
                    act.wait_ge(q(name + ".cent"), ft + 1)
                    act_(T8[:, ft, :], X[:, ft, :], ACT.Square).then_inc(q(name + ".sq8"), 1)
                root(name, L[1][:, 0:S], eps1, ".var")
                for ft in range(KC + 1):
                    if ft < KC:
                        act.wait_ge(q(name + ".xn"), ft + 1)
                        act_(X[:, ft, :], X[:, ft, :], ACT.Identity, bias=pc(lnb, ft), scale=pc(lng, ft))\
                            .then_inc(q(name + ".xf"), 1)
                    if ft:
                        after(ft - 1)

            def after1(ft):
                act.wait_ge(q("ln1.t"), ft + 1)
                act_(x_hi[:, ft, :], T8[:, ft, :], ACT.Copy).then_inc(q("ln1.hi"), 1)

            def after2(ft):
                act.wait_ge(q("ffout.xf"), ft + 1)
                hi_and_squares("ln2", ft, lambda k: ("ffn1", k))

            layer_norm("wout", st["woutb"], "ln1_g", "ln1_b", after1, 2, 1)
            ffn_in(st["ffin"], None, 512, 2)
            layer_norm("ffout", st["ffout"], "ln2_g", "ln2_b", after2, 1, 2)

            def xattn(l, before):
                name = f"xa{l}"
                for slot in range(4):
                    splits_to(st[f"xq{l}"].n0 + slot + AHEAD)
                    if slot == 0:
                        root(before, L[0][:, 0:S], eps2)
                attention(name, XH, lambda t: S, 0)
                features_hi(name + "t", 0)
                residual(f"xo{l}", st[f"xo{l}"], lambda ft: ("ffn2", 8 * l + ft), 2, 1)

            ffn_in(st["f1in0"], "ln2", 256, 1)
            residual("f1out0", st["f1out0"], None, 1, 2)
            root("f1out0", L[0][:, 0:S], eps2)
            splits_to(st["pool"].n0 + AHEAD)
            for g in range(4):
                act.wait_ge(q("pmix.p"), g + 1)
                src = (wa, wb)[g % 2]
                act_(x_hi[:, 2 * g:2 * g + 2, :], src[:, 2 * g:2 * g + 2, :], ACT.Copy).then_inc(q("pmix.hi"), 1)
            residual("pool", st["pool"], lambda ft: ("xattn", ft), 2, 0)
            xattn(0, "pool")
            ffn_in(st["f2in0"], "xo0", 256, 1)
            residual("f2out0", st["f2out0"], lambda ft: ("ffn1", 8 + ft), 1, 2)

            ffn_in(st["f1in1"], "f2out0", 256, 1)
            residual("f1out1", st["f1out1"], lambda ft: ("mix", 8 + ft), 1, 2)
            splits_to(st["nq"].n0 + AHEAD)
            root("f1out1", L[0][:, 0:S], eps2)
            root("f1out1", T[0][:, 0:2], eps2, count=2, out=RTs[:])
            for slot in range(1, 4):
                splits_to(st["nq"].n0 + slot + AHEAD)
            for b, name in enumerate(("nkc", "nvc")):
                splits_to(st[name].n0 + AHEAD)
                act.wait_ge(q("nsa.blk"), b + 1)
                act_(bk_hi[b][:], bk[:].rearrange("p j g n -> p j (g n)"), ACT.Copy).then_inc(q("nsa.bkh"), 1)
            splits_to(st["nks"].n0 + AHEAD)
            splits_to(st["nkw"].n0 + AHEAD)
            for name, out in (("nvs", vs), ("nvw", vw)):
                s = st[name]
                splits_to(s.n0 + AHEAD)
                result(s, 0)
                if name == "nvs":
                    act.wait_ge(q("nsa.rt"), 1)
                for t in range(2):
                    last = act_(out[:, t, :], G[s.j0 % 2][:, t * 256:(t + 1) * 256], ACT.Copy, scale=RT[:, t:t + 1])
                last.then_inc(s_ev[s.j0 % 2], 1)
            s = st["ng"]
            splits_to(s.n0 + AHEAD)
            result(s, 0)
            for t in range(2):
                last = act_(gates[:, t, :], G[s.j0 % 2][:, t * 48:(t + 1) * 48], ACT.Sigmoid, scale=RT[:, t:t + 1])
            last.then_inc(s_ev[s.j0 % 2], 1)
            for b, name in enumerate(("cmpk", "cmpv")):
                s = st[name]
                for slot in range(2):
                    splits_to(s.n0 + slot + AHEAD)
                result(s, 1)
                act_(GH[b][0:GB, :], G[s.j0 % 2][0:GB, 0:256], ACT.Gelu_apprx_tanh).then_inc(s_ev[s.j0 % 2], 1)
            act.wait_ge(q("nsa.ht"), 1)
            act_(HG[:], T[0][:, 0:2 * GB].rearrange("p (k n) -> p k n", k=2), ACT.Copy).then_inc(q("nsa.hx"), 1)
            act.wait_ge(q("nsa.ht"), 2)
            for k in range(2):
                last = act_(HX[:, k, :].rearrange("p (g h n) -> p g h n", g=G_KV, h=2),
                            bc(T[1][:, k * GB:(k + 1) * GB].rearrange("p (g n) -> p g n", g=G_KV).unsqueeze(2),
                               [P, G_KV, 2, NCMP]), ACT.Copy)
            last.then_inc(q("nsa.hx"), 1)
            act.wait_ge(q("nsa.kc"), 1)
            act_(KC_T[:], T[0][:, 0:60].rearrange("p (g n) -> p g n", g=G_KV), ACT.Copy).then_inc(q("nsa.ready"), 1)
            for t in range(2):
                act.wait_ge(q("nc.l"), t + 1)
                act_(LC[:, t, :], LC[:, t, :], ACT.Exp).then_inc(q("nc.p"), 1)
            for t in range(2):
                for half in range(2):
                    act.wait_ge(q("nc.pv"), 2 * t + half + 1)
                    act_(AO[:, t, :].rearrange("p (h two d) -> p two h d", two=2, d=HD)[:, half], h8((O, G)[t][half][:, :]),
                         ACT.Copy).then_inc(q("nc.o"), 1)
            attention("ns", H, lambda t: P * (t + 1), 32,
                      lambda u: beside(st["xk1"], u, lambda k: Xk[:, 2 * k:2 * k + 2, :]))
            attention("nw", H, lambda t: P * (t + 1), 64,
                      lambda u: beside(st["xv1"], u, lambda k: Xv[:, :, k * 256:(k + 1) * 256]))
            features_hi("nsat", 0)
            residual("no", st["no"], lambda ft: ("xattn", 8 + ft), 2, 1)
            xattn(1, "no")
            ffn_in(st["f2in1"], "xo1", 256, 1)
            residual("f2out1", st["f2out1"], None, 1, 2)
            root("f2out1", L[0][:, 0:S], eps2)

        @block.vector
        def _(dve):
            v = nc.vector
            own = Chain(dve, "dve_own")
            at, mods = [0], [0]

            def modulation_half(k, f):
                w_, load = mod_buffer(k)
                if f == 0:
                    dve.wait_ge(q(f"ada_load{load[0]}"), load[1])
                part = w_[:, f * D:(f + 1) * D]
                last = v.tensor_tensor_reduce(out=part, in0=part, in1=cond[:], scale=1.0, scalar=0.0, op0=ALU.mult,
                                              op1=ALU.add, accum_out=mod[:, 2 * k + f:2 * k + f + 1])
                if f == 1:
                    last.then_inc(q("ada"), 1)

            def modulation():
                for f in range(2):
                    modulation_half(mods[0], f)
                mods[0] += 1

            def gated_update(s, g, nf, per, gate0):
                j = s.j0 + g
                result(s, g * per + per - 1)
                for ft in range(g * nf, g * nf + nf):
                    f = ft - g * nf
                    last = v.scalar_tensor_tensor(X[:, ft, :], G[j % 2][:, f * S:(f + 1) * S],
                                                  mod1[:, gate0 + ft:gate0 + ft + 1], X[:, ft, :], ALU.mult, ALU.add)
                last.then_inc(s_ev[j % 2], 1)

            def modulations_to(count):
                while mods[0] < count:
                    modulation()

            def biased(a_, b_):
                dve.wait_ge(q("ada"), b_ // 2)
                own(v.tensor_tensor(mod[:, a_:b_], mod[:, a_:b_], par[:, COL["b_ada"] + a_:COL["b_ada"] + b_], ALU.add))
                own(v.tensor_scalar(mod1[:, a_:b_], mod[:, a_:b_], 1.0, None, ALU.add))

            def split(s, slot, i=0):
                b = (s.n0 + slot) % RING
                dve.wait_ge(s_hi, s.n0 + slot + 1 + i * RING)
                v.tensor_tensor(w_lo[b][:, 0:s.size], raw[b][:, 0:s.size], w_hi[b][:, 0:s.size].bitcast(F32),
                                ALU.subtract).then_inc(s_lo, 1)

            def splits_to(k):
                while at[0] <= min(k, len(split_order) - 1):
                    split(*split_order[at[0]])
                    at[0] += 1

            def result(s, slot, i=0):
                dve.wait_ge(s_mm, s.n0 + slot + 1 + i * RING)

            def splits_over(s):
                for slot in range(s.slots):
                    splits_to(s.n0 + slot + AHEAD)

            def inverse(name):
                dve.wait_ge(q(name + ".root"), nth(name + ".root", 1))
                own(v.reciprocal(R[:], Rs[:]))

            def row_scale(name, src):
                dve.wait_ge(q(name + ".root"), nth(name + ".root", 1))
                own(v.reciprocal(rtok[:], rtoks[:]))
                for t in range(2):
                    last = v.tensor_scalar(src[:, t, :], src[:, t, :], rtok[:, t:t + 1], None, ALU.mult)
                last.then_inc(q(name + ".y"), 1)

            def features_lo(name, chunk0, gain=None):
                for b in range(4):
                    dve.wait_ge(q(name + ".hi"), nth(name + ".hi", 2 * b + 2))
                    for f in range(2):
                        ft = 2 * b + f
                        v.scalar_tensor_tensor(hid_lo[:, chunk0 + ft, :], T[b % 2][:, f * S:(f + 1) * S],
                                               pc(gain, ft) if gain else 1.0, hid_hi[:, chunk0 + ft, :].bitcast(F32),
                                               ALU.mult, ALU.subtract).then_inc(q(name + ".lo"), 1)
                    dve.wait_ge(q(name + ".lo"), nth(name + ".lo", 2 * b + 2))
                    dve.nop().then_inc(q(name + ".tev"), 1)

            def beside(s, step):
                slot, part = divmod(step, SHARE)
                if slot < s.slots and part >= 4:
                    t, k = split_order[s.n0 + slot + AHEAD]
                    n, each = t.n0 + k, t.size // 4
                    c = slice((part - 4) * each, (part - 3) * each)
                    if part == 4:
                        dve.wait_ge(s_hi, n + 1)
                    last = v.tensor_tensor(w_lo[n % RING][:, c], raw[n % RING][:, c], w_hi[n % RING][:, c].bitcast(F32),
                                           ALU.subtract)
                    if part == 7:
                        last.then_inc(s_lo, 1)
                        at[0] += 1

            def attention(name, heads, hd, keys, masks, base, take, beside_=lambda step: None):
                units = [(h, t) for h in range(heads) for t in range(2)]
                per = 512 // hd
                for step in range(len(units) + 2):
                    if step < len(units):
                        h, t = units[step]
                        nk, col = keys(t), base + t * heads + h
                        dve.wait_ge(q(name + ".qk"), nth(name + ".qk", step + 1))
                        if step >= 2:
                            dve.wait_ge(q(name + ".p"), nth(name + ".p", step - 1))
                        v.tensor_tensor_reduce(out=Lm[step % 2][:, 0:nk], in0=L[step % 2][:, 0:nk], in1=masks(t),
                                               scale=-1.0, scalar=3e38, op0=ALU.add, op1=ALU.min,
                                               accum_out=nmax[:, col:col + 1]).then_inc(q(name + ".l"), 1)
                    if 1 <= step <= len(units):
                        u = step - 1
                        h, t = units[u]
                        nk = keys(t)
                        rows_, nch = min(nk, P), (nk + P - 1) // P
                        dve.wait_ge(q(name + ".tp"), nth(name + ".tp", u + 1))
                        if u >= 2:
                            dve.wait_ge(q(name + ".pv"), nth(name + ".pv", u - 1))
                        v.tensor_copy(PT[u % 2][0:rows_, 0:nch, :],
                                      T[u % 2][0:rows_, 0:nch * P].rearrange("p (c n) -> p c n", c=nch))\
                            .then_inc(q(name + ".pt"), 1)
                    beside_(step)
                    if step >= 3 and (step - 1) % (2 * per) == 0:
                        half = (step - 1) // (2 * per) - 1
                        for t in range(2):
                            dve.wait_ge(q(name + ".pv"), nth(name + ".pv", 2 * per * (half + 1) - 1 + t))
                            cols = slice(base + t * heads + half * per, base + t * heads + (half + 1) * per)
                            own(v.reciprocal(rs[:, 0:per], ssum[:, cols]))
                            take(half, t)
                            dve.wait_ge(q(name + ".o"), nth(name + ".o", 2 * half + t + 1))

            def out_view(half, t):
                return AO[:, t, half * 512:(half + 1) * 512]

            def plain_take(name, per):
                def take(half, t):
                    v.tensor_tensor(out_view(half, t).rearrange("p (h d) -> p h d", h=per),
                                    O[t][:, :].rearrange("p (h d) -> p h d", h=per),
                                    bc(rs[:, 0:per].unsqueeze(2), [P, per, 512 // per]), ALU.mult)\
                        .then_inc(q(name + ".o"), 1)
                return take

            def residual(name, s, nf, per, factor, gain):
                def lo(ft):
                    dve.wait_ge(q(name + ".hi"), nth(name + ".hi", ft + 1))
                    v.scalar_tensor_tensor(x_lo[:, ft, :], X[:, ft, :], pc(*gain(ft)), x_hi[:, ft, :].bitcast(F32),
                                           ALU.mult, ALU.subtract).then_inc(q(name + ".lo"), 1)

                for g in range(KC // nf):
                    j = s.j0 + g
                    if s.name == "pool":
                        if g < 3:
                            dve.wait_ge(q("pmix.mm"), g + 1)
                        else:
                            result(s, 0)
                    else:
                        splits_to(s.n0 + g * per + per - 1 + AHEAD)
                        result(s, g * per + per - 1)
                    for f in range(nf):
                        ft = g * nf + f
                        last = v.scalar_tensor_tensor(X[:, ft, :], G[j % 2][:, f * S:(f + 1) * S],
                                                      factor if isinstance(factor, float) else factor(ft),
                                                      X[:, ft, :], ALU.mult, ALU.add)
                    last.then_inc(s_ev[j % 2], 1)
                    if gain and g:
                        for f in range(nf):
                            lo((g - 1) * nf + f)
                if gain:
                    for f in range(nf):
                        lo(KC - nf + f)

            def ffn_in(s, before, width, chunks):
                def lo(slot, i=0):
                    dve.wait_ge(q(s.name + ".hi"), nth(s.name + ".hi", slot + 1 + i * RING))
                    c0 = chunks * slot + i * (chunks * RING)
                    v.tensor_tensor(hid_lo[:, bass.ds(c0, chunks), :],
                                    hb[slot % 2][:, 0:width].rearrange("p (k c) -> p k c", k=chunks),
                                    hid_hi[:, bass.ds(c0, chunks), :].bitcast(F32), ALU.subtract)\
                        .then_inc(q(s.name + ".lo"), 1)

                def slot_(slot, split_ahead, i=0):
                    j = s.j0 + slot
                    if chunks == 1:
                        result(s, slot, i)
                        v.tensor_tensor(gu[slot % 2][:], tiles2(G[j % 2]), bc(R[:].unsqueeze(1), [P, 2, S]), ALU.mult)\
                            .then_inc(s_ev[j % 2], 1)
                        split_ahead()
                    if slot:
                        lo(slot - 1, i)
                    if chunks == 1:
                        dve.wait_ge(q(s.name + ".sg"), nth(s.name + ".sg", slot + 1 + i * RING))
                        taken(dve, j, i)
                        other = gu[slot % 2][:, 1, :]
                    else:
                        taken(dve, j, i)
                        other = sg[slot % 2][:, 0:width]
                    v.tensor_tensor(hb[slot % 2][:, 0:width], sg[slot % 2][:, 0:width], other, ALU.mult)\
                        .then_inc(q(s.name + ".h"), 1)
                    if chunks == 2:
                        split_ahead()

                for slot in range(4):
                    if slot == 0 and before:
                        inverse(before)
                    slot_(slot, lambda: splits_to(s.n0 + slot + AHEAD))
                turns = (s.slots - AHEAD) // RING - 1
                with dve.Fori(0, turns) as i:
                    for slot in range(4, 8):
                        slot_(slot, lambda: split(s, slot + AHEAD, i), i)
                at[0] += turns * RING
                for slot in range(4 + 4 * turns, s.slots):
                    slot_(slot, lambda: splits_to(s.n0 + slot + AHEAD))
                lo(s.slots - 1)

            dve.wait_ge(q("cact"), 1)
            modulations_to(1)
            dve.wait_ge(s_par, 32)
            dve.wait_ge(q("mem.root"), 1)
            own(v.reciprocal(R[:], Rs[:]))
            for ft in range(KC + 1):
                if ft < KC:
                    v.scalar_tensor_tensor(T8[:, ft, :], memN[:, ft, :], pc("mem", ft), R[:], ALU.mult, ALU.mult)\
                        .then_inc(q("mem0.t"), 1)
                if ft:
                    dve.wait_ge(q("mem0.hi"), ft)
                    v.tensor_tensor(ml[:, ft - 1, :], T8[:, ft - 1, :], mh[:, ft - 1, :].bitcast(F32),
                                    ALU.subtract).then_inc(q("mem0.lo"), 1)
            splits_to(1)
            dve.wait_ge(q("mem0.t"), KC)
            own(v.tensor_tensor(memN[:], memN[:], bc(R[:].unsqueeze(1), [P, KC, S]), ALU.mult))
            for slot in range(4):
                modulations_to(2 * slot + 2)
                splits_to(slot + AHEAD)
            biased(0, 16)
            dve.wait_ge(s_in, 16)
            for ft in range(KC + 1):
                if ft < KC:
                    v.tensor_scalar(T8[:, ft, :], X[:, ft, :], mod1[:, 8 + ft:9 + ft], mod[:, ft:ft + 1],
                                    ALU.mult, ALU.add).then_inc(q("h0.t"), 1)
                if ft:
                    dve.wait_ge(q("h0.hi"), ft)
                    v.tensor_tensor(x_lo[:, ft - 1, :], T8[:, ft - 1, :], x_hi[:, ft - 1, :].bitcast(F32),
                                    ALU.subtract).then_inc(q("h0.lo"), 1)
            splits_over(st["xv0"])

            s = st["dtf"]
            splits_to(s.n0 + AHEAD)
            result(s, 0)
            t32 = lambda c0: bc(rows[:, c0:c0 + 32].unsqueeze(1), [P, 2, 32])
            v.tensor_tensor(tok["v"][:], G[s.j0 % 2][:, 0:64].rearrange("p (t c) -> p t c", t=2), t32(0), ALU.add)\
                .then_inc(s_ev[s.j0 % 2], 1)
            taken(dve, s.j0)
            v.tensor_scalar(tok["v"][:, :, 16:32], tok["v"][:, :, 16:32], -1.0, None, ALU.mult).then_inc(q("ssm.v"), 1)
            dve.wait_ge(q("ssm.exp"), 2)
            own(v.tensor_scalar(tok["den"][:], tok["e"][:], 2.0, None, ALU.add))
            own(v.reciprocal(tok["y"][:], tok["den"][:]))
            own(v.tensor_tensor(tok["y"][:], tok["y"][:], tok["e"][:], ALU.mult))
            own(v.tensor_tensor(tok["y2"][:], tok["y"][:], tok["y"][:], ALU.mult))
            own(v.tensor_scalar(tok["poly"][:], tok["y2"][:], 2.0 / 17, 2.0 / 15, ALU.mult, ALU.add))
            for k in (13, 11, 9, 7, 5, 3, 1):
                own(v.tensor_tensor(tok["poly"][:], tok["poly"][:], tok["y2"][:], ALU.mult))
                own(v.tensor_scalar(tok["poly"][:], tok["poly"][:], 2.0 / k, None, ALU.add))
            own(v.tensor_tensor(tok["poly"][:], tok["poly"][:], tok["y"][:], ALU.mult))
            own(v.scalar_tensor_tensor(tok["sp"][:], tok["v"][:], 0.0, tok["poly"][:], ALU.max, ALU.add))
            own(v.tensor_copy(dt_t[:], tok["sp"][:, :, 0:16]))
            own(v.tensor_scalar(lf[:], tok["sp"][:, :, 16:32], -1.0, None, ALU.mult))
            own(v.tensor_scalar(negA[:], negA[:], -1.0, None, ALU.mult))
            v.tensor_tensor(a_t[:], dt_t[:], bc(negA[:].unsqueeze(1), [P, 2, H]), ALU.mult).then_inc(q("ssm.a"), 1)

            s = st["xbc"]
            for slot in range(s.slots):
                splits_to(s.n0 + slot + AHEAD)
                taken(dve, s.j0 + slot)
                for ft in (2 * xbc_slot(slot), 2 * xbc_slot(slot) + 1):
                    own(v.tensor_scalar(XB[:, ft, :], CX[:, ft, 3:3 + S], pc("conv_w", 36 + ft), pc("conv_b", ft),
                                        ALU.mult, ALU.add))
                    for k in (2, 1, 0):
                        last = v.scalar_tensor_tensor(XB[:, ft, :], CX[:, ft, k:k + S], pc("conv_w", 12 * k + ft),
                                                      XB[:, ft, :], ALU.mult, ALU.add)
                        if k:
                            own(last)
                    last.then_inc(q("ssm.cv"), 1)

            heads8 = lambda ap: bc(ap.unsqueeze(2), [P, 8, HD])
            dve.wait_ge(q("ssm.cb"), 1)
            v.tensor_tensor(CB[:], O[0][:, :].rearrange("p (k c) -> p k c", k=4), bc(U[:].unsqueeze(1), [P, 4, P]),
                            ALU.mult).then_inc(q("ssm.cbm"), 1)
            for b in range(4):
                t, fh = divmod(b, 2)
                splits_to(min(st["z"].n0 + b + AHEAD - 1, st["q"].n0 - 1))
                dve.wait_ge(q("ssm.xt"), b + 1)
                own(v.tensor_tensor(h8(xc[:, t, fh * 512:(fh + 1) * 512]), h8(XsT[:, t, fh * 512:(fh + 1) * 512]),
                                    heads8(dt_t[:, t, 8 * fh:8 * fh + 8]), ALU.mult))
            dve.wait_ge(q("ssm.ex"), 2)
            v.tensor_tensor(xce[:].rearrange("p (h d) -> p h d", h=H), xc[:, 0, :].rearrange("p (h d) -> p h d", h=H),
                            bc(dend[:].unsqueeze(2), [P, H, HD]), ALU.mult).then_inc(q("ssm.xce"), 1)
            dve.wait_ge(q("ssm.cbm"), 1)
            for u in range(9):
                if u < 8:
                    dve.wait_ge(q("ssm.e"), u + 1)
                    v.tensor_tensor(E[u % 2][:], E[u % 2][:], bc(CB[:, u // 2, :].unsqueeze(1), [P, 4, P]), ALU.mult)\
                        .then_inc(q("ssm.sc"), 1)
                if u and u % 2 == 0:
                    c, g = divmod(u // 2 - 1, 2)
                    cols = slice(g * 512, (g + 1) * 512)
                    dve.wait_ge(q("ssm.ydiag"), u)
                    if u == 2:
                        dve.wait_ge(q("ssm.dx"), 1)
                    v.tensor_tensor(Y[:, c, cols], O[g][:, :], Y[:, c, cols], ALU.add).then_inc(q("ssm.yo"), 1)
                    if c == 1:
                        dve.wait_ge(q("ssm.off"), g + 1)
                        tmp = T8[:, 0:2, :].rearrange("p a b -> p (a b)")
                        own(v.tensor_tensor(h8(tmp), h8(L[g][:, :]), heads8(dout[:, 8 * g:8 * g + 8]), ALU.mult))
                        dve.wait_ge(q("ssm.yo"), u // 2)
                        own(v.tensor_tensor(Y[:, c, cols], Y[:, c, cols], tmp, ALU.add))
            dve.wait_ge(q("ssm.yo"), 4)
            v.tensor_tensor(Y[:], Y[:], Zs[:], ALU.mult).then_inc(q("ssmt.in"), 1)
            splits_to(st["q"].n0 + 1)
            row_scale("ssmt", Y)
            features_lo("ssmt", 0, "ssm_w")

            for name in "qkv":
                for slot in range(4):
                    splits_to(st[name].n0 + slot + AHEAD)
                    modulations_to(mods[0] + 1)
            causal = lambda t: mask[:, P:2 * P] if t == 0 else mask[:, :]
            biased(16, 24)
            dve.wait_ge(q("wout.ax"), 1)

            def beside_fox(step):
                slot, part = divmod(step, SHARE)
                if part == 0 and slot in range(1, 5):
                    gated_update(st["wouta"], slot - 1, 2, 1, 16)
                if part in (1, 3) and slot < 4:
                    modulation_half(20 + slot, part // 2)
                beside(st["wouta"], step)

            attention("fox", H, HD, lambda t: P * (t + 1), causal, 0, plain_take("fox", 8), beside_fox)
            mods[0] = MOD_SLOTS
            dve.wait_ge(q("fox.o"), nth("fox.o", 4))
            dve.nop().then_inc(q("foxt.in"), 1)
            row_scale("foxt", AO)
            features_lo("foxt", 8, "attn_w")

            def layer_norm(name, s, gate0, nf, per):
                if name != "wout":
                    dve.wait_ge(q(name + ".ax"), 1)
                for g in range(KC // nf):
                    splits_to(s.n0 + g * per + per - 1 + AHEAD)
                    gated_update(s, g, nf, per, gate0)
                dve.wait_ge(q(name + ".mean"), nth(name + ".mean", 1))
                for ft in range(KC):
                    v.tensor_tensor(X[:, ft, :], X[:, ft, :], L[0][:, 0:S], ALU.subtract).then_inc(q(name + ".cent"), 1)
                dve.wait_ge(q(name + ".cent"), KC)
                inverse(name)

            def normalised(name, ft):
                v.tensor_tensor(X[:, ft, :], X[:, ft, :], R[:], ALU.mult).then_inc(q(name + ".xn"), 1)

            biased(24, 40)
            layer_norm("wout", st["woutb"], 16, 2, 1)
            for step in range(KC + 2):
                if step < KC:
                    normalised("wout", step)
                if 1 <= step <= KC:
                    ft = step - 1
                    dve.wait_ge(q("wout.xf"), ft + 1)
                    v.tensor_scalar(T8[:, ft, :], X[:, ft, :], mod1[:, 32 + ft:33 + ft], mod[:, 24 + ft:25 + ft],
                                    ALU.mult, ALU.add).then_inc(q("ln1.t"), 1)
                if step >= 2:
                    dve.wait_ge(q("ln1.hi"), nth("ln1.hi", step - 1))
                    v.tensor_tensor(x_lo[:, step - 2, :], T8[:, step - 2, :], x_hi[:, step - 2, :].bitcast(F32),
                                    ALU.subtract).then_inc(q("ln1.lo"), 1)
            ffn_in(st["ffin"], None, 512, 2)
            biased(40, 48)
            layer_norm("ffout", st["ffout"], 40, 1, 2)
            for step in range(KC + 1):
                if step < KC:
                    normalised("ffout", step)
                if step:
                    ft = step - 1
                    dve.wait_ge(q("ln2.hi"), nth("ln2.hi", ft + 1))
                    v.scalar_tensor_tensor(x_lo[:, ft, :], X[:, ft, :], pc("ffn1", ft), x_hi[:, ft, :].bitcast(F32),
                                           ALU.mult, ALU.subtract).then_inc(q("ln2.lo"), 1)

            def scaled_queries(s, scale, before):
                for slot in range(4):
                    j = s.j0 + slot
                    splits_to(s.n0 + slot + AHEAD)
                    if slot == 0:
                        inverse(before)
                    result(s, slot)
                    v.scalar_tensor_tensor(qT[:, 2 * slot:2 * slot + 2, :], tiles2(G[j % 2]), scale,
                                           bc(R[:].unsqueeze(1), [P, 2, S]), ALU.mult, ALU.mult).then_inc(s_ev[j % 2], 1)

            def xattn(l, before):
                name = f"xa{l}"
                scaled_queries(st[f"xq{l}"], 0.0625, before)
                attention(name, XH, 256, lambda t: S, lambda t: bc(zero[:], [P, S]), 0, plain_take(name, 2))
                dve.wait_ge(q(name + ".o"), nth(name + ".o", 4))
                dve.nop().then_inc(q(name + "t.y"), 1)
                features_lo(name + "t", 0)
                residual(f"xo{l}", st[f"xo{l}"], 2, 1, 1.0, lambda ft: ("ffn2", 8 * l + ft))

            ffn_in(st["f1in0"], "ln2", 256, 1)
            residual("f1out0", st["f1out0"], 1, 2, 0.5, None)
            inverse("f1out0")
            splits_to(st["pool"].n0 + AHEAD)
            for ft in range(KC):
                last = v.scalar_tensor_tensor(T8[:, ft, :], X[:, ft, :], pc("mix", ft), R[:], ALU.mult, ALU.mult)
            own(last)
            own(v.reciprocal(icnt[:], icnt[:]))
            src = T8
            for g, dst in enumerate((wa, wb, wa, wb)):
                w_, c0 = 1 << g, 2 * g
                own(v.tensor_copy(dst[:, c0:KC, 0:w_], src[:, c0:KC, 0:w_]))
                own(v.tensor_tensor(dst[:, c0:KC, w_:S], src[:, c0:KC, w_:S], src[:, c0:KC, 0:S - w_], ALU.add))
                src = dst
            for g, dst in enumerate((wa, wb, wa, wb)):
                c = slice(2 * g, 2 * g + 2)
                own(v.tensor_tensor(dst[:, c, 0:16], dst[:, c, 0:16], bc(icnt[:, g, :].unsqueeze(1), [P, 2, 16]), ALU.mult))
                own(v.tensor_tensor(dst[:, c, 0:16], dst[:, c, 0:16], T8[:, c, 0:16], ALU.subtract))
                v.scalar_tensor_tensor(dst[:, c, 16:S], dst[:, c, 16:S], 1.0 / (2 << g), T8[:, c, 16:S],
                                       ALU.mult, ALU.subtract).then_inc(q("pmix.p"), 1)
                dve.wait_ge(q("pmix.hi"), g + 1)
                v.tensor_tensor(x_lo[:, c, :], dst[:, c, :], x_hi[:, c, :].bitcast(F32), ALU.subtract)\
                    .then_inc(q("pmix.lo"), 1)
            own(v.tensor_tensor(pool_bs[:], par[:, COL["pool_b"]:COL["pool_b"] + 8],
                                par[:, COL["pool_s"]:COL["pool_s"] + 8], ALU.mult))
            for ft in range(KC):
                last = v.tensor_scalar(X[:, ft, :], X[:, ft, :], pool_bs[:, ft:ft + 1], None, ALU.add)
            own(last)
            residual("pool", st["pool"], 2, 0, lambda ft: pc("pool_s", ft), lambda ft: ("xattn", ft))
            xattn(0, "pool")
            ffn_in(st["f2in0"], "xo0", 256, 1)
            residual("f2out0", st["f2out0"], 1, 2, 0.5, lambda ft: ("ffn1", 8 + ft))

            ffn_in(st["f1in1"], "f2out0", 256, 1)
            residual("f1out1", st["f1out1"], 1, 2, 0.5, lambda ft: ("mix", 8 + ft))
            scaled_queries(st["nq"], 0.125, "f1out1")
            dve.wait_ge(q("f1out1.root"), nth("f1out1.root", 2))
            v.reciprocal(RT[:], RTs[:]).then_inc(q("nsa.rt"), 1)

            def both_halves(s, dst, shift):
                result(s, 0)
                src = tiles2(G[s.j0 % 2])
                for half in range(2):
                    for to in range(2):
                        d_ = shift * to
                        a_, b_ = slice(half * 64, half * 64 + 64), slice(to * 64, to * 64 + 64)
                        last = v.tensor_tensor(dst[b_, half:G_KV:2, 0:S - d_], src[a_, :, d_:S],
                                               bc(R[a_, d_:S].unsqueeze(1), [64, 2, S - d_]), ALU.mult)
                last.then_inc(s_ev[s.j0 % 2], 1)

            for b, name in enumerate(("nkc", "nvc")):
                s = st[name]
                splits_to(s.n0 + AHEAD)
                both_halves(s, Z, 1)
                taken(dve, s.j0)
                Zr = Z[:, :, :].rearrange("p g (n s) -> p s g n", s=16)
                pos = COL["pos_k" if b == 0 else "pos_v"]
                for hj in range(2):
                    last = v.tensor_tensor(bk[:, 8 * hj:8 * hj + 8], Zr[:, 0:16:2, :, hj:hj + NCMP],
                                           bc(par[:, pos + 8 * hj:pos + 8 * hj + 8].unsqueeze(2).unsqueeze(3),
                                              [P, 8, G_KV, NCMP]), ALU.add)
                last.then_inc(q("nsa.blk"), 1)
                dve.wait_ge(q("nsa.bkh"), b + 1)
                v.tensor_tensor(bk_lo[b][:], bk[:].rearrange("p j g n -> p j (g n)"), bk_hi[b][:].bitcast(F32),
                                ALU.subtract).then_inc(q("nsa.bk"), 1)
            for name, dst in (("nks", ksd), ("nkw", kwd)):
                splits_to(st[name].n0 + AHEAD)
                both_halves(st[name], dst, 0)
            for name in ("nvs", "nvw", "ng", "cmpk", "cmpv"):
                splits_over(st[name])

            def gated_take(name, branch):
                def take(half, t):
                    g_ = gates[:, t, 24 * half + branch:24 * half + 24:3]
                    own(v.tensor_tensor(rs[:], rs[:], g_, ALU.mult))
                    o3 = h8(O[t][:, :])
                    v.tensor_tensor(h8(Ot[:]), o3, heads8(rs[:]), ALU.mult).then_inc(q(name + ".o"), 1)
                    dve.wait_ge(q(name + ".o"), nth(name + ".o", 2 * half + t + 1))
                    own(v.tensor_tensor(out_view(half, t), out_view(half, t), Ot[:], ALU.add))
                return take

            dve.wait_ge(q("nsa.kc"), 2)
            v.tensor_tensor(h8(VB[0:HB, :]), bc(T[1][0:HB, 0:HD].unsqueeze(1), [HB, 8, HD]),
                            bc(own_rows[0:HB, :].unsqueeze(2), [HB, 8, HD]), ALU.mult)\
                .then_inc(q("nsa.vc"), 1)
            heads = lambda ap: ap.rearrange("p (h n) -> p h n", h=H)
            each = lambda ap: bc(ap.unsqueeze(2), [P, H, NCMP])
            for t in range(2):
                dve.wait_ge(q("nc.qk"), H * (t + 1))
                for odd in range(2):
                    own(v.tensor_tensor(heads(LC[:, t, :])[:, 8 * odd:8 * odd + 8],
                                        (L, G)[t][odd][:, 0:HB].rearrange("p (h n) -> p h n", h=8),
                                        bc(cmask[:, t, :].unsqueeze(1), [P, 8, NCMP]), ALU.add))
                own(v.tensor_reduce(out=wc[:, t, :], in_=heads(LC[:, t, :]), op=ALU.max, axis=AX.X))
                v.tensor_tensor(heads(LC[:, t, :]), heads(LC[:, t, :]), each(wc[:, t, :]), ALU.subtract)\
                    .then_inc(q("nc.l"), 1)
            for t in range(2):
                dve.wait_ge(q("nc.p"), t + 1)
                own(v.tensor_reduce(out=wc[:, t, :], in_=heads(LC[:, t, :]), op=ALU.add, axis=AX.X))
                own(v.reciprocal(wc[:, t, :], wc[:, t, :]))
                own(v.tensor_tensor(wc[:, t, :].rearrange("p (two h) -> p two h", two=2),
                                    wc[:, t, :].rearrange("p (two h) -> p two h", two=2),
                                    gates[:, t, :].rearrange("p (h two b) -> p b two h", two=2, b=3)[:, 0], ALU.mult))
                if t == 0:
                    own(v.tensor_scalar(wc[:, t, :], wc[:, t, :], vis[:], None, ALU.mult))
                v.tensor_tensor(heads(LC[:, t, :]), heads(LC[:, t, :]), each(wc[:, t, :]), ALU.mult).then_inc(q("nc.w"), 1)
            for t in range(2):
                dve.wait_ge(q("nc.tp"), t + 1)
                v.tensor_copy(PT[t][0:HB, :, :], T[t][0:HB, 0:2 * P].rearrange("p (c n) -> p c n", c=2)).then_inc(q("nc.pt"), 1)
            dve.wait_ge(q("nc.o"), 4)
            attention("ns", H, HD, lambda t: P * (t + 1), causal, 32, gated_take("ns", 1),
                      lambda step: beside(st["xk1"], step))
            attention("nw", H, HD, lambda t: P * (t + 1), causal, 64, gated_take("nw", 2),
                      lambda step: beside(st["xv1"], step))
            dve.nop().then_inc(q("nsat.y"), 1)
            features_lo("nsat", 0)
            residual("no", st["no"], 2, 1, 1.0, lambda ft: ("xattn", 8 + ft))
            xattn(1, "no")
            ffn_in(st["f2in1"], "xo1", 256, 1)
            residual("f2out1", st["f2out1"], 1, 2, 0.5, None)
            inverse("f2out1")
            for ft in range(KC):
                v.scalar_tensor_tensor(T8[:, ft, :], X[:, ft, :], pc("final", ft), R[:], ALU.mult, ALU.mult)\
                    .then_inc(q("final"), 1)

        @block.gpsimd
        def _(pool):
            g_ = nc.gpsimd
            own = Chain(pool, "pool_own")

            def select(out, pattern, cm, op, fill, base=0):
                own(g_.affine_select(out=out, in_=out, compare_op=op, fill=fill, base=base, pattern=pattern,
                                     channel_multiplier=cm))

            def load_modulation(k):
                w_, load = mod_buffer(k)
                if MOD_FIRST > k >= 4:
                    pool.wait_ge(q("ada"), k - 3)
                if k >= MOD_FIRST + 3:
                    pool.wait_ge(q("ada"), k - 2)
                g_.dma_start(w_[:], w["ada"][k]).then_inc(q(f"ada_load{load[0]}"), 16)

            for k in range(4):
                load_modulation(k)
            for t_, x_ in ((ones_d, 1.0 / D), (ones, 1.0), (zero, 0.0), (eps1, EPS1), (eps2, EPS2), (ident, 0.0),
                           (U, 1.0), (SG, 1.0), (mask, 0.0), (vis, 1.0), (own_rows, 1.0), (cmask, 0.0)):
                last = g_.memset(t_[:], x_)
            own(last)
            select(ident[:], [[-1, P]], 1, ALU.not_equal, 1.0)
            select(U[:], [[1, P]], -1, ALU.is_ge, 0.0)
            select(SG[:, P:2 * P], [[-1, P]], 1, ALU.is_gt, 0.0)
            select(mask[:, P:2 * P], [[-1, P]], 1, ALU.is_ge, NEG)
            select(vis[:], [[0, 1]], 1, ALU.is_ge, 0.0, base=-31)
            for t in range(2):
                select(cmask[:, t, :], [[-16, NCMP]], 1, ALU.is_ge, NEG, base=P * t - 31)
            select(own_rows[:], [[-NCMP, 8]], 1, ALU.is_ge, 0.0)
            select(own_rows[:], [[NCMP, 8]], -1, ALU.is_ge, 0.0, base=NCMP - 1)
            own(g_.iota(icnt[:, 3, :], [[1, 16]], base=1, channel_multiplier=0, allow_small_or_imprecise_dtypes=True))
            for g in range(4):
                last = g_.tensor_scalar(icnt[:, g, :], icnt[:, 3, :], float(2 << g), None, ALU.min)
            own(last)
            g_.nop().then_inc(q("consts"), 1)
            for k in range(4, MOD_FIRST):
                load_modulation(k)
            pool.wait_ge(q("ada"), MOD_FIRST)
            own(g_.memset(CX[:, :, 0:3], 0.0))
            g_.nop().then_inc(q("ssm.pad"), 1)

            pool.wait_ge(q("ssm.a"), 1)
            for u in range(8):
                c, g, hq = u // 4, u // 2 % 2, u % 2
                if u >= 2:
                    pool.wait_ge(q("ssm.seg"), u - 1)
                g_.tensor_tensor(AS[u % 2][:], bc(SG[:, P:2 * P].unsqueeze(1), [P, 4, P]),
                                 bc(a_t[:, c, 8 * g + 4 * hq:8 * g + 4 * hq + 4].unsqueeze(2), [P, 4, P]), ALU.mult)\
                    .then_inc(q("ssm.as"), 1)
                if u == 1:
                    pool.wait_ge(q("ssm.xt"), 4)
                    for t in range(2):
                        last = g_.tensor_tensor(Y[:, t, :].rearrange("p (h d) -> p h d", h=H),
                                                XsT[:, t, :].rearrange("p (h d) -> p h d", h=H),
                                                bc(rows[:, 48:64].unsqueeze(2), [P, H, HD]), ALU.mult)
                    last.then_inc(q("ssm.dx"), 1)
            pool.wait_ge(q("ssmt.y"), nth("ssmt.y", 1))
            pool.wait_ge(q("ssmt.tr"), 4)
            for k in range(MOD_FIRST, 20):
                load_modulation(k)
            for h in range(H):
                if h >= 2 and h % 2 == 0 and 20 + h // 2 - 1 < MOD_SLOTS:
                    load_modulation(20 + h // 2 - 1)
                if h >= 2:
                    pool.wait_ge(q("fox.qk"), nth("fox.qk", 2 * h - 2))
                g_.tensor_scalar(RB[h % 2][:, 0:P], SG[:, P:2 * P], lf[:, 0, h:h + 1], None, ALU.mult)
                g_.tensor_scalar(RB[h % 2][:, P:3 * P], SG[:, :], lf[:, 1, h:h + 1], None, ALU.mult)\
                    .then_inc(q("fox.rb"), 1)

            def sums(name, src, event, count=lambda k: k + 1):
                for ft in range(KC):
                    event(ft)
                    if ft == 0:
                        ins = g_.tensor_copy(acc[:], src[:, 0, :])
                    else:
                        pool.wait_ge(q(name + ".acc"), nth(name + ".acc", ft))
                        ins = g_.tensor_tensor(acc[:], acc[:], src[:, ft, :], ALU.add)
                    ins.then_inc(q(name + ".acc"), 1)

            def squares(name):
                sums(name, T8, lambda ft: pool.wait_ge(q(name + ".sq"), nth(name + ".sq", ft + 1)))

            def mem(l, m_hi, m_lo):
                for ft in range(KC):
                    own(g_.tensor_scalar(mtmp[:, ft % 2, :], memN[:, ft, :], pc("mem", 8 * l + ft), None, ALU.mult))
                    own(g_.tensor_copy(m_hi[:, ft, :], mtmp[:, ft % 2, :]))
                    g_.tensor_tensor(m_lo[:, ft, :], mtmp[:, ft % 2, :], m_hi[:, ft, :].bitcast(F32),
                                     ALU.subtract).then_inc(q(f"mem{l}.lo"), 1)

            sums("wout", X, lambda ft: taken(pool, st["woutb"].j0 + ft // 2))
            sums("ffout", X, lambda ft: taken(pool, st["ffout"].j0 + ft))
            squares("ln2")
            squares("f1out0")
            squares("pool")
            squares("xo0")
            squares("f2out0")
            squares("f1out1")
            pool.wait_ge(s_mm, st["ng"].n0 + 1)
            mem(1, x_hi, x_lo)
            squares("no")
            squares("xo1")
            squares("f2out1")


def _cols(a):
    import numpy as np
    return np.ascontiguousarray(np.reshape(a, (-1, P)).T)


def _slots(a, cols):
    import numpy as np
    k, n = a.shape
    a = np.reshape(a, (k // P, P, n // cols, cols))
    return np.ascontiguousarray(np.transpose(a, (2, 1, 0, 3)).reshape(n // cols, P, -1))


def _rows(a):
    import numpy as np
    a = np.reshape(a.T, (a.shape[1] // (2 * P), 2, P, D))
    return np.ascontiguousarray(np.transpose(a, (0, 2, 1, 3)).reshape(-1, P, 2 * D))


def _tiles(a, parts):
    import numpy as np
    k, n = a.shape
    a = np.reshape(a, (parts, k // P // parts, P, n // P, P))
    return np.ascontiguousarray(np.transpose(a, (3, 0, 2, 1, 4)).reshape(n // P * parts, P, -1))


def _pairs(a):
    import numpy as np
    k, n = a.shape
    a = np.reshape(a, (k // P, P, 2, n // 2 // P, P))
    return np.ascontiguousarray(np.transpose(a, (3, 1, 0, 2, 4)).reshape(n // 2 // P, P, -1))


def _features(a):
    import numpy as np
    return np.ascontiguousarray(np.transpose(np.reshape(a, (S, KC, P)), (2, 1, 0)))


def lay_out(x):
    import numpy as np
    g = lambda n: np.asarray(x[n])
    out = {}
    ada, w_in = g("w_ada")[0], g("w_in")[0]
    out["ada"] = _rows(ada)
    out["z"], out["xbc"] = _slots(w_in[:, :1024], 256), _slots(w_in[:, 1024:2560], 256)[[4, 5, 0, 1, 2, 3]]
    out["dtf"] = _slots(np.concatenate([w_in[:, 2560:2576], w_in[:, 5648:5664]], 1), 32)
    for k, name in enumerate("qkv"):
        out[name] = _slots(w_in[:, 2576 + 1024 * k:3600 + 1024 * k], 256)
    out["wouta"], out["woutb"] = _slots(g("w_out")[0][:D], 256), _slots(g("w_out")[0][D:], 256)
    out["ffin"], out["ffout"] = _slots(g("w_ff_in")[0], 256), _tiles(g("w_ff_out")[0], 2)
    for l in range(2):
        for f in (1, 2):
            out[f"f{f}in{l}"] = _pairs(g(f"ffn{f}_w_in_2")[l])
            out[f"f{f}out{l}"] = _tiles(g(f"ffn{f}_w_out_2")[l], 2)
        kv = g("xattn_w_kv_2")[l]
        out[f"xk{l}"], out[f"xv{l}"] = _slots(kv[:, :1024], 256), _slots(kv[:, 1024:], 256)
        out[f"xq{l}"], out[f"xo{l}"] = _slots(g("xattn_w_q_2")[l], 256), _slots(g("xattn_w_o_2")[l], 256)
    pool = np.reshape(g("pool_w_2")[0], (4, 2, P, 256))
    out["pool"] = np.ascontiguousarray(np.transpose(pool, (2, 0, 1, 3)).reshape(1, P, -1))
    nsa = g("nsa_w_in_2")[0]
    out["nq"] = _slots(nsa[:, :1024], 256)
    for k, name in enumerate(("nkc", "nvc", "nks", "nvs", "nkw", "nvw")):
        out[name] = _slots(nsa[:, 1024 + 256 * k:1280 + 256 * k], 256)
    out["ng"] = _slots(nsa[:, 2560:], 48)
    for k, name in enumerate(("cmpk", "cmpv")):
        w1 = g("nsa_cmp_w1_2")[0, k]
        out[name] = np.concatenate([_slots(w1[:D], 256), _slots(w1[D:], 256)])
    out["no"] = _slots(g("nsa_w_o_2")[0], 256)

    conv = g("conv_w")[0]
    w2 = np.reshape(g("nsa_cmp_w2_2")[0], (2, 2, P, HD))
    w2k = np.transpose(w2[0], (1, 0, 2))
    pos = np.reshape(g("nsa_cmp_pos_2")[0], (2, CMP_J, P))
    parts = {"b_ada": _cols(g("b_ada")),
             "conv_w": np.concatenate([_cols(conv[k]) for k in range(4)], 1), "conv_b": _cols(g("conv_b")),
             "ssm_w": _cols(g("ssm_norm_w")), "attn_w": _cols(g("attn_norm_w")),
             "ln1_g": _cols(g("ln1_g")), "ln1_b": _cols(g("ln1_b")), "ln2_g": _cols(g("ln2_g")),
             "ln2_b": _cols(g("ln2_b")), "ffn1": _cols(g("ffn1_norm_2")), "mix": _cols(g("mix_norm_2")),
             "xattn": _cols(g("xattn_norm_2")), "mem": _cols(g("mem_norm_2")), "ffn2": _cols(g("ffn2_norm_2")),
             "pool_b": _cols(g("pool_b_2")), "pool_s": _cols(g("pool_scale_2")), "final": _cols(g("final_norm_2")),
             "pos_k": pos[0].T, "pos_v": pos[1].T,
             "w2k": np.concatenate([w2k, w2k], 2).reshape(P, 256),
             "w2v": np.transpose(w2[1], (1, 0, 2)).reshape(P, 128)}
    par = np.ascontiguousarray(np.concatenate([parts[n] for n, _ in _WIDTHS], 1))
    rows = np.concatenate([g("dt_bias")[0], g("f_bias")[0], g("a_log")[0], g("d_skip")[0]])
    rows = np.ascontiguousarray(np.broadcast_to(rows, (P, 64)))
    cond = np.ascontiguousarray(np.broadcast_to(g("c"), (P, D)))
    return out, _features(g("x")[0]), _features(g("mem_2")[0]), par, rows, cond


def kernel(**inputs):
    import numpy as np
    import concourse.bacc as bacc
    from concourse.bass_utils import run_bass_kernel_spmd

    streams, x, mem, par, rows, cond = lay_out(inputs)
    nc = bacc.Bacc("TRN2", target_bir_lowering=False, num_devices=1)
    arrays = {}

    def given(name, a):
        arrays[name] = a
        return nc.dram_tensor(name, a.shape, F32, kind="ExternalInput").ap()

    w = {name: given("w_" + name, streams[name]) for name in streams}
    args = [given(n, a) for n, a in (("xT", x), ("memT", mem), ("par_in", par), ("rows_in", rows),
                                 ("cond_in", cond))]
    out = nc.dram_tensor("out", (P, KC, S), F32, kind="ExternalOutput").ap()
    build(nc, w, *args, out)
    got = run_bass_kernel_spmd(nc, [arrays], core_ids=[0]).results[0]["out"]
    return np.ascontiguousarray(np.transpose(got, (2, 1, 0)).reshape(1, S, D))
```

```python
from contextlib import ExitStack

import concourse.bass as bass
from concourse import mybir

F32 = mybir.dt.float32
F32R = mybir.dt.float32r
ACT = mybir.ActivationFunctionType
ALU = mybir.AluOpType
AX = mybir.AxisListType

P = 128
S = 256
D = 1024
KC = D // P
H = 16
HD = 64
XH = 4
G_KV = 4
NCMP = (S - 32) // 16 + 1
GB = G_KV * NCMP
HB = 8 * NCMP
CMP_J = 16
HID1 = 4 * D // P
HID2 = 22
RING = 4
SLOT = 2048
AHEAD = 2
SHARE = 8
NEG = -1e30
ALPHA = 2.0 ** 0.25
EPS1, EPS2 = 1e-5, 1e-6

_WIDTHS = [("b_ada", 48), ("conv_w", 48), ("conv_b", 12), ("ssm_w", 8), ("attn_w", 8),
           ("ln1_g", 8), ("ln1_b", 8), ("ln2_g", 8), ("ln2_b", 8), ("ffn1", 16), ("mix", 16),
           ("xattn", 16), ("mem", 16), ("ffn2", 16), ("pool_b", 8), ("pool_s", 8), ("final", 8),
           ("pos_k", 16), ("pos_v", 16), ("w2k", 256), ("w2v", 128)]
COL, NPAR = {}, 0
for _name, _width in _WIDTHS:
    COL[_name] = NPAR
    NPAR += _width

_FFN = lambda l, f: [(f"f{f}in{l}", HID2, SLOT), (f"f{f}out{l}", 16, 11 * P)]
_XMEM = lambda l: [(f"xk{l}", 4, SLOT), (f"xv{l}", 4, SLOT)]
_XATTN = lambda l: [(f"xq{l}", 4, SLOT), (f"xo{l}", 4, SLOT)]
STAGES = (_XMEM(0) + [("dtf", 1, 256), ("xbc", 6, SLOT), ("z", 4, SLOT), ("q", 4, SLOT),
                      ("k", 4, SLOT), ("v", 4, SLOT), ("wouta", 4, SLOT), ("woutb", 4, SLOT),
                      ("ffin", 16, SLOT), ("ffout", 16, SLOT)]
          + _FFN(0, 1) + [("pool", 1, SLOT)] + _XATTN(0) + _FFN(0, 2)
          + _FFN(1, 1) + [("nq", 4, SLOT), ("nkc", 1, SLOT), ("nvc", 1, SLOT),
                          ("nks", 1, SLOT), ("nkw", 1, SLOT), ("nvs", 1, SLOT),
                          ("nvw", 1, SLOT), ("ng", 1, 384), ("cmpk", 2, SLOT),
                          ("cmpv", 2, SLOT)] + _XMEM(1) + [("no", 4, SLOT)] + _XATTN(1) + _FFN(1, 2))
MOD_SLOTS, MOD_FIRST = 24, 8


_FAMILIES = {
    "att": ([("fox", 32), ("xa0", 8), ("ns", 32), ("nw", 32), ("xa1", 8)],
            {k: None for k in ("qk", "l", "p", "tp", "pt", "pv")} | {"o": 4}),
    "res": ([("wout", 1), ("ln1", 1), ("ffout", 1), ("ln2", 1), ("f1out0", 1), ("pool", 1), ("xo0", 1),
             ("f2out0", 1), ("f1out1", 1), ("no", 1), ("xo1", 1), ("f2out1", 1)],
            {"hi": 8, "lo": 8, "sq": 8, "acc": 8, "mean": 1, "root": 1}),
    "ffn": ([("ffin", 16), ("f1in0", 22), ("f2in0", 22), ("f1in1", 22), ("f2in1", 22)],
            {k: None for k in ("sg", "h", "hi", "lo")}),
    "mix": ([("ssmt", 1), ("foxt", 1), ("xa0t", 1), ("nsat", 1), ("xa1t", 1)],
            {"y": 1, "tr": 4, "tev": 4, "hi": 8, "lo": 8}),
}
_ODD = {("wout", "hi"): 0, ("wout", "lo"): 0, ("wout", "sq"): 0,
        ("ln1", "sq"): 0, ("ln1", "acc"): 0, ("ln1", "mean"): 0, ("ln1", "root"): 0,
        ("ffout", "hi"): 0, ("ffout", "lo"): 0, ("ffout", "sq"): 0, ("ffin", "sg"): 0,
        ("f2out1", "hi"): 0, ("f2out1", "lo"): 0,
        ("f1out1", "mean"): 2, ("f1out1", "root"): 2}
SHARED = {}
for _fam, (_steps, _kinds) in _FAMILIES.items():
    for _kind, _each in _kinds.items():
        _before = 0
        for _step, _units in _steps:
            SHARED[f"{_step}.{_kind}"] = (f"{_fam}_{_kind}", _before)
            _before += _ODD.get((_step, _kind), _units if _each is None else _each)


class Stage:

    def __init__(self, name, slots, size, n0, j0):
        self.name, self.slots, self.size, self.n0, self.j0 = name, slots, size, n0, j0


def plan():
    out, n, j = {}, 0, 0
    for name, slots, size in STAGES:
        out[name] = Stage(name, slots, size, n, j)
        n += slots
        if name != "pool":
            j += slots // 2 if name[:3] == "cmp" or name[0] == "f" and "out" in name else slots
    return out


def build(nc, w, xT_d, memT_d, par_d, rows_d, cond_d, out_d):
    st = plan()
    split_order = [(s, k) for s in st.values() for k in range(s.slots)]
    mem_kv = nc.dram_tensor("mem_kv", (2, P, KC * S), F32).ap()
    ctx = ExitStack()
    with ctx:
        def sb(name, shape, dt=F32, stack=ctx):
            return stack.enter_context(nc.sbuf_tensor(name, shape, dt))

        def sem(name):
            return ctx.enter_context(nc.semaphore(name))

        with ExitStack() as a:
            raw = [sb(f"raw{b}", [P, SLOT], F32, a) for b in range(RING)]
        w_lo = [sb(f"w_lo{b}", [P, SLOT], F32R) for b in range(RING)]
        w_hi = [sb(f"w_hi{b}", [P, SLOT], F32R) for b in range(RING)]
        X = sb("X", [P, KC, S])
        x_hi = sb("x_hi", [P, KC, S], F32R)
        x_lo = sb("x_lo", [P, KC, S], F32R)
        memN = sb("memN", [P, KC, S])
        par = sb("par", [P, NPAR])
        rows = sb("rows", [P, 64])
        ident = sb("ident", [P, P])
        U = sb("U", [P, P])
        SG = sb("SG", [P, S])
        mask = sb("mask", [P, S])
        ones_d = sb("ones_d", [P, P])
        ones = sb("ones", [P, P])
        zero = sb("zero", [P, 1])
        eps1 = sb("eps1", [P, 1])
        eps2 = sb("eps2", [P, 1])
        mod = sb("mod", [P, 48])
        mod1 = sb("mod1", [P, 48])
        ln_mod = sb("ln_mod", [P, 2, KC])
        R = sb("R", [P, S])
        Rs = sb("Rs", [P, S])
        RT = sb("RT", [P, 2])
        RTs = sb("RTs", [P, 2])
        acc = sb("acc", [P, S])
        icnt = sb("icnt", [P, 4, 16])
        pool_bs = sb("pool_bs", [P, KC])
        nmax = sb("nmax", [P, 96])
        ssum = sb("ssum", [P, 96])

        vis = sb("vis", [P, 1])
        cmask = sb("cmask", [P, 2, NCMP])
        KD = sb("KD", [P, G_KV, 2, NCMP])
        own_rows = sb("own_rows", [P, 8])
        wc = sb("wc", [P, 2, H])
        gates = sb("gates", [P, 2, 48])
        tok = {n: sb("tok_" + n, [P, 2, 32]) for n in ("v", "mag", "e", "den", "y", "y2", "poly", "sp")}
        dt_t = sb("dt_t", [P, 2, H])
        lf = sb("lf", [P, 2, H])
        a_t = sb("a_t", [P, 2, H])
        negA = sb("negA", [P, H])
        dend = sb("dend", [P, H])
        dout = sb("dout", [P, H])
        rtok = sb("rtok", [P, 2])
        rtoks = sb("rtoks", [P, 2])
        rs = sb("rs", [P, 8])

        def place(name, shape, dt, kib):
            with ExitStack() as a:
                if kib:
                    sb(f"pad_{name}", [P, int(kib * 256)], F32, a)
                return sb(name, shape, dt, a)

        gu = [place(f"gu{b}", [P, 2, S], F32, 2 * b) for b in range(2)]
        sg = [place(f"sg{b}", [P, 2 * S], F32, 4 + 2 * b) for b in range(2)]
        hb = [place(f"hb{b}", [P, 2 * S], F32, 8 + 2 * b) for b in range(2)]
        Lm = [place(f"Lm{b}", [P, S], F32, b) for b in range(2)]
        Pr = [place(f"Pr{b}", [P, S], F32, 2 + b) for b in range(2)]
        PT = [place(f"PT{b}", [P, 2, P], F32, 4 + b) for b in range(2)]
        Ot = [place(f"Ot{t}", [P, 512], F32, 6 + 2 * t) for t in range(2)]
        AS = [place(f"AS{b}", [P, 4, P], F32, 2 * b) for b in range(2)]
        E = [place(f"E{b}", [P, 4, P], F32, 4 + 2 * b) for b in range(2)]
        cond = place("cond", [P, D], F32, 8)
        HG = place("HG", [P, 2, 60], F32, 10)
        work_space = sb("work_space", [P, 12 * 256])

        hid_hi = place("hid_hi", [P, 32, S], F32R, 0)
        hid_lo = place("hid_lo", [P, 32, S], F32R, 32)
        T8 = place("T8", [P, KC, S], F32, 64)
        AO = place("AO", [P, 2, D], F32, 72)
        CX = place("CX", [P, 12, S + 4], F32, 0)
        Zs = place("Zs", [P, 2, D], F32, 16)
        XsT = place("XsT", [P, 2, D], F32, 24)
        XB = place("XB", [P, 12, S], F32, 32)
        STt = place("STt", [P, 2, 512], F32, 44)
        mod_w = [place(f"mod_w{k}", [P, SLOT], F32, kib) for k, kib in enumerate((8, 40, 0, 32))]
        mod_w2 = [place(f"mod_x{k}", [P, SLOT], F32, kib) for k, kib in enumerate((8, 40))]
        mh = place("mh", [P, KC, S], F32R, 48)
        ml = place("ml", [P, KC, S], F32R, 56)
        V0 = place("V0", [P, 2, D], F32, 16)
        xc = place("xc", [P, 2, D], F32, 48)
        Y = place("Y", [P, 2, D], F32, 56)
        BT = place("BT", [P, 2, P], F32, 72)
        xce = place("xce", [P, D], F32, 68)
        CB = place("CB", [P, 4, P], F32, 78)
        RB = [place(f"RB{b}", [P, 384], F32, 68 + 1.5 * b) for b in range(2)]
        qT = place("qT", [P, KC, S], F32, 16)
        kT = place("kT", [P, KC, S], F32, 24)
        V = place("V", [P, 2, D], F32, 48)
        ks = place("ks", [P, 2, G_KV, S], F32, 24)
        kw = place("kw", [P, 2, G_KV, S], F32, 32)
        kz = [place(f"kz{b}", [P, KC, S], F32, (24, 56)[b]) for b in range(2)]
        vs = place("vs", [P, 2, 256], F32, 48)
        vw = place("vw", [P, 2, 256], F32, 50)
        Z = place("Z", [P, G_KV, S], F32, 52)
        bk = place("bk", [P, CMP_J, G_KV, NCMP], F32, 56)
        bk_hi = [place(f"bk_hi{b}", [P, CMP_J, 60], F32R, 60 + 8 * b) for b in range(2)]
        bk_lo = [place(f"bk_lo{b}", [P, CMP_J, 60], F32R, 64 + 8 * b) for b in range(2)]
        Xk = place("Xk", [P, KC, S], F32, 40)
        Xv = place("Xv", [P, 2, D], F32, 8)
        LC = place("LC", [P, 2, H * NCMP], F32, 52)
        HX = place("HX", [P, 2, HB], F32, 54)
        VB = place("VB", [P, 512], F32, 56)
        GH = [place(f"GH{b}", [GB, 256], F32, 58 + b) for b in range(2)]
        wa = place("wa", [P, KC, S], F32, 16)
        wb = place("wb", [P, KC, S], F32, 24)
        arena = sb("arena", [P, 80 * 256])

        def pb(name):
            return ctx.enter_context(nc.psum_tensor(name, [P, 512], F32))

        G = [pb(f"G{b}") for b in range(2)]
        L = [pb(f"L{b}") for b in range(2)]
        T = [pb(f"T{b}") for b in range(2)]
        O = [pb(f"O{b}") for b in range(2)]

        pool_bank = T + O

        sems = {}

        def q(name):
            key = SHARED[name][0] if name in SHARED else name.replace(".", "_")
            if key not in sems:
                sems[key] = sem(key)
            return sems[key]

        def nth(name, count):
            return (SHARED[name][1] if name in SHARED else 0) + count

        s_load = [sem(f"s_load{b}") for b in range(RING)]
        s_hi = sem("s_hi")
        s_lo = sem("s_lo")
        s_mm = sem("s_mm")
        s_ev = [sem(f"s_ev{b}") for b in range(2)]
        s_in = sem("s_in")
        s_par = sem("s_par")
        s_rows = sem("s_rows")
        s_spill = sem("s_spill")
        s_back = sem("s_back")
        s_out = sem("s_out")

        def mod_buffer(k):
            if k < MOD_FIRST:
                return mod_w[k % 4], (k % 4, 16 * (k // 4 + 1))
            k -= MOD_FIRST
            return mod_w2[k % 2], (4 + k % 2, 16 * (k // 2 + 1))

        beside_slots = {"fox": [("wouta", 0), ("wouta", 1), ("wouta", 2)],
                        "ns": [("xk1", 2), ("xk1", 3), ("xv1", 0)], "nw": [("xv1", 1), ("xv1", 2)]}

        def mem_out(name, slot):
            return Xk[:, 2 * slot:2 * slot + 2, :] if name == "xk1" else Xv[:, :, slot * 256:(slot + 1) * 256]

        def window_sums(own, eng, c0, c1, turns):
            src = T8
            for g, dst in enumerate(turns):
                w_, c = 1 << g, slice(max(c0, 2 * g), c1)
                own(eng.tensor_copy(dst[:, c, 0:w_], src[:, c, 0:w_]))
                own(eng.tensor_tensor(dst[:, c, w_:S], src[:, c, w_:S], src[:, c, 0:S - w_], ALU.add))
                src = dst

        def window_means(own, eng, g):
            dst, c = (wa, wb)[g % 2], slice(2 * g, 2 * g + 2)
            own(eng.tensor_tensor(dst[:, c, 0:16], dst[:, c, 0:16], bc(icnt[:, g, :].unsqueeze(1), [P, 2, 16]), ALU.mult))
            own(eng.tensor_scalar(dst[:, c, 16:S], dst[:, c, 16:S], 1.0 / (2 << g), None, ALU.mult))
            own(eng.tensor_tensor(dst[:, c, :], dst[:, c, :], T8[:, c, :], ALU.subtract))

        def xbc_slot(slot):
            return (slot + 4) % 6

        def pc(name, k=0):
            return par[:, COL[name] + k:COL[name] + k + 1]

        def bc(ap, shape):
            return ap.broadcast_to(shape)

        class Chain:

            def __init__(self, eng, name):
                self.eng, self.sem, self.n = eng, q(name), 0

            def __call__(self, ins):
                self.n += 1
                ins.then_inc(self.sem, 1)
                self.eng.wait_ge(self.sem, self.n)

        def taken(eng, j, i=0, groups=4):
            eng.wait_ge(s_ev[j % 2], j // 2 + 1 + i * (groups // 2))

        def all_taken(eng, j):
            for back in (1, 2):
                taken(eng, j - back)

        def tiles2(bank):
            return bank[:, :].rearrange("p (f c) -> p f c", f=2)

        def h8(ap):
            return ap.rearrange("p (h d) -> p h d", h=8)

        block = ctx.enter_context(nc.Block())

        @block.sync
        def _(sp):
            sp.dma_start(memN[:], memT_d).then_inc(q("mem_in"), 16)
            sp.dma_start(par[:], par_d).then_inc(s_par, 16)

            def load(s, slot, i=0):
                n = s.n0 + slot
                if n >= RING:
                    sp.wait_ge(s_mm, n - RING + 1 + i * RING)
                sp.dma_start(raw[n % RING][:, 0:s.size], w[s.name][slot + i * RING]).then_inc(s_load[n % RING], 16)

            for s in st.values():
                turns = s.slots // RING
                if s.name == "dtf":
                    all_taken(sp, st["xv0"].j0)
                    sp.dma_start(mem_kv[0], kT[:]).then_inc(s_spill, 16)
                if s.name == "xo0":
                    sp.wait_ge(s_mm, st["f1out0"].n0 + 16)
                    sp.wait_ge(s_spill, 32)
                    sp.dma_start(Xk[:], mem_kv[0]).then_inc(s_back, 16)
                    sp.dma_start(Xv[:], mem_kv[1]).then_inc(s_back, 16)
                if turns >= 2:
                    with sp.Fori(0, turns) as i:
                        for slot in range(RING):
                            load(s, slot, i)
                for slot in range(turns * RING if turns >= 2 else 0, s.slots):
                    load(s, slot)
                    if s.n0 + slot == 1:
                        sp.dma_start(rows[:], rows_d).then_inc(s_rows, 16)
                        sp.dma_start(cond[:], cond_d).then_inc(q("cond_in"), 16)
                    if s.n0 + slot == 3:
                        sp.dma_start(X[:], xT_d).then_inc(s_in, 16)
                    if s.name == "xbc" and slot == 4:
                        all_taken(sp, st["dtf"].j0)
                        sp.dma_start(mem_kv[1], V0[:]).then_inc(s_spill, 16)
            for ft in range(KC):
                sp.wait_ge(q("final"), ft + 1)
                sp.dma_start(out_d[:, ft, :], T8[:, ft, :]).then_inc(s_out, 16)
            sp.wait_ge(s_out, 16 * KC)

        @block.tensor
        def _(pe):
            mm = nc.tensor.matmul

            def mm3(out, l_hi, l_lo, r_hi, r_lo, start, stop):
                mm(out, l_hi, r_hi, start=start, stop=False)
                mm(out, l_hi, r_lo, start=False, stop=False)
                return mm(out, l_lo, r_hi, start=False, stop=stop)

            def slot_begins(s, slot, j, i, groups):
                pe.wait_ge(s_lo, s.n0 + slot + 1 + i * RING)
                if j is not None and j >= 2:
                    pe.wait_ge(s_ev[j % 2], j // 2 + i * (groups // 2))

            def gemm_a(s, slot, j, x_h, x_l, kn=KC, nf=2, k0=0, start=True, stop=True, cols=S,
                       ready=None, i=0, groups=4):
                n = s.n0 + slot
                slot_begins(s, slot, j if start else None, i, groups)
                wh = w_hi[n % RING][:, 0:kn * nf * P].rearrange("p (k f c) -> p k f c", k=kn, f=nf)
                wl = w_lo[n % RING][:, 0:kn * nf * P].rearrange("p (k f c) -> p k f c", k=kn, f=nf)
                for f in range(nf):
                    for k in range(kn):
                        if ready and f == 0:
                            pe.wait_ge(q(ready), nth(ready, k + 1))
                        last = mm3(G[j % 2][:, f * S:f * S + cols], wh[:, k, f, :], wl[:, k, f, :],
                                   x_h[:, k0 + k, 0:cols], x_l[:, k0 + k, 0:cols],
                                   start and k == 0, stop and k == kn - 1)
                last.then_inc(s_mm, 1)

            def gemm_b(s, slot, j, x_h, x_l, width=256, ready=None, k0=0):
                n = s.n0 + slot
                slot_begins(s, slot, j, 0, 4)
                wh = w_hi[n % RING][:, 0:KC * width].rearrange("p (k c) -> p k c", k=KC)
                wl = w_lo[n % RING][:, 0:KC * width].rearrange("p (k c) -> p k c", k=KC)
                for t in range(2):
                    for k in range(KC):
                        if ready and t == 0:
                            pe.wait_ge(q(ready), nth(ready, k + 1))
                        tk = slice(t * P, t * P + P)
                        last = mm3(G[j % 2][:, t * width:(t + 1) * width], x_h[:, k0 + k, tk], x_l[:, k0 + k, tk],
                                   wh[:, k, :], wl[:, k, :], k == 0, k == KC - 1)
                last.then_inc(s_mm, 1)

            def share(attention_name, at_, x_h, x_l, ready=None):
                turn, part = divmod(at_, SHARE)
                if turn >= len(beside_slots[attention_name]):
                    return
                name, slot = beside_slots[attention_name][turn]
                s, tokens_first = st[name], name == "xv1"
                n, j, each = s.n0 + slot, s.j0 + slot, 2 * KC // SHARE
                if part == 0:
                    slot_begins(s, slot, j, 0, 4)
                wh = w_hi[n % RING][:, :].rearrange("p (k c) -> p k c", k=KC)
                wl = w_lo[n % RING][:, :].rearrange("p (k c) -> p k c", k=KC)
                for both in range(part * each, (part + 1) * each):
                    f, k = divmod(both, KC)
                    if ready and at_ < SHARE // 2:
                        pe.wait_ge(q(ready), nth(ready, k + 1))
                    c = slice(f * P, f * P + P)
                    if tokens_first:
                        last = mm3(G[j % 2][:, f * S:(f + 1) * S], x_h[:, k, c], x_l[:, k, c],
                                   wh[:, k, :], wl[:, k, :], k == 0, k == KC - 1)
                    else:
                        last = mm3(G[j % 2][:, f * S:(f + 1) * S], wh[:, k, c], wl[:, k, c],
                                   x_h[:, k, :], x_l[:, k, :], k == 0, k == KC - 1)
                if part == SHARE - 1:
                    last.then_inc(s_mm, 1)

            def mean(name, bank, by_token=False):
                pe.wait_ge(q(name + ".acc"), nth(name + ".acc", KC))
                last = mm(bank[:, 0:S], ones_d[:], acc[:], start=True, stop=True)
                last.then_inc(q(name + ".mean"), 1)
                if by_token:
                    for t in range(2):
                        last = mm(T[0][:, t:t + 1], acc[:, t * P:(t + 1) * P], ones_d[:, 0:1], start=True, stop=True)
                    last.then_inc(q(name + ".mean"), 1)

            def mean8(name, bank, ready=None):
                for k in range(KC):
                    if ready:
                        pe.wait_ge(q(ready), k + 1)
                    last = mm(bank[:, 0:S], ones_d[:], T8[:, k, :], start=k == 0, stop=k == KC - 1)
                last.then_inc(q(name + ".var"), 1)

            def transposes(name, src):
                pe.wait_ge(q(name + ".y"), nth(name + ".y", 1))
                for b in range(4):
                    if b >= 2:
                        pe.wait_ge(q(name + ".tev"), nth(name + ".tev", b - 1))
                    for f in range(2):
                        for t in range(2):
                            ft = 2 * b + f
                            last = nc.tensor.transpose(T[b % 2][:, f * S + t * P:f * S + t * P + P],
                                                       src[:, t, ft * P:(ft + 1) * P], ident[:])
                    last.then_inc(q(name + ".tr"), 1)

            def attention(name, heads, hd, keys, qk, pv, beside=None):
                units = [(h, t) for h in range(heads) for t in range(2)]
                per = 512 // hd
                for step in range(len(units) + 2):
                    if step < len(units):
                        h, t = units[step]
                        if step >= 2:
                            pe.wait_ge(q(name + ".l"), nth(name + ".l", step - 1))
                        qk(h, t, L[step % 2]).then_inc(q(name + ".qk"), 1)
                    if 1 <= step <= len(units):
                        u = step - 1
                        h, t = units[u]
                        nk = keys(t)
                        pe.wait_ge(q(name + ".p"), nth(name + ".p", u + 1))
                        if u >= 2:
                            pe.wait_ge(q(name + ".pt"), nth(name + ".pt", u - 1))
                        for c in range((nk + P - 1) // P):
                            w_ = min(P, nk - c * P)
                            last = nc.tensor.transpose(T[u % 2][0:w_, c * P:(c + 1) * P],
                                                       Pr[u % 2][:, c * P:c * P + w_], ident[:])
                        last.then_inc(q(name + ".tp"), 1)
                    if step >= 2:
                        u = step - 2
                        h, t = units[u]
                        nk = keys(t)
                        pe.wait_ge(q(name + ".pt"), nth(name + ".pt", u + 1))
                        half = h // per
                        if half and h % per == 0:
                            pe.wait_ge(q(name + ".o"), nth(name + ".o", 2 * (half - 1) + t + 1))
                        nch = (nk + P - 1) // P
                        for c in range(nch):
                            w_ = min(P, nk - c * P)
                            last = mm(O[t][:, (h % per) * hd:(h % per + 1) * hd], PT[u % 2][0:w_, c, :],
                                      pv(h, c), start=c == 0, stop=c == nch - 1)
                        last.then_inc(q(name + ".pv"), 1)
                    if beside:
                        beside(step)

            pe.wait_ge(q("consts"), 1)
            pe.wait_ge(q("mem.acc"), 1)
            mm(L[1][:, 0:S], ones_d[:], T8[:, 0, :], start=True, stop=True).then_inc(q("mem.var"), 1)
            for slot in range(4):
                gemm_a(st["xk0"], slot, st["xk0"].j0 + slot, mh, ml, ready="mem0.lo" if slot == 0 else None)
            for slot in range(4):
                gemm_b(st["xv0"], slot, st["xv0"].j0 + slot, mh, ml)
            gemm_b(st["dtf"], 0, st["dtf"].j0, x_hi, x_lo, width=32, ready="h0.lo")
            for slot in range(6):
                gemm_a(st["xbc"], slot, st["xbc"].j0 + slot, x_hi, x_lo)

            def z_slot(slot):
                gemm_b(st["z"], slot, st["z"].j0 + slot, x_hi, x_lo)

            pe.wait_ge(q("ssm.conv"), 4)
            for g in range(2):
                last = nc.tensor.transpose(L[0][:, g * P:(g + 1) * P], XB[:, 8 + g, 0:P], ident[:])
            last.then_inc(q("ssm.bt"), 1)
            for cg in range(4):
                c, g = divmod(cg, 2)
                last = mm(O[0][:, cg * P:(cg + 1) * P], XB[:, 8 + g, c * P:(c + 1) * P],
                          XB[:, 10 + g, c * P:(c + 1) * P], start=True, stop=True)
            last.then_inc(q("ssm.cb"), 1)
            pe.wait_ge(q("ssm.a"), 1)
            mm(L[1][:, 0:H], SG[:, P:2 * P], a_t[:, 0, :], start=True, stop=True)
            mm(L[1][:, H:2 * H], U[:], a_t[:, 1, :], start=True, stop=True).then_inc(q("ssm.cs"), 1)
            z_slot(0)
            for b in range(4):
                t, fh = divmod(b, 2)
                pe.wait_ge(q("ssm.conv"), 4 * fh + 8)
                if b >= 2:
                    pe.wait_ge(q("ssm.xt"), b - 1)
                for k in range(4):
                    last = nc.tensor.transpose(T[b % 2][:, k * P:(k + 1) * P], XB[:, 4 * fh + k, t * P:(t + 1) * P], ident[:])
                last.then_inc(q("ssm.xtr"), 1)
                if b == 1:
                    z_slot(1)
            z_slot(2)
            z_slot(3)
            pe.wait_ge(q("ssm.xt"), 4)

            def chunk_states():
                pe.wait_ge(q("ssm.xce"), 1)
                pe.wait_ge(q("ssm.bts"), 1)
                all_taken(pe, st["q"].j0)
                for g in range(2):
                    mm(G[g][:, :], BT[:, g, :], xce[:, g * 512:(g + 1) * 512], start=True, stop=True)\
                        .then_inc(q("ssm.state"), 1)

            def from_states():
                for g in range(2):
                    pe.wait_ge(q("ssm.st"), g + 1)
                    mm(L[g][:, :], XB[:, 10 + g, P:2 * P], STt[:, g, :], start=True, stop=True).then_inc(q("ssm.off"), 1)

            for u in range(9):
                if u < 8:
                    pe.wait_ge(q("ssm.as"), u + 1)
                    if u >= 2:
                        pe.wait_ge(q("ssm.e"), u - 1)
                    for k in range(4):
                        last = mm(T[u % 2][:, k * P:(k + 1) * P], AS[u % 2][:, k, :], U[:], start=True, stop=True)
                    last.then_inc(q("ssm.seg"), 1)
                if u >= 1:
                    v = u - 1
                    c, g, hq = v // 4, v // 2 % 2, v % 2
                    pe.wait_ge(q("ssm.sc"), v + 1)
                    if v >= 4 and hq == 0:
                        pe.wait_ge(q("ssm.yo"), v // 2 - 1)
                    for k in range(4):
                        h = 8 * g + 4 * hq + k
                        last = mm(O[g][:, (4 * hq + k) * HD:(4 * hq + k + 1) * HD], E[v % 2][:, k, :],
                                  xc[:, c, h * HD:(h + 1) * HD], start=True, stop=True)
                    last.then_inc(q("ssm.ydiag"), 1)
                if u == 2:
                    chunk_states()
                if u == 4:
                    from_states()

            for slot in range(4):
                gemm_a(st["q"], slot, st["q"].j0 + slot, x_hi, x_lo)
                if slot == 1:
                    transposes("ssmt", Y)
            for slot in range(4):
                gemm_a(st["k"], slot, st["k"].j0 + slot, x_hi, x_lo)
            for slot in range(4):
                gemm_b(st["v"], slot, st["v"].j0 + slot, x_hi, x_lo)

            def qk_fox(h, t, bank):
                if t == 0:
                    pe.wait_ge(q("fox.rb"), h + 1)
                    mm(bank[:, 0:P], U[:], RB[h % 2][:, 0:P], start=True, stop=False)
                    return mm(bank[:, 0:P], qT[:, h // 2, 0:P], kz[h % 2][:, h // 2, 0:P], start=False, stop=True)
                mm(bank[:, 0:S], U[:], RB[h % 2][:, P:3 * P], start=True, stop=False)
                mm(bank[:, 0:P], ones[:], RB[h % 2][:, 0:P], start=False, stop=False)
                return mm(bank[:, 0:S], qT[:, h // 2, P:S], kz[h % 2][:, h // 2, :], start=False, stop=True)

            all_taken(pe, st["wouta"].j0)
            pe.wait_ge(q("fox.zero"), 1)
            attention("fox", H, HD, lambda t: P * (t + 1), qk_fox, lambda h, c: V[:, c, h * HD:(h + 1) * HD],
                      lambda step: share("fox", step, hid_hi, hid_lo, ready="ssmt.lo"))
            gemm_a(st["wouta"], 3, st["wouta"].j0 + 3, hid_hi, hid_lo)
            transposes("foxt", AO)

            s = st["woutb"]
            for slot in range(4):
                gemm_a(s, slot, s.j0 + slot, hid_hi, hid_lo, k0=8, ready="foxt.lo" if slot == 0 else None)
            mean("wout", L[0])
            mean8("wout", L[1], "wout.sq8")

            def ffn_in(s, ready, after_first=None):
                gemm_a(s, 0, s.j0, x_hi, x_lo, ready=ready)
                if after_first:
                    after_first()
                for slot in range(1, 4):
                    gemm_a(s, slot, s.j0 + slot, x_hi, x_lo)
                turns = s.slots // RING - 1
                with pe.Fori(0, turns) as i:
                    for slot in range(4, 8):
                        gemm_a(s, slot, s.j0 + slot, x_hi, x_lo, i=i)
                for slot in range(4 + 4 * turns, s.slots):
                    gemm_a(s, slot, s.j0 + slot, x_hi, x_lo)

            def ffn_out(s, hidden, chunks, per_slot):
                kn = chunks // 2

                def tile_of(g, i=0, first=False):
                    for part in range(2):
                        if first:
                            pe.wait_ge(q(hidden), nth(hidden, (part + 1) * kn // per_slot))
                        gemm_a(s, 2 * g + part, s.j0 + g, hid_hi, hid_lo, kn=kn, nf=1, k0=part * kn,
                               start=part == 0, stop=part == 1, i=i, groups=2)

                tile_of(0, first=True)
                tile_of(1)
                with pe.Fori(0, 3) as i:
                    tile_of(2, i)
                    tile_of(3, i)

            ffn_in(st["ffin"], "ln1.lo")
            ffn_out(st["ffout"], "ffin.lo", HID1, 2)
            mean("ffout", L[0])
            mean8("ffout", L[1], "ffout.sq8")

            def ffn(l, f, before):
                ffn_in(st[f"f{f}in{l}"], before + ".lo", lambda: mean(before, L[0]))
                ffn_out(st[f"f{f}out{l}"], f"f{f}in{l}.lo", HID2, 1)

            def xattn(l, before):
                name = f"xa{l}"
                j = {x: st[f"x{x}{l}"].j0 for x in "qo"}
                for slot in range(4):
                    gemm_a(st[f"xq{l}"], slot, j["q"] + slot, x_hi, x_lo,
                           ready=before + ".lo" if slot == 0 else None)
                    if slot == 0:
                        mean(before, L[0])
                all_taken(pe, j["o"])
                if l == 0:
                    pe.wait_ge(s_back, 32)

                def qk(h, t, bank):
                    for c in range(2):
                        last = mm(bank[:, 0:S], qT[:, 2 * h + c, t * P:(t + 1) * P], Xk[:, 2 * h + c, :],
                                  start=c == 0, stop=c == 1)
                    return last

                attention(name, XH, 256, lambda t: S, qk, lambda h, c: Xv[:, c, h * 256:(h + 1) * 256])
                transposes(name + "t", AO)
                for slot in range(4):
                    gemm_a(st[f"xo{l}"], slot, j["o"] + slot, hid_hi, hid_lo,
                           ready=name + "t.lo" if slot == 0 else None)

            ffn(0, 1, "ln2")
            s = st["pool"]
            pe.wait_ge(s_lo, s.n0 + 1)
            wh = w_hi[s.n0 % RING][:, :].rearrange("p (g k f c) -> p g k f c", g=4, k=2, f=2)
            wl = w_lo[s.n0 % RING][:, :].rearrange("p (g k f c) -> p g k f c", g=4, k=2, f=2)
            for g in range(4):
                if g == 3:
                    mean("f1out0", L[0])
                pe.wait_ge(q("f1out0.lo"), nth("f1out0.lo", 2 * g + 2))
                for f in range(2):
                    for k in range(2):
                        last = mm3(pool_bank[g][:, f * S:(f + 1) * S], wh[:, g, k, f, :], wl[:, g, k, f, :],
                                   x_hi[:, 2 * g + k, :], x_lo[:, 2 * g + k, :], k == 0, k == 1)
                last.then_inc(q("pmix.mm") if g < 3 else s_mm, 1)
            xattn(0, "pool")
            ffn(0, 2, "xo0")

            ffn(1, 1, "f2out0")
            for slot in range(4):
                gemm_a(st["nq"], slot, st["nq"].j0 + slot, x_hi, x_lo,
                       ready="f1out1.lo" if slot == 0 else None)
                if slot == 0:
                    mean("f1out1", L[0], by_token=True)
            for name in ("nkc", "nvc", "nks", "nkw"):
                gemm_a(st[name], 0, st[name].j0, x_hi, x_lo)
            for name, width in (("nvs", 256), ("nvw", 256), ("ng", 48)):
                gemm_b(st[name], 0, st[name].j0, x_hi, x_lo, width=width)
            for b, name in enumerate(("cmpk", "cmpv")):
                pe.wait_ge(q("nsa.bk"), b + 1)
                for slot in range(2):
                    s = st[name]
                    n = s.n0 + slot
                    slot_begins(s, slot, s.j0 if slot == 0 else None, 0, 4)
                    wh = w_hi[n % RING][:, :].rearrange("p (k c) -> p k c", k=KC)
                    wl = w_lo[n % RING][:, :].rearrange("p (k c) -> p k c", k=KC)
                    for k in range(KC):
                        last = mm3(G[s.j0 % 2][0:GB, 0:256], bk_hi[b][:, KC * slot + k, :], bk_lo[b][:, KC * slot + k, :],
                                   wh[:, k, :], wl[:, k, :], slot == 0 and k == 0, slot == 1 and k == KC - 1)
                    last.then_inc(s_mm, 1)
            gemm_a(st["xk1"], 0, st["xk1"].j0, x_hi, x_lo, ready="mem1.lo")
            w2k = par[:, COL["w2k"]:COL["w2k"] + 256].rearrange("p (k c) -> p k c", k=2)
            w2v = par[:, COL["w2v"]:COL["w2v"] + 128].rearrange("p (k c) -> p k c", k=2)
            for b, name in enumerate(("cmpk", "cmpv")):
                taken(pe, st[name].j0)
                for k in range(2):
                    last = nc.tensor.transpose(T[b][:, k * GB:(k + 1) * GB], GH[b][0:GB, k * P:(k + 1) * P],
                                               ident[0:GB, 0:GB])
                last.then_inc(q("nsa.ht"), 1)
            pe.wait_ge(q("nsa.hx"), 1)
            for k in range(2):
                last = mm(T[0][:, 0:60], w2k[:, k, :], HG[:, k, :], start=k == 0, stop=k == 1)
            last.then_inc(q("nsa.kc"), 1)
            pe.wait_ge(q("nsa.hx"), 2)
            for k in range(2):
                last = mm(T[1][0:HB, 0:HD], HX[:, k, :], w2v[:, k, :], start=k == 0, stop=k == 1)
            last.then_inc(q("nsa.kc"), 1)
            pe.wait_ge(q("nsa.ready"), 1)
            for t in range(2):
                both = L[t][:, 0:H * NCMP].rearrange("p (two c n) -> p c two n", two=2, n=NCMP)
                for c in range(KC):
                    last = mm(both[:, c], qT[:, c, t * P:(t + 1) * P], KD[:, c // 2], start=True, stop=True)
                last.then_inc(q("nc.qk"), 1)
            gemm_a(st["xk1"], 1, st["xk1"].j0 + 1, x_hi, x_lo)
            pe.wait_ge(q("nsa.vc"), 1)
            for t in range(2):
                pe.wait_ge(q("nc.w"), t + 1)
                for half in range(2):
                    last = nc.tensor.transpose(T[t][0:HB, half * P:(half + 1) * P],
                                               LC[:, t, half * HB:(half + 1) * HB], ident[:])
                last.then_inc(q("nc.tp"), 1)
            for t in range(2):
                pe.wait_ge(q("nc.pt"), t + 1)
                for half in range(2):
                    mm((O, L)[t][half][:, :], PT[t][0:HB, half, :], VB[0:HB, :], start=True, stop=True)\
                        .then_inc(q("nc.pv"), 1)

            def qk_nsa(keys):
                def f(h, t, bank):
                    nk = P * (t + 1)
                    return mm(bank[:, 0:nk], qT[:, h // 2, t * P:(t + 1) * P], keys[:, h % 2, h // 4, 0:nk],
                              start=True, stop=True)
                return f

            pe.wait_ge(q("nc.o"), 4)
            pe.wait_ge(q("nsa.halves"), 4)
            pe.wait_ge(q("nsa.zero"), 2)
            attention("ns", H, HD, lambda t: P * (t + 1), qk_nsa(ks),
                      lambda h, c: vs[:, c, (h // 4) * HD:(h // 4 + 1) * HD],
                      lambda step: share("ns", step, x_hi, x_lo))
            pe.wait_ge(q("ns.o"), nth("ns.o", 4))
            attention("nw", H, HD, lambda t: P * (t + 1), qk_nsa(kw),
                      lambda h, c: vw[:, c, (h // 4) * HD:(h // 4 + 1) * HD],
                      lambda step: share("nw", step, x_hi, x_lo))
            gemm_b(st["xv1"], 3, st["xv1"].j0 + 3, x_hi, x_lo)
            transposes("nsat", AO)
            for slot in range(4):
                gemm_a(st["no"], slot, st["no"].j0 + slot, hid_hi, hid_lo,
                       ready="nsat.lo" if slot == 0 else None)
            xattn(1, "no")
            ffn(1, 2, "xo1")
            mean("f2out1", L[0])

        @block.scalar
        def _(act):
            act_ = nc.scalar.activation
            own = Chain(act, "act_own")
            at = [0]

            def split(s, slot, i=0):
                n = s.n0 + slot
                act.wait_ge(s_load[n % RING], 16 * (n // RING + 1) + 16 * i)
                act_(w_hi[n % RING][:, 0:s.size], raw[n % RING][:, 0:s.size], ACT.Copy).then_inc(s_hi, 1)

            def splits_to(k):
                while at[0] <= min(k, len(split_order) - 1):
                    split(*split_order[at[0]])
                    at[0] += 1

            def result(s, slot, i=0):
                act.wait_ge(s_mm, s.n0 + slot + 1 + i * RING)

            def root(name, bank, eps, event=".mean", count=1, out=Rs[:]):
                act.wait_ge(q(name + event), nth(name + event, count))
                act_(out, bank, ACT.Sqrt, bias=eps[:]).then_inc(q(name + ".root"), 1)

            def copies(s, outs, func=ACT.Copy, scale=1.0):
                for slot in range(s.slots):
                    splits_to(s.n0 + slot + AHEAD)
                    result(s, slot)
                    act_(outs(slot), tiles2(G[(s.j0 + slot) % 2]), func, scale=scale).then_inc(s_ev[(s.j0 + slot) % 2], 1)

            def row_squares(name, src, junk):
                act.wait_ge(q(name + ".in"), nth(name + ".in", 1))
                for t in range(2):
                    act_(junk, src[:, t, :], ACT.Square, accum_out=rtok[:, t:t + 1]).then_inc(q(name + ".ss"), 1)
                    act.wait_ge(q(name + ".ss"), nth(name + ".ss", t + 1))
                act_(rtoks[:], rtok[:], ACT.Sqrt, bias=eps1[:], scale=1.0 / D).then_inc(q(name + ".root"), 1)

            def features_hi(name, chunk0, gain=None):
                for b in range(4):
                    act.wait_ge(q(name + ".tr"), nth(name + ".tr", b + 1))
                    for f in range(2):
                        ft = 2 * b + f
                        act_(hid_hi[:, chunk0 + ft, :], T[b % 2][:, f * S:(f + 1) * S], ACT.Copy,
                             scale=pc(gain, ft) if gain else 1.0).then_inc(q(name + ".hi"), 1)

            def beside(attention_name, u, out):
                turn, part = divmod(u, SHARE)
                slots = beside_slots[attention_name]
                if turn < len(slots) and part < 4:
                    name, slot = slots[turn]
                    t, k = split_order[st[name].n0 + slot + AHEAD]
                    n, each = t.n0 + k, t.size // 4
                    c = slice(part * each, (part + 1) * each)
                    if part == 0:
                        act.wait_ge(s_load[n % RING], 16 * (n // RING + 1))
                    last = act_(w_hi[n % RING][:, c], raw[n % RING][:, c], ACT.Copy)
                    if part == 3:
                        last.then_inc(s_hi, 1)
                        at[0] += 1
                if out and part == 0 and 1 <= turn <= len(slots):
                    take_mem(*slots[turn - 1])

            def take_mem(name, slot):
                j = st[name].j0 + slot
                result(st[name], slot)
                act_(mem_out(name, slot), tiles2(G[j % 2]), ACT.Copy).then_inc(s_ev[j % 2], 1)

            def attention(name, heads, keys, base, beside_=lambda u: None):
                for u in range(2 * heads):
                    h, t = divmod(u, 2)
                    act.wait_ge(q(name + ".l"), nth(name + ".l", u + 1))
                    if u >= 2:
                        act.wait_ge(q(name + ".tp"), nth(name + ".tp", u - 1))
                    nk, col = keys(t), base + t * heads + h
                    act_(Pr[u % 2][:, 0:nk], Lm[u % 2][:, 0:nk], ACT.Exp, bias=nmax[:, col:col + 1], scale=-1.0,
                         accum_out=ssum[:, col:col + 1]).then_inc(q(name + ".p"), 1)
                    beside_(u)
                beside_(2 * heads)

            def hi_and_squares(name, ft, gain, squares=True):
                if gain:
                    act_(x_hi[:, ft, :], X[:, ft, :], ACT.Copy, scale=pc(*gain(ft))).then_inc(q(name + ".hi"), 1)
                if squares:
                    act_(T8[:, ft, :], X[:, ft, :], ACT.Square).then_inc(q(name + ".sq"), 1)

            def residual(name, s, gain, nf, per):
                for g in range(KC // nf):
                    if s.name != "pool":
                        splits_to(s.n0 + g * per + per - 1 + AHEAD)
                        taken(act, s.j0 + g)
                    else:
                        act.wait_ge(q("pmix.u"), g + 1)
                    for f in range(nf):
                        hi_and_squares(name, g * nf + f, gain)

            def ffn_in(s, before, width, chunks):
                def slot_(slot, i=0):
                    j = s.j0 + slot
                    if chunks == 2:
                        result(s, slot, i)
                        act_(sg[slot % 2][:, :], G[j % 2][:, :], ACT.Relu).then_inc(s_ev[j % 2], 1)
                    else:
                        taken(act, j, i)
                        act_(sg[slot % 2][:, 0:S], gu[slot % 2][:, 0, :], ACT.Silu).then_inc(q(s.name + ".sg"), 1)
                    act.wait_ge(q(s.name + ".h"), nth(s.name + ".h", slot + 1 + i * RING))
                    c0 = chunks * slot + i * (chunks * RING)
                    act_(hid_hi[:, bass.ds(c0, chunks), :], hb[slot % 2][:, 0:width].rearrange("p (k c) -> p k c", k=chunks),
                         ACT.Copy).then_inc(q(s.name + ".hi"), 1)

                for slot in range(4):
                    splits_to(s.n0 + slot + AHEAD)
                    if slot == 0 and before:
                        root(before, L[0][:, 0:S], eps2)
                    slot_(slot)
                turns = (s.slots - AHEAD) // RING - 1
                with act.Fori(0, turns) as i:
                    for slot in range(4, 8):
                        split(s, slot + AHEAD, i)
                        slot_(slot, i)
                at[0] += turns * RING
                for slot in range(4 + 4 * turns, s.slots):
                    splits_to(s.n0 + slot + AHEAD)
                    slot_(slot)

            act.wait_ge(q("mem_in"), 16)
            act_(T8[:], memN[:], ACT.Square).then_inc(q("mem.sq"), 1)
            act.wait_ge(q("consts"), 1)
            root("mem", L[1][:, 0:S], eps2, ".var")
            splits_to(0)
            act.wait_ge(s_par, 16)
            for ft in range(KC):
                act.wait_ge(q("mem0.t"), ft + 1)
                act_(mh[:, ft, :], T8[:, ft, :], ACT.Copy).then_inc(q("mem0.hi"), 1)
            splits_to(1)
            act.wait_ge(q("cond_in"), 16)
            act_(cond[:], cond[:], ACT.Silu).then_inc(q("cact"), 1)
            copies(st["xk0"], lambda k: kT[:, 2 * k:2 * k + 2, :])
            for ft in range(KC):
                act.wait_ge(q("h0.t"), ft + 1)
                act_(x_hi[:, ft, :], T8[:, ft, :], ACT.Copy).then_inc(q("h0.hi"), 1)
            copies(st["xv0"], lambda k: V0[:, :, k * 256:(k + 1) * 256])
            s = st["xbc"]

            def conv_silu(ft, count):
                act.wait_ge(q("ssm.cv"), count)
                act_(XB[:, ft, :], XB[:, ft, :], ACT.Silu).then_inc(q("ssm.conv"), 1)

            def exps():
                act.wait_ge(s_rows, 16)
                act.wait_ge(q("ssm.v"), 1)
                own(act_(tok["mag"][:], tok["v"][:], ACT.Abs))
                act_(tok["e"][:], tok["mag"][:], ACT.Exp, scale=-1.0).then_inc(q("ssm.exp"), 1)
                act_(negA[:], rows[:, 32:48], ACT.Exp).then_inc(q("ssm.exp"), 1)

            def z_silu(slot):
                z = st["z"]
                splits_to(z.n0 + slot + AHEAD)
                result(z, slot)
                if slot == 0:
                    act.wait_ge(s_spill, 32)
                act_(Zs[:, :, slot * 256:(slot + 1) * 256], tiles2(G[(z.j0 + slot) % 2]), ACT.Silu)\
                    .then_inc(s_ev[(z.j0 + slot) % 2], 1)

            splits_to(st["dtf"].n0 + AHEAD)
            act.wait_ge(q("ssm.pad"), 1)
            for slot in range(s.slots):
                splits_to(s.n0 + slot + AHEAD)
                result(s, slot)
                f0 = 2 * xbc_slot(slot)
                act_(CX[:, f0:f0 + 2, 3:3 + S], tiles2(G[(s.j0 + slot) % 2]), ACT.Copy)\
                    .then_inc(s_ev[(s.j0 + slot) % 2], 1)
                if slot:
                    f0 = 2 * xbc_slot(slot - 1)
                    conv_silu(f0, 2 * slot - 1)
                    conv_silu(f0 + 1, 2 * slot)
                if slot == 1:
                    exps()
            conv_silu(6, 11)
            conv_silu(7, 12)
            act.wait_ge(q("ssm.bt"), 1)
            act_(BT[:], L[0][:, 0:S].rearrange("p (g c) -> p g c", g=2), ACT.Copy).then_inc(q("ssm.bts"), 1)
            z_silu(0)
            for b in range(4):
                t, fh = divmod(b, 2)
                act.wait_ge(q("ssm.xtr"), b + 1)
                if b == 0:
                    act.wait_ge(s_spill, 16)
                act_(XsT[:, t, fh * 512:(fh + 1) * 512], T[b % 2][:, :], ACT.Copy).then_inc(q("ssm.xt"), 1)
                if b == 1:
                    z_silu(1)
            z_silu(2)
            z_silu(3)
            act.wait_ge(q("ssm.cs"), 1)
            act_(dend[:], L[1][:, 0:H], ACT.Exp).then_inc(q("ssm.ex"), 1)
            act_(dout[:], L[1][:, H:2 * H], ACT.Exp).then_inc(q("ssm.ex"), 1)
            for u in range(8):
                act.wait_ge(q("ssm.seg"), u + 1)
                if u >= 2:
                    act.wait_ge(q("ssm.ydiag"), u - 1)
                act_(E[u % 2][:], T[u % 2][:, :].rearrange("p (k c) -> p k c", k=4), ACT.Exp).then_inc(q("ssm.e"), 1)
                if u == 3:
                    for g in range(2):
                        act.wait_ge(q("ssm.state"), g + 1)
                        act_(STt[:, g, :], G[g][:, :], ACT.Copy).then_inc(q("ssm.st"), 1)
            row_squares("ssmt", Y, xce[:])

            s = st["q"]
            for slot in range(4):
                splits_to(s.n0 + slot + AHEAD)
                result(s, slot)
                act_(qT[:, 2 * slot:2 * slot + 2, :], tiles2(G[(s.j0 + slot) % 2]), ACT.Copy, scale=0.125)\
                    .then_inc(s_ev[(s.j0 + slot) % 2], 1)
                if slot == 1:
                    features_hi("ssmt", 0, "ssm_w")
            s = st["k"]
            for slot in range(4):
                splits_to(s.n0 + slot + AHEAD)
                result(s, slot)
                for half in range(2):
                    rows_ = slice(half * HD, half * HD + HD)
                    last = act_(kz[half][rows_, 2 * slot:2 * slot + 2, :], tiles2(G[(s.j0 + slot) % 2])[rows_], ACT.Copy)
                last.then_inc(s_ev[(s.j0 + slot) % 2], 1)
            copies(st["v"], lambda k: V[:, :, k * 256:(k + 1) * 256])
            act_(X[:], X[:], ACT.Copy, scale=ALPHA).then_inc(q("wout.ax"), 1)
            attention("fox", H, lambda t: P * (t + 1), 0, lambda u: beside("fox", u, None))
            splits_to(st["wouta"].n0 + 3 + AHEAD)
            row_squares("foxt", AO, T8[:, 0:4, :].rearrange("p a b -> p (a b)"))
            features_hi("foxt", 8, "attn_w")

            def layer_norm(name, s, after, nf, per):
                if name != "wout":
                    act.wait_ge(q("ln1.x"), 1)
                    act_(X[:], X[:], ACT.Copy, scale=ALPHA).then_inc(q(name + ".ax"), 1)
                for g in range(KC // nf):
                    splits_to(s.n0 + g * per + per - 1 + AHEAD)
                for ft in range(KC):
                    act.wait_ge(q(name + ".cent"), ft + 1)
                    act_(T8[:, ft, :], X[:, ft, :], ACT.Square).then_inc(q(name + ".sq8"), 1)
                root(name, L[1][:, 0:S], eps1, ".var")
                for ft in range(KC):
                    act.wait_ge(q(name + ".xn"), ft + 1)
                    after(ft)

            def after1(ft):
                if ft == 0:
                    act.wait_ge(q("ln1.mod"), 1)
                act_(T8[:, ft, :], X[:, ft, :], ACT.Identity, bias=ln_mod[:, 1, ft:ft + 1], scale=ln_mod[:, 0, ft:ft + 1])\
                    .then_inc(q("ln1.t"), 1)
                act.wait_ge(q("ln1.t"), ft + 1)
                act_(x_hi[:, ft, :], T8[:, ft, :], ACT.Copy).then_inc(q("ln1.hi"), 1)

            def after2(ft):
                if ft % 2 == 0:
                    own(act_(X[:, ft, :], X[:, ft, :], ACT.Identity, bias=pc("ln2_b", ft), scale=pc("ln2_g", ft)))
                else:
                    act.wait_ge(q("ln2.odd"), ft // 2 + 1)
                hi_and_squares("ln2", ft, lambda k: ("ffn1", k))

            layer_norm("wout", st["woutb"], after1, 2, 1)
            ffn_in(st["ffin"], None, 512, 2)
            layer_norm("ffout", st["ffout"], after2, 1, 2)

            def xattn(l, before):
                name = f"xa{l}"
                for slot in range(4):
                    splits_to(st[f"xq{l}"].n0 + slot + AHEAD)
                    if slot == 0:
                        root(before, L[0][:, 0:S], eps2)
                attention(name, XH, lambda t: S, 0)
                features_hi(name + "t", 0)
                residual(f"xo{l}", st[f"xo{l}"], lambda ft: ("ffn2", 8 * l + ft), 2, 1)

            ffn_in(st["f1in0"], "ln2", 256, 1)
            residual("f1out0", st["f1out0"], lambda ft: ("mix", ft), 1, 2)
            root("f1out0", L[0][:, 0:S], eps2)
            splits_to(st["pool"].n0 + AHEAD)
            for ft in range(KC):
                act.wait_ge(q("f1out0.lo"), nth("f1out0.lo", ft + 1))
                act_(X[:, ft, :], X[:, ft, :], ACT.Identity, bias=pool_bs[:, ft:ft + 1]).then_inc(q("pmix.x"), 1)
            residual("pool", st["pool"], lambda ft: ("xattn", ft), 2, 0)
            xattn(0, "pool")
            ffn_in(st["f2in0"], "xo0", 256, 1)
            residual("f2out0", st["f2out0"], lambda ft: ("ffn1", 8 + ft), 1, 2)

            ffn_in(st["f1in1"], "f2out0", 256, 1)
            residual("f1out1", st["f1out1"], lambda ft: ("mix", 8 + ft), 1, 2)
            splits_to(st["nq"].n0 + AHEAD)
            root("f1out1", L[0][:, 0:S], eps2)
            root("f1out1", T[0][:, 0:2], eps2, count=2, out=RTs[:])
            for slot in range(1, 4):
                splits_to(st["nq"].n0 + slot + AHEAD)
            def both_halves(s, turn, dst, shift):
                taken(act, s.j0)
                if turn == 1:
                    act.wait_ge(q("nsa.blk"), 1)
                for half in range(2):
                    for to in range(2):
                        d_ = shift * to
                        a_, b_ = slice(half * 64, half * 64 + 64), slice(to * 64, to * 64 + 64)
                        last = act_(dst(to)[b_, half:G_KV:2, 0:S - d_], gu[turn % 2][a_, :, d_:S], ACT.Copy)
                last.then_inc(q("nsa.halves"), 1)

            for b, name in enumerate(("nkc", "nvc")):
                splits_to(st[name].n0 + AHEAD)
                both_halves(st[name], b, lambda to: Z, 1)
                act.wait_ge(q("nsa.blk"), b + 1)
                act_(bk_hi[b][:], bk[:].rearrange("p j g n -> p j (g n)"), ACT.Copy).then_inc(q("nsa.bkh"), 1)
            for b, (name, dst) in enumerate((("nks", ks), ("nkw", kw))):
                splits_to(st[name].n0 + AHEAD)
                both_halves(st[name], 2 + b, lambda to: dst[:, to], 0)
            for name, out in (("nvs", vs), ("nvw", vw)):
                s = st[name]
                splits_to(s.n0 + AHEAD)
                result(s, 0)
                if name == "nvs":
                    act.wait_ge(q("nsa.rt"), 1)
                for t in range(2):
                    last = act_(out[:, t, :], G[s.j0 % 2][:, t * 256:(t + 1) * 256], ACT.Copy, scale=RT[:, t:t + 1])
                last.then_inc(s_ev[s.j0 % 2], 1)
            s = st["ng"]
            splits_to(s.n0 + AHEAD)
            result(s, 0)
            for t in range(2):
                last = act_(gates[:, t, :], G[s.j0 % 2][:, t * 48:(t + 1) * 48], ACT.Sigmoid, scale=RT[:, t:t + 1])
            last.then_inc(s_ev[s.j0 % 2], 1)
            for ft in range(KC):
                act_(x_hi[:, ft, :], memN[:, ft, :], ACT.Copy, scale=pc("mem", 8 + ft)).then_inc(q("mem1.hi"), 1)
            for b, name in enumerate(("cmpk", "cmpv")):
                s = st[name]
                for slot in range(2):
                    splits_to(s.n0 + slot + AHEAD)
                result(s, 1)
                act_(GH[b][0:GB, :], G[s.j0 % 2][0:GB, 0:256], ACT.Gelu_apprx_tanh).then_inc(s_ev[s.j0 % 2], 1)
            splits_to(st["xk1"].n0 + AHEAD)
            act.wait_ge(q("nsa.ht"), 1)
            act_(HG[:], T[0][:, 0:2 * GB].rearrange("p (k n) -> p k n", k=2), ACT.Copy).then_inc(q("nsa.hx"), 1)
            act.wait_ge(q("nsa.ht"), 2)
            for k in range(2):
                last = act_(HX[:, k, :].rearrange("p (g h n) -> p g h n", g=G_KV, h=2),
                            bc(T[1][:, k * GB:(k + 1) * GB].rearrange("p (g n) -> p g n", g=G_KV).unsqueeze(2),
                               [P, G_KV, 2, NCMP]), ACT.Copy)
            last.then_inc(q("nsa.hx"), 1)
            act.wait_ge(q("nsa.kc"), 1)
            for half in range(2):
                rows_ = slice(half * HD, half * HD + HD)
                last = act_(KD[rows_, :, half], T[0][rows_, 0:GB].rearrange("p (g n) -> p g n", g=G_KV), ACT.Copy)
            last.then_inc(q("nsa.ready"), 1)
            take_mem("xk1", 0)
            splits_to(st["xk1"].n0 + 1 + AHEAD)
            for t in range(2):
                act.wait_ge(q("nc.l"), t + 1)
                act_(LC[:, t, :], LC[:, t, :], ACT.Exp).then_inc(q("nc.p"), 1)
            for t in range(2):
                for half in range(2):
                    if t == 0 and half == 0:
                        take_mem("xk1", 1)
                    act.wait_ge(q("nc.pv"), 2 * t + half + 1)
                    act_(AO[:, t, :].rearrange("p (h two d) -> p two h d", two=2, d=HD)[:, half], h8((O, L)[t][half][:, :]),
                         ACT.Copy).then_inc(q("nc.o"), 1)
            attention("ns", H, lambda t: P * (t + 1), 32,
                      lambda u: beside("ns", u, True))
            attention("nw", H, lambda t: P * (t + 1), 64,
                      lambda u: beside("nw", u, True))
            splits_to(st["xv1"].n0 + 3 + AHEAD)
            take_mem("xv1", 3)
            features_hi("nsat", 0)
            residual("no", st["no"], lambda ft: ("xattn", 8 + ft), 2, 1)
            xattn(1, "no")
            ffn_in(st["f2in1"], "xo1", 256, 1)
            residual("f2out1", st["f2out1"], None, 1, 2)
            root("f2out1", L[0][:, 0:S], eps2)

        @block.vector
        def _(dve):
            v = nc.vector
            own = Chain(dve, "dve_own")
            at, mods = [0], [0]

            def modulation_half(k, f):
                w_, load = mod_buffer(k)
                if f == 0:
                    dve.wait_ge(q(f"ada_load{load[0]}"), load[1])
                part = w_[:, f * D:(f + 1) * D]
                last = v.tensor_tensor_reduce(out=part, in0=part, in1=cond[:], scale=1.0, scalar=0.0, op0=ALU.mult,
                                              op1=ALU.add, accum_out=mod[:, 2 * k + f:2 * k + f + 1])
                if f == 1:
                    last.then_inc(q("ada"), 1)

            def modulation():
                for f in range(2):
                    modulation_half(mods[0], f)
                mods[0] += 1

            def gated_update(s, g, nf, per, gate0):
                j = s.j0 + g
                result(s, g * per + per - 1)
                for ft in range(g * nf, g * nf + nf):
                    f = ft - g * nf
                    last = v.scalar_tensor_tensor(X[:, ft, :], G[j % 2][:, f * S:(f + 1) * S],
                                                  mod1[:, gate0 + ft:gate0 + ft + 1], X[:, ft, :], ALU.mult, ALU.add)
                last.then_inc(s_ev[j % 2], 1)

            def modulations_to(count):
                while mods[0] < count:
                    modulation()

            def biased(a_, b_):
                dve.wait_ge(q("ada"), b_ // 2)
                own(v.tensor_tensor(mod[:, a_:b_], mod[:, a_:b_], par[:, COL["b_ada"] + a_:COL["b_ada"] + b_], ALU.add))
                own(v.tensor_scalar(mod1[:, a_:b_], mod[:, a_:b_], 1.0, None, ALU.add))

            def split(s, slot, i=0):
                b = (s.n0 + slot) % RING
                dve.wait_ge(s_hi, s.n0 + slot + 1 + i * RING)
                v.tensor_tensor(w_lo[b][:, 0:s.size], raw[b][:, 0:s.size], w_hi[b][:, 0:s.size].bitcast(F32),
                                ALU.subtract).then_inc(s_lo, 1)

            def splits_to(k):
                while at[0] <= min(k, len(split_order) - 1):
                    split(*split_order[at[0]])
                    at[0] += 1

            def result(s, slot, i=0):
                dve.wait_ge(s_mm, s.n0 + slot + 1 + i * RING)

            def splits_over(s):
                for slot in range(s.slots):
                    splits_to(s.n0 + slot + AHEAD)

            def inverse(name):
                dve.wait_ge(q(name + ".root"), nth(name + ".root", 1))
                own(v.reciprocal(R[:], Rs[:]))

            def row_scale(name, src):
                dve.wait_ge(q(name + ".root"), nth(name + ".root", 1))
                own(v.reciprocal(rtok[:], rtoks[:]))
                for t in range(2):
                    last = v.tensor_scalar(src[:, t, :], src[:, t, :], rtok[:, t:t + 1], None, ALU.mult)
                last.then_inc(q(name + ".y"), 1)

            def features_lo(name, chunk0, gain=None):
                for b in range(4):
                    dve.wait_ge(q(name + ".hi"), nth(name + ".hi", 2 * b + 2))
                    for f in range(2):
                        ft = 2 * b + f
                        v.scalar_tensor_tensor(hid_lo[:, chunk0 + ft, :], T[b % 2][:, f * S:(f + 1) * S],
                                               pc(gain, ft) if gain else 1.0, hid_hi[:, chunk0 + ft, :].bitcast(F32),
                                               ALU.mult, ALU.subtract).then_inc(q(name + ".lo"), 1)
                    dve.wait_ge(q(name + ".lo"), nth(name + ".lo", 2 * b + 2))
                    dve.nop().then_inc(q(name + ".tev"), 1)

            def beside(attention_name, step):
                turn, part = divmod(step, SHARE)
                slots = beside_slots[attention_name]
                if turn < len(slots) and part >= 4:
                    name, slot = slots[turn]
                    t, k = split_order[st[name].n0 + slot + AHEAD]
                    n, each = t.n0 + k, t.size // 4
                    c = slice((part - 4) * each, (part - 3) * each)
                    if part == 4:
                        dve.wait_ge(s_hi, n + 1)
                    last = v.tensor_tensor(w_lo[n % RING][:, c], raw[n % RING][:, c], w_hi[n % RING][:, c].bitcast(F32),
                                           ALU.subtract)
                    if part == 7:
                        last.then_inc(s_lo, 1)
                        at[0] += 1

            def attention(name, heads, hd, keys, masks, base, take, beside_=lambda step: None):
                units = [(h, t) for h in range(heads) for t in range(2)]
                per = 512 // hd
                for step in range(len(units) + 2):
                    if step < len(units):
                        h, t = units[step]
                        nk, col = keys(t), base + t * heads + h
                        dve.wait_ge(q(name + ".qk"), nth(name + ".qk", step + 1))
                        if step >= 2:
                            dve.wait_ge(q(name + ".p"), nth(name + ".p", step - 1))
                        v.tensor_tensor_reduce(out=Lm[step % 2][:, 0:nk], in0=L[step % 2][:, 0:nk], in1=masks(t),
                                               scale=-1.0, scalar=3e38, op0=ALU.add, op1=ALU.min,
                                               accum_out=nmax[:, col:col + 1]).then_inc(q(name + ".l"), 1)
                    if 1 <= step <= len(units):
                        u = step - 1
                        h, t = units[u]
                        nk = keys(t)
                        rows_, nch = min(nk, P), (nk + P - 1) // P
                        dve.wait_ge(q(name + ".tp"), nth(name + ".tp", u + 1))
                        if u >= 2:
                            dve.wait_ge(q(name + ".pv"), nth(name + ".pv", u - 1))
                        v.tensor_copy(PT[u % 2][0:rows_, 0:nch, :],
                                      T[u % 2][0:rows_, 0:nch * P].rearrange("p (c n) -> p c n", c=nch))\
                            .then_inc(q(name + ".pt"), 1)
                    beside_(step)
                    if step >= 3 and (step - 1) % (2 * per) == 0:
                        half = (step - 1) // (2 * per) - 1
                        for t in range(2):
                            dve.wait_ge(q(name + ".pv"), nth(name + ".pv", 2 * per * (half + 1) - 1 + t))
                            cols = slice(base + t * heads + half * per, base + t * heads + (half + 1) * per)
                            own(v.reciprocal(rs[:, 0:per], ssum[:, cols]))
                            take(half, t)
                            dve.wait_ge(q(name + ".o"), nth(name + ".o", 2 * half + t + 1))

            def out_view(half, t):
                return AO[:, t, half * 512:(half + 1) * 512]

            def plain_take(name, per):
                def take(half, t):
                    v.tensor_tensor(out_view(half, t).rearrange("p (h d) -> p h d", h=per),
                                    O[t][:, :].rearrange("p (h d) -> p h d", h=per),
                                    bc(rs[:, 0:per].unsqueeze(2), [P, per, 512 // per]), ALU.mult)\
                        .then_inc(q(name + ".o"), 1)
                return take

            def residual(name, s, nf, per, factor, gain):
                def lo(ft):
                    dve.wait_ge(q(name + ".hi"), nth(name + ".hi", ft + 1))
                    v.scalar_tensor_tensor(x_lo[:, ft, :], X[:, ft, :], pc(*gain(ft)), x_hi[:, ft, :].bitcast(F32),
                                           ALU.mult, ALU.subtract).then_inc(q(name + ".lo"), 1)

                for g in range(KC // nf):
                    j = s.j0 + g
                    if s.name == "pool":
                        if g < 2:
                            dve.wait_ge(q(f"pmix.p{g}"), 1)
                        src = (wa, wb)[g % 2][:, 2 * g:2 * g + 2, :]
                    else:
                        splits_to(s.n0 + g * per + per - 1 + AHEAD)
                        result(s, g * per + per - 1)
                        src = G[j % 2][:, 0:nf * S].rearrange("p (f c) -> p f c", f=nf)
                    for f in range(nf):
                        ft = g * nf + f
                        last = v.scalar_tensor_tensor(X[:, ft, :], src[:, f, :],
                                                      factor if isinstance(factor, float) else factor(ft),
                                                      X[:, ft, :], ALU.mult, ALU.add)
                    last.then_inc(q("pmix.u") if s.name == "pool" else s_ev[j % 2], 1)
                    if gain and g:
                        for f in range(nf):
                            lo((g - 1) * nf + f)
                if gain:
                    for f in range(nf):
                        lo(KC - nf + f)

            def ffn_in(s, before, width, chunks):
                def lo(slot, i=0):
                    dve.wait_ge(q(s.name + ".hi"), nth(s.name + ".hi", slot + 1 + i * RING))
                    c0 = chunks * slot + i * (chunks * RING)
                    v.tensor_tensor(hid_lo[:, bass.ds(c0, chunks), :],
                                    hb[slot % 2][:, 0:width].rearrange("p (k c) -> p k c", k=chunks),
                                    hid_hi[:, bass.ds(c0, chunks), :].bitcast(F32), ALU.subtract)\
                        .then_inc(q(s.name + ".lo"), 1)

                def slot_(slot, split_ahead, i=0):
                    j = s.j0 + slot
                    if chunks == 1:
                        result(s, slot, i)
                        v.tensor_tensor(gu[slot % 2][:], tiles2(G[j % 2]), bc(R[:].unsqueeze(1), [P, 2, S]), ALU.mult)\
                            .then_inc(s_ev[j % 2], 1)
                        split_ahead()
                    if slot:
                        lo(slot - 1, i)
                    if chunks == 1:
                        dve.wait_ge(q(s.name + ".sg"), nth(s.name + ".sg", slot + 1 + i * RING))
                        taken(dve, j, i)
                        other = gu[slot % 2][:, 1, :]
                    else:
                        taken(dve, j, i)
                        other = sg[slot % 2][:, 0:width]
                    v.tensor_tensor(hb[slot % 2][:, 0:width], sg[slot % 2][:, 0:width], other, ALU.mult)\
                        .then_inc(q(s.name + ".h"), 1)
                    if chunks == 2:
                        split_ahead()

                for slot in range(4):
                    if slot == 0 and before:
                        inverse(before)
                    slot_(slot, lambda: splits_to(s.n0 + slot + AHEAD))
                turns = (s.slots - AHEAD) // RING - 1
                with dve.Fori(0, turns) as i:
                    for slot in range(4, 8):
                        slot_(slot, lambda: split(s, slot + AHEAD, i), i)
                at[0] += turns * RING
                for slot in range(4 + 4 * turns, s.slots):
                    slot_(slot, lambda: splits_to(s.n0 + slot + AHEAD))
                lo(s.slots - 1)

            dve.wait_ge(q("consts"), 1)
            own(v.reciprocal(icnt[:], icnt[:]))
            dve.wait_ge(q("mem.sq"), 1)
            for half in (4, 2):
                own(v.tensor_tensor(T8[:, 0:half, :], T8[:, 0:half, :], T8[:, half:2 * half, :], ALU.add))
            v.tensor_tensor(T8[:, 0, :], T8[:, 0, :], T8[:, 1, :], ALU.add).then_inc(q("mem.acc"), 1)
            dve.wait_ge(s_par, 16)
            dve.wait_ge(q("mem.root"), 1)
            own(v.reciprocal(R[:], Rs[:]))
            for ft in range(KC):
                v.scalar_tensor_tensor(T8[:, ft, :], memN[:, ft, :], pc("mem", ft), R[:], ALU.mult, ALU.mult)\
                    .then_inc(q("mem0.t"), 1)
            splits_to(0)
            for ft in range(KC):
                dve.wait_ge(q("mem0.hi"), ft + 1)
                v.tensor_tensor(ml[:, ft, :], T8[:, ft, :], mh[:, ft, :].bitcast(F32), ALU.subtract)\
                    .then_inc(q("mem0.lo"), 1)
            splits_to(1)
            dve.wait_ge(q("cact"), 1)
            dve.wait_ge(q("mem0.t"), KC)
            own(v.tensor_tensor(memN[:], memN[:], bc(R[:].unsqueeze(1), [P, KC, S]), ALU.mult))
            own(v.tensor_tensor(pool_bs[:], par[:, COL["pool_b"]:COL["pool_b"] + 8],
                                par[:, COL["pool_s"]:COL["pool_s"] + 8], ALU.mult))
            for slot in range(4):
                modulations_to(2 * slot + 2)
                splits_to(slot + AHEAD)
            biased(0, 16)
            dve.wait_ge(s_in, 16)
            for ft in range(KC + 1):
                if ft < KC:
                    v.tensor_scalar(T8[:, ft, :], X[:, ft, :], mod1[:, 8 + ft:9 + ft], mod[:, ft:ft + 1],
                                    ALU.mult, ALU.add).then_inc(q("h0.t"), 1)
                if ft:
                    dve.wait_ge(q("h0.hi"), ft)
                    v.tensor_tensor(x_lo[:, ft - 1, :], T8[:, ft - 1, :], x_hi[:, ft - 1, :].bitcast(F32),
                                    ALU.subtract).then_inc(q("h0.lo"), 1)
            splits_over(st["xv0"])

            s = st["dtf"]
            splits_to(s.n0 + AHEAD)
            result(s, 0)
            t32 = lambda c0: bc(rows[:, c0:c0 + 32].unsqueeze(1), [P, 2, 32])
            dve.wait_ge(s_rows, 16)
            v.tensor_tensor(tok["v"][:], G[s.j0 % 2][:, 0:64].rearrange("p (t c) -> p t c", t=2), t32(0), ALU.add)\
                .then_inc(s_ev[s.j0 % 2], 1)
            taken(dve, s.j0)
            v.tensor_scalar(tok["v"][:, :, 16:32], tok["v"][:, :, 16:32], -1.0, None, ALU.mult).then_inc(q("ssm.v"), 1)
            def steps_and_gates():
                dve.wait_ge(q("ssm.exp"), 2)
                own(v.tensor_scalar(tok["den"][:], tok["e"][:], 2.0, None, ALU.add))
                own(v.reciprocal(tok["y"][:], tok["den"][:]))
                own(v.tensor_tensor(tok["y"][:], tok["y"][:], tok["e"][:], ALU.mult))
                own(v.tensor_tensor(tok["y2"][:], tok["y"][:], tok["y"][:], ALU.mult))
                own(v.tensor_scalar(tok["poly"][:], tok["y2"][:], 2.0 / 17, 2.0 / 15, ALU.mult, ALU.add))
                for k in (13, 11, 9, 7, 5, 3, 1):
                    own(v.tensor_tensor(tok["poly"][:], tok["poly"][:], tok["y2"][:], ALU.mult))
                    own(v.tensor_scalar(tok["poly"][:], tok["poly"][:], 2.0 / k, None, ALU.add))
                own(v.tensor_tensor(tok["poly"][:], tok["poly"][:], tok["y"][:], ALU.mult))
                own(v.scalar_tensor_tensor(tok["sp"][:], tok["v"][:], 0.0, tok["poly"][:], ALU.max, ALU.add))
                own(v.tensor_copy(dt_t[:], tok["sp"][:, :, 0:16]))
                own(v.tensor_scalar(lf[:], tok["sp"][:, :, 16:32], -1.0, None, ALU.mult))
                own(v.tensor_scalar(negA[:], negA[:], -1.0, None, ALU.mult))
                v.tensor_tensor(a_t[:], dt_t[:], bc(negA[:].unsqueeze(1), [P, 2, H]), ALU.mult).then_inc(q("ssm.a"), 1)

            s = st["xbc"]
            for slot in range(s.slots):
                splits_to(s.n0 + slot + AHEAD)
                taken(dve, s.j0 + slot)
                for ft in (2 * xbc_slot(slot), 2 * xbc_slot(slot) + 1):
                    own(v.tensor_scalar(XB[:, ft, :], CX[:, ft, 3:3 + S], pc("conv_w", 36 + ft), pc("conv_b", ft),
                                        ALU.mult, ALU.add))
                    for k in (2, 1, 0):
                        last = v.scalar_tensor_tensor(XB[:, ft, :], CX[:, ft, k:k + S], pc("conv_w", 12 * k + ft),
                                                      XB[:, ft, :], ALU.mult, ALU.add)
                        if k:
                            own(last)
                    last.then_inc(q("ssm.cv"), 1)
                if slot == 1:
                    steps_and_gates()

            heads8 = lambda ap: bc(ap.unsqueeze(2), [P, 8, HD])
            dve.wait_ge(q("ssm.cb"), 1)
            v.tensor_tensor(CB[:], O[0][:, :].rearrange("p (k c) -> p k c", k=4), bc(U[:].unsqueeze(1), [P, 4, P]),
                            ALU.mult).then_inc(q("ssm.cbm"), 1)
            for b in range(4):
                t, fh = divmod(b, 2)
                splits_to(st["z"].n0 + b + AHEAD)
                dve.wait_ge(q("ssm.xt"), b + 1)
                own(v.tensor_tensor(h8(xc[:, t, fh * 512:(fh + 1) * 512]), h8(XsT[:, t, fh * 512:(fh + 1) * 512]),
                                    heads8(dt_t[:, t, 8 * fh:8 * fh + 8]), ALU.mult))
            dve.wait_ge(q("ssm.ex"), 2)
            v.tensor_tensor(xce[:].rearrange("p (h d) -> p h d", h=H), xc[:, 0, :].rearrange("p (h d) -> p h d", h=H),
                            bc(dend[:].unsqueeze(2), [P, H, HD]), ALU.mult).then_inc(q("ssm.xce"), 1)
            dve.wait_ge(q("ssm.cbm"), 1)
            for u in range(9):
                if u < 8:
                    dve.wait_ge(q("ssm.e"), u + 1)
                    v.tensor_tensor(E[u % 2][:], E[u % 2][:], bc(CB[:, u // 2, :].unsqueeze(1), [P, 4, P]), ALU.mult)\
                        .then_inc(q("ssm.sc"), 1)
                if u and u % 2 == 0:
                    c, g = divmod(u // 2 - 1, 2)
                    cols = slice(g * 512, (g + 1) * 512)
                    dve.wait_ge(q("ssm.ydiag"), u)
                    if u == 2:
                        dve.wait_ge(q("ssm.dx"), 1)
                    v.tensor_tensor(Y[:, c, cols], O[g][:, :], Y[:, c, cols], ALU.add).then_inc(q("ssm.yo"), 1)
                    if c == 1:
                        dve.wait_ge(q("ssm.off"), g + 1)
                        tmp = T8[:, 0:2, :].rearrange("p a b -> p (a b)")
                        own(v.tensor_tensor(h8(tmp), h8(L[g][:, :]), heads8(dout[:, 8 * g:8 * g + 8]), ALU.mult))
                        dve.wait_ge(q("ssm.yo"), u // 2)
                        own(v.tensor_tensor(Y[:, c, cols], Y[:, c, cols], tmp, ALU.add))
            dve.wait_ge(q("ssm.yo"), 4)
            v.tensor_tensor(Y[:], Y[:], Zs[:], ALU.mult).then_inc(q("ssmt.in"), 1)
            row_scale("ssmt", Y)

            for name in "qkv":
                for slot in range(4):
                    splits_to(st[name].n0 + slot + AHEAD)
                    if mods[0] < 18:
                        modulation()
                    if name == "q" and slot == 1:
                        features_lo("ssmt", 0, "ssm_w")
            causal = lambda t: mask[:, P:2 * P] if t == 0 else mask[:, :]
            biased(16, 24)
            dve.wait_ge(q("wout.ax"), 1)

            def beside_fox(step):
                slot, part = divmod(step, SHARE)
                if part == 0 and 1 <= slot <= 3:
                    gated_update(st["wouta"], slot - 1, 2, 1, 16)
                if part in (1, 2, 3) and slot < 4:
                    modulation_half(18 + (3 * slot + part - 1) // 2, (3 * slot + part - 1) % 2)
                beside("fox", step)

            attention("fox", H, HD, lambda t: P * (t + 1), causal, 0, plain_take("fox", 8), beside_fox)
            mods[0] = MOD_SLOTS
            dve.wait_ge(q("fox.o"), nth("fox.o", 4))
            dve.nop().then_inc(q("foxt.in"), 1)
            splits_to(st["wouta"].n0 + 3 + AHEAD)
            gated_update(st["wouta"], 3, 2, 1, 16)
            row_scale("foxt", AO)
            features_lo("foxt", 8, "attn_w")

            def layer_norm(name, s, gate0, nf, per):
                if name != "wout":
                    dve.wait_ge(q(name + ".ax"), 1)
                for g in range(KC // nf):
                    splits_to(s.n0 + g * per + per - 1 + AHEAD)
                    gated_update(s, g, nf, per, gate0)
                dve.wait_ge(q(name + ".mean"), nth(name + ".mean", 1))
                for ft in range(KC):
                    v.tensor_tensor(X[:, ft, :], X[:, ft, :], L[0][:, 0:S], ALU.subtract).then_inc(q(name + ".cent"), 1)
                dve.wait_ge(q(name + ".cent"), KC)
                inverse(name)

            def normalised(name, ft):
                v.tensor_tensor(X[:, ft, :], X[:, ft, :], R[:], ALU.mult).then_inc(q(name + ".xn"), 1)

            biased(24, 40)
            own(v.tensor_tensor(ln_mod[:, 0, :], par[:, COL["ln1_g"]:COL["ln1_g"] + 8], mod1[:, 32:40], ALU.mult))
            own(v.tensor_tensor(ln_mod[:, 1, :], par[:, COL["ln1_b"]:COL["ln1_b"] + 8], mod1[:, 32:40], ALU.mult))
            v.tensor_tensor(ln_mod[:, 1, :], ln_mod[:, 1, :], mod[:, 24:32], ALU.add).then_inc(q("ln1.mod"), 1)
            layer_norm("wout", st["woutb"], 16, 2, 1)
            for ft in range(KC):
                normalised("wout", ft)
            for ft in range(KC):
                dve.wait_ge(q("ln1.hi"), nth("ln1.hi", ft + 1))
                v.tensor_tensor(x_lo[:, ft, :], T8[:, ft, :], x_hi[:, ft, :].bitcast(F32), ALU.subtract)\
                    .then_inc(q("ln1.lo"), 1)
            for ft in range(KC):
                last = v.tensor_scalar(X[:, ft, :], X[:, ft, :], pc("ln1_g", ft), pc("ln1_b", ft), ALU.mult, ALU.add)
            last.then_inc(q("ln1.x"), 1)
            ffn_in(st["ffin"], None, 512, 2)
            biased(40, 48)
            layer_norm("ffout", st["ffout"], 40, 1, 2)
            for ft in range(KC):
                normalised("ffout", ft)
            for ft in range(0, KC, 2):
                dve.wait_ge(q("ffout.xn"), ft + 2)
                v.tensor_scalar(X[:, ft + 1, :], X[:, ft + 1, :], pc("ln2_g", ft + 1), pc("ln2_b", ft + 1),
                                ALU.mult, ALU.add).then_inc(q("ln2.odd"), 1)
            for ft in range(KC):
                dve.wait_ge(q("ln2.hi"), nth("ln2.hi", ft + 1))
                v.scalar_tensor_tensor(x_lo[:, ft, :], X[:, ft, :], pc("ffn1", ft), x_hi[:, ft, :].bitcast(F32),
                                       ALU.mult, ALU.subtract).then_inc(q("ln2.lo"), 1)

            def scaled_queries(s, scale, before):
                for slot in range(4):
                    j = s.j0 + slot
                    splits_to(s.n0 + slot + AHEAD)
                    if slot == 0:
                        inverse(before)
                    result(s, slot)
                    v.scalar_tensor_tensor(qT[:, 2 * slot:2 * slot + 2, :], tiles2(G[j % 2]), scale,
                                           bc(R[:].unsqueeze(1), [P, 2, S]), ALU.mult, ALU.mult).then_inc(s_ev[j % 2], 1)

            def xattn(l, before):
                name = f"xa{l}"
                scaled_queries(st[f"xq{l}"], 0.0625, before)
                attention(name, XH, 256, lambda t: S, lambda t: bc(zero[:], [P, S]), 0, plain_take(name, 2))
                dve.wait_ge(q(name + ".o"), nth(name + ".o", 4))
                dve.nop().then_inc(q(name + "t.y"), 1)
                features_lo(name + "t", 0)
                residual(f"xo{l}", st[f"xo{l}"], 2, 1, 1.0, lambda ft: ("ffn2", 8 * l + ft))

            ffn_in(st["f1in0"], "ln2", 256, 1)
            residual("f1out0", st["f1out0"], 1, 2, 0.5, lambda ft: ("mix", ft))
            inverse("f1out0")
            splits_to(st["pool"].n0 + AHEAD)
            for g in range(4):
                if g < 3:
                    dve.wait_ge(q("pmix.mm"), g + 1)
                else:
                    result(st["pool"], 0)
                v.tensor_tensor(T8[:, 2 * g:2 * g + 2, :], tiles2(pool_bank[g]), bc(R[:].unsqueeze(1), [P, 2, S]),
                                ALU.mult).then_inc(q("pmix.h"), 1)
            dve.wait_ge(q("pmix.h"), 4)
            window_sums(own, v, 4, KC, (wa, wb, wa, wb))
            window_means(own, v, 2)
            window_means(own, v, 3)
            dve.wait_ge(q("pmix.x"), KC)
            residual("pool", st["pool"], 2, 0, lambda ft: pc("pool_s", ft), lambda ft: ("xattn", ft))
            xattn(0, "pool")
            ffn_in(st["f2in0"], "xo0", 256, 1)
            residual("f2out0", st["f2out0"], 1, 2, 0.5, lambda ft: ("ffn1", 8 + ft))

            ffn_in(st["f1in1"], "f2out0", 256, 1)
            residual("f1out1", st["f1out1"], 1, 2, 0.5, lambda ft: ("mix", 8 + ft))
            scaled_queries(st["nq"], 0.125, "f1out1")
            dve.wait_ge(q("f1out1.root"), nth("f1out1.root", 2))
            v.reciprocal(RT[:], RTs[:]).then_inc(q("nsa.rt"), 1)

            def scaled_keys(s, turn):
                if turn >= 2:
                    dve.wait_ge(q("nsa.halves"), turn - 1)
                result(s, 0)
                v.tensor_tensor(gu[turn % 2][:], tiles2(G[s.j0 % 2]), bc(R[:].unsqueeze(1), [P, 2, S]), ALU.mult)\
                    .then_inc(s_ev[s.j0 % 2], 1)

            for b, name in enumerate(("nkc", "nvc")):
                s = st[name]
                splits_to(s.n0 + AHEAD)
                scaled_keys(s, b)
                dve.wait_ge(q("nsa.halves"), b + 1)
                Zr = Z[:, :, :].rearrange("p g (n s) -> p s g n", s=16)
                pos = COL["pos_k" if b == 0 else "pos_v"]
                for hj in range(2):
                    last = v.tensor_tensor(bk[:, 8 * hj:8 * hj + 8], Zr[:, 0:16:2, :, hj:hj + NCMP],
                                           bc(par[:, pos + 8 * hj:pos + 8 * hj + 8].unsqueeze(2).unsqueeze(3),
                                              [P, 8, G_KV, NCMP]), ALU.add)
                last.then_inc(q("nsa.blk"), 1)
                dve.wait_ge(q("nsa.bkh"), b + 1)
                v.tensor_tensor(bk_lo[b][:], bk[:].rearrange("p j g n -> p j (g n)"), bk_hi[b][:].bitcast(F32),
                                ALU.subtract).then_inc(q("nsa.bk"), 1)
            for b, name in enumerate(("nks", "nkw")):
                splits_to(st[name].n0 + AHEAD)
                scaled_keys(st[name], 2 + b)
            for name in ("nvs", "nvw", "ng"):
                splits_over(st[name])
            for ft in range(KC):
                dve.wait_ge(q("mem1.hi"), ft + 1)
                v.scalar_tensor_tensor(x_lo[:, ft, :], memN[:, ft, :], pc("mem", 8 + ft), x_hi[:, ft, :].bitcast(F32),
                                       ALU.mult, ALU.subtract).then_inc(q("mem1.lo"), 1)
            for name in ("cmpk", "cmpv"):
                splits_over(st[name])
            splits_to(st["xk1"].n0 + AHEAD)

            def gated_take(name, branch):
                def take(half, t):
                    g_ = gates[:, t, 24 * half + branch:24 * half + 24:3]
                    own(v.tensor_tensor(rs[:], rs[:], g_, ALU.mult))
                    o3 = h8(O[t][:, :])
                    count = 4 * (branch - 1) + 2 * half + t
                    if count >= 2:
                        dve.wait_ge(q("nsa.sum"), count - 1)
                    v.tensor_tensor(h8(Ot[t][:]), o3, heads8(rs[:]), ALU.mult).then_inc(q(name + ".o"), 1)
                return take

            dve.wait_ge(q("nsa.kc"), 2)
            v.tensor_tensor(h8(VB[0:HB, :]), bc(T[1][0:HB, 0:HD].unsqueeze(1), [HB, 8, HD]),
                            bc(own_rows[0:HB, :].unsqueeze(2), [HB, 8, HD]), ALU.mult)\
                .then_inc(q("nsa.vc"), 1)
            heads = lambda ap: ap.rearrange("p (h n) -> p h n", h=H)
            each = lambda ap: bc(ap.unsqueeze(2), [P, H, NCMP])
            for t in range(2):
                dve.wait_ge(q("nc.qk"), t + 1)
                own(v.tensor_tensor(heads(LC[:, t, :]), heads(L[t][:, 0:H * NCMP]),
                                    bc(cmask[:, t, :].unsqueeze(1), [P, H, NCMP]), ALU.add))
                own(v.tensor_reduce(out=wc[:, t, :], in_=heads(LC[:, t, :]), op=ALU.max, axis=AX.X))
                v.tensor_tensor(heads(LC[:, t, :]), heads(LC[:, t, :]), each(wc[:, t, :]), ALU.subtract)\
                    .then_inc(q("nc.l"), 1)
            splits_to(st["xk1"].n0 + 1 + AHEAD)
            for t in range(2):
                dve.wait_ge(q("nc.p"), t + 1)
                own(v.tensor_reduce(out=wc[:, t, :], in_=heads(LC[:, t, :]), op=ALU.add, axis=AX.X))
                own(v.reciprocal(wc[:, t, :], wc[:, t, :]))
                own(v.tensor_tensor(wc[:, t, :].rearrange("p (two h) -> p two h", two=2),
                                    wc[:, t, :].rearrange("p (two h) -> p two h", two=2),
                                    gates[:, t, :].rearrange("p (h two b) -> p b two h", two=2, b=3)[:, 0], ALU.mult))
                if t == 0:
                    own(v.tensor_scalar(wc[:, t, :], wc[:, t, :], vis[:], None, ALU.mult))
                v.tensor_tensor(heads(LC[:, t, :]), heads(LC[:, t, :]), each(wc[:, t, :]), ALU.mult).then_inc(q("nc.w"), 1)
            for t in range(2):
                dve.wait_ge(q("nc.tp"), t + 1)
                v.tensor_copy(PT[t][0:HB, :, :], T[t][0:HB, 0:2 * P].rearrange("p (c n) -> p c n", c=2)).then_inc(q("nc.pt"), 1)
            dve.wait_ge(q("nc.o"), 4)
            attention("ns", H, HD, lambda t: P * (t + 1), causal, 32, gated_take("ns", 1),
                      lambda step: beside("ns", step))
            attention("nw", H, HD, lambda t: P * (t + 1), causal, 64, gated_take("nw", 2),
                      lambda step: beside("nw", step))
            dve.wait_ge(q("nsa.sum"), 8)
            dve.nop().then_inc(q("nsat.y"), 1)
            splits_to(st["xv1"].n0 + 3 + AHEAD)
            features_lo("nsat", 0)
            residual("no", st["no"], 2, 1, 1.0, lambda ft: ("xattn", 8 + ft))
            xattn(1, "no")
            ffn_in(st["f2in1"], "xo1", 256, 1)
            residual("f2out1", st["f2out1"], 1, 2, 0.5, None)
            inverse("f2out1")
            for ft in range(KC):
                v.scalar_tensor_tensor(T8[:, ft, :], X[:, ft, :], pc("final", ft), R[:], ALU.mult, ALU.mult)\
                    .then_inc(q("final"), 1)

        @block.gpsimd
        def _(pool):
            g_ = nc.gpsimd
            own = Chain(pool, "pool_own")

            def select(out, pattern, cm, op, fill, base=0):
                own(g_.affine_select(out=out, in_=out, compare_op=op, fill=fill, base=base, pattern=pattern,
                                     channel_multiplier=cm))

            def zeros(name, even, odd):
                if name == "fox":
                    pool.wait_ge(q("ssmt.tr"), 4)
                else:
                    pool.wait_ge(s_mm, st["f1out1"].n0 + 16)
                    pool.wait_ge(q("f1out1.acc"), nth("f1out1.acc", KC))
                own(g_.memset(even[HD:P], 0.0))
                own(g_.memset(odd[0:HD], 0.0))
                g_.nop().then_inc(q(name + ".zero"), 1)

            def load_modulation(k):
                w_, load = mod_buffer(k)
                if MOD_FIRST > k >= 4:
                    pool.wait_ge(q("ada"), k - 3)
                if k >= MOD_FIRST + 2:
                    pool.wait_ge(q("ada"), k - 1)
                g_.dma_start(w_[:], w["ada"][k]).then_inc(q(f"ada_load{load[0]}"), 16)

            for t_, x_ in ((ones_d, 1.0 / D), (ones, 1.0), (zero, 0.0), (eps1, EPS1), (eps2, EPS2), (ident, 0.0),
                           (U, 1.0), (SG, 1.0), (mask, 0.0), (vis, 1.0), (own_rows, 1.0), (cmask, 0.0), (KD, 0.0)):
                last = g_.memset(t_[:], x_)
            own(last)
            select(ident[:], [[-1, P]], 1, ALU.not_equal, 1.0)
            select(U[:], [[1, P]], -1, ALU.is_ge, 0.0)
            select(SG[:, P:2 * P], [[-1, P]], 1, ALU.is_gt, 0.0)
            select(mask[:, P:2 * P], [[-1, P]], 1, ALU.is_ge, NEG)
            select(vis[:], [[0, 1]], 1, ALU.is_ge, 0.0, base=-31)
            for t in range(2):
                select(cmask[:, t, :], [[-16, NCMP]], 1, ALU.is_ge, NEG, base=P * t - 31)
            select(own_rows[:], [[-NCMP, 8]], 1, ALU.is_ge, 0.0)
            select(own_rows[:], [[NCMP, 8]], -1, ALU.is_ge, 0.0, base=NCMP - 1)
            own(g_.iota(icnt[:, 3, :], [[1, 16]], base=1, channel_multiplier=0, allow_small_or_imprecise_dtypes=True))
            for g in range(4):
                last = g_.tensor_scalar(icnt[:, g, :], icnt[:, 3, :], float(2 << g), None, ALU.min)
            own(last)
            g_.nop().then_inc(q("consts"), 1)
            for k in range(MOD_FIRST):
                pool.wait_ge(s_load[min(k, 2) + 1], 16)
                load_modulation(k)
            pool.wait_ge(q("ada"), MOD_FIRST)
            own(g_.memset(CX[:, :, 0:3], 0.0))
            g_.nop().then_inc(q("ssm.pad"), 1)

            pool.wait_ge(q("ssm.a"), 1)
            for u in range(8):
                c, g, hq = u // 4, u // 2 % 2, u % 2
                if u >= 2:
                    pool.wait_ge(q("ssm.seg"), u - 1)
                g_.tensor_tensor(AS[u % 2][:], bc(SG[:, P:2 * P].unsqueeze(1), [P, 4, P]),
                                 bc(a_t[:, c, 8 * g + 4 * hq:8 * g + 4 * hq + 4].unsqueeze(2), [P, 4, P]), ALU.mult)\
                    .then_inc(q("ssm.as"), 1)
                if u == 1:
                    pool.wait_ge(q("ssm.xt"), 4)
                    pool.wait_ge(s_rows, 16)
                    for t in range(2):
                        last = g_.tensor_tensor(Y[:, t, :].rearrange("p (h d) -> p h d", h=H),
                                                XsT[:, t, :].rearrange("p (h d) -> p h d", h=H),
                                                bc(rows[:, 48:64].unsqueeze(2), [P, H, HD]), ALU.mult)
                    last.then_inc(q("ssm.dx"), 1)
            def scaled_masks(h):
                g_.tensor_scalar(RB[h % 2][:, 0:P], SG[:, P:2 * P], lf[:, 0, h:h + 1], None, ALU.mult)
                g_.tensor_scalar(RB[h % 2][:, P:3 * P], SG[:, :], lf[:, 1, h:h + 1], None, ALU.mult)\
                    .then_inc(q("fox.rb"), 1)

            pool.wait_ge(q("ssmt.in"), 1)
            for k in range(MOD_FIRST, 20):
                if k == MOD_FIRST + 2:
                    zeros("fox", kz[0], kz[1])
                if k == 18:
                    scaled_masks(0)
                    scaled_masks(1)
                load_modulation(k)
            for h in range(2, H):
                if h in (4, 6, 8, 11):
                    load_modulation({4: 20, 6: 21, 8: 22, 11: 23}[h])
                pool.wait_ge(q("fox.qk"), nth("fox.qk", 2 * h - 2))
                scaled_masks(h)

            def sums(name, src, event, count=lambda k: k + 1):
                for ft in range(KC):
                    event(ft)
                    if ft == 0:
                        ins = g_.tensor_copy(acc[:], src[:, 0, :])
                    else:
                        pool.wait_ge(q(name + ".acc"), nth(name + ".acc", ft))
                        ins = g_.tensor_tensor(acc[:], acc[:], src[:, ft, :], ALU.add)
                    ins.then_inc(q(name + ".acc"), 1)

            def squares(name):
                sums(name, T8, lambda ft: pool.wait_ge(q(name + ".sq"), nth(name + ".sq", ft + 1)))

            sums("wout", X, lambda ft: taken(pool, st["woutb"].j0 + ft // 2))
            sums("ffout", X, lambda ft: taken(pool, st["ffout"].j0 + ft))
            squares("ln2")
            squares("f1out0")
            pool.wait_ge(q("f1out0.acc"), nth("f1out0.acc", KC))
            pool.wait_ge(q("pmix.h"), 2)
            window_sums(own, g_, 0, 4, (wa, wb))
            for g in range(2):
                window_means(own, g_, g)
                g_.nop().then_inc(q(f"pmix.p{g}"), 1)
            squares("pool")
            squares("xo0")
            squares("f2out0")
            squares("f1out1")
            zeros("nsa", ks[:, 0], ks[:, 1])
            zeros("nsa", kw[:, 0], kw[:, 1])
            pool.wait_ge(q("nc.o"), 4)
            for name in ("ns", "nw"):
                for k in range(4):
                    half, t = divmod(k, 2)
                    pool.wait_ge(q(name + ".o"), nth(name + ".o", k + 1))
                    view = AO[:, t, half * 512:(half + 1) * 512]
                    g_.tensor_tensor(view, view, Ot[t][:], ALU.add).then_inc(q("nsa.sum"), 1)
                    pool.wait_ge(q("nsa.sum"), 4 * (name == "nw") + k + 1)
            squares("no")
            squares("xo1")
            squares("f2out1")


def _cols(a):
    import numpy as np
    return np.ascontiguousarray(np.reshape(a, (-1, P)).T)


def _slots(a, cols):
    import numpy as np
    k, n = a.shape
    a = np.reshape(a, (k // P, P, n // cols, cols))
    return np.ascontiguousarray(np.transpose(a, (2, 1, 0, 3)).reshape(n // cols, P, -1))


def _rows(a):
    import numpy as np
    a = np.reshape(a.T, (a.shape[1] // (2 * P), 2, P, D))
    return np.ascontiguousarray(np.transpose(a, (0, 2, 1, 3)).reshape(-1, P, 2 * D))


def _tiles(a, parts):
    import numpy as np
    k, n = a.shape
    a = np.reshape(a, (parts, k // P // parts, P, n // P, P))
    return np.ascontiguousarray(np.transpose(a, (3, 0, 2, 1, 4)).reshape(n // P * parts, P, -1))


def _pairs(a):
    import numpy as np
    k, n = a.shape
    a = np.reshape(a, (k // P, P, 2, n // 2 // P, P))
    return np.ascontiguousarray(np.transpose(a, (3, 1, 0, 2, 4)).reshape(n // 2 // P, P, -1))


def _features(a):
    import numpy as np
    return np.ascontiguousarray(np.transpose(np.reshape(a, (S, KC, P)), (2, 1, 0)))


def lay_out(x):
    import numpy as np
    g = lambda n: np.asarray(x[n])
    out = {}
    ada, w_in = g("w_ada")[0], g("w_in")[0]
    out["ada"] = _rows(ada)
    out["z"], out["xbc"] = _slots(w_in[:, :1024], 256), _slots(w_in[:, 1024:2560], 256)[[4, 5, 0, 1, 2, 3]]
    out["dtf"] = _slots(np.concatenate([w_in[:, 2560:2576], w_in[:, 5648:5664]], 1), 32)
    for k, name in enumerate("qkv"):
        out[name] = _slots(w_in[:, 2576 + 1024 * k:3600 + 1024 * k], 256)
    out["wouta"], out["woutb"] = _slots(g("w_out")[0][:D], 256), _slots(g("w_out")[0][D:], 256)
    out["ffin"], out["ffout"] = _slots(g("w_ff_in")[0], 256), _tiles(g("w_ff_out")[0], 2)
    for l in range(2):
        for f in (1, 2):
            out[f"f{f}in{l}"] = _pairs(g(f"ffn{f}_w_in_2")[l])
            out[f"f{f}out{l}"] = _tiles(g(f"ffn{f}_w_out_2")[l], 2)
        kv = g("xattn_w_kv_2")[l]
        out[f"xk{l}"], out[f"xv{l}"] = _slots(kv[:, :1024], 256), _slots(kv[:, 1024:], 256)
        out[f"xq{l}"], out[f"xo{l}"] = _slots(g("xattn_w_q_2")[l], 256), _slots(g("xattn_w_o_2")[l], 256)
    pool = np.reshape(g("pool_w_2")[0], (4, 2, P, 256))
    out["pool"] = np.ascontiguousarray(np.transpose(pool, (2, 0, 1, 3)).reshape(1, P, -1))
    nsa = g("nsa_w_in_2")[0]
    out["nq"] = _slots(nsa[:, :1024], 256)
    for k, name in enumerate(("nkc", "nvc", "nks", "nvs", "nkw", "nvw")):
        out[name] = _slots(nsa[:, 1024 + 256 * k:1280 + 256 * k], 256)
    out["ng"] = _slots(nsa[:, 2560:], 48)
    for k, name in enumerate(("cmpk", "cmpv")):
        w1 = g("nsa_cmp_w1_2")[0, k]
        out[name] = np.concatenate([_slots(w1[:D], 256), _slots(w1[D:], 256)])
    out["no"] = _slots(g("nsa_w_o_2")[0], 256)

    conv = g("conv_w")[0]
    w2 = np.reshape(g("nsa_cmp_w2_2")[0], (2, 2, P, HD))
    w2k = np.transpose(w2[0], (1, 0, 2))
    pos = np.reshape(g("nsa_cmp_pos_2")[0], (2, CMP_J, P))
    parts = {"b_ada": _cols(g("b_ada")),
             "conv_w": np.concatenate([_cols(conv[k]) for k in range(4)], 1), "conv_b": _cols(g("conv_b")),
             "ssm_w": _cols(g("ssm_norm_w")), "attn_w": _cols(g("attn_norm_w")),
             "ln1_g": _cols(g("ln1_g")), "ln1_b": _cols(g("ln1_b")), "ln2_g": _cols(g("ln2_g")),
             "ln2_b": _cols(g("ln2_b")), "ffn1": _cols(g("ffn1_norm_2")), "mix": _cols(g("mix_norm_2")),
             "xattn": _cols(g("xattn_norm_2")), "mem": _cols(g("mem_norm_2")), "ffn2": _cols(g("ffn2_norm_2")),
             "pool_b": _cols(g("pool_b_2")), "pool_s": _cols(g("pool_scale_2")), "final": _cols(g("final_norm_2")),
             "pos_k": pos[0].T, "pos_v": pos[1].T,
             "w2k": np.concatenate([w2k, w2k], 2).reshape(P, 256),
             "w2v": np.transpose(w2[1], (1, 0, 2)).reshape(P, 128)}
    par = np.ascontiguousarray(np.concatenate([parts[n] for n, _ in _WIDTHS], 1))
    rows = np.concatenate([g("dt_bias")[0], g("f_bias")[0], g("a_log")[0], g("d_skip")[0]])
    rows = np.ascontiguousarray(np.broadcast_to(rows, (P, 64)))
    cond = np.ascontiguousarray(np.broadcast_to(g("c"), (P, D)))
    return out, _features(g("x")[0]), _features(g("mem_2")[0]), par, rows, cond


def kernel(**inputs):
    import numpy as np
    import concourse.bacc as bacc
    from concourse.bass_utils import run_bass_kernel_spmd

    streams, x, mem, par, rows, cond = lay_out(inputs)
    nc = bacc.Bacc("TRN2", target_bir_lowering=False, num_devices=1)
    arrays = {}

    def given(name, a):
        arrays[name] = a
        return nc.dram_tensor(name, a.shape, F32, kind="ExternalInput").ap()

    w = {name: given("w_" + name, streams[name]) for name in streams}
    args = [given(n, a) for n, a in (("xT", x), ("memT", mem), ("par_in", par), ("rows_in", rows),
                                 ("cond_in", cond))]
    out = nc.dram_tensor("out", (P, KC, S), F32, kind="ExternalOutput").ap()
    build(nc, w, *args, out)
    got = run_bass_kernel_spmd(nc, [arrays], core_ids=[0]).results[0]["out"]
    return np.ascontiguousarray(np.transpose(got, (2, 1, 0)).reshape(1, S, D))
```
